# Optimizing a Trainium2 kernel written in Bass

```python
import math
import jax, jax.numpy as jnp
from jax import lax
import numpy as np

D_MODEL = 2048
BATCH = 1
SEQ = 256
DEPTH = 1

N_MIXERS = 3
D_FF = 4 * D_MODEL
D_PLE = 256
NORM_EPS = 1e-6
LN_EPS = 1e-5
NEG = -1e30

NSA_HEADS = 16
NSA_KV_HEADS = 4
NSA_HPG = NSA_HEADS // NSA_KV_HEADS
NSA_HEAD_DIM = D_MODEL // NSA_HEADS
NSA_CMP_LEN = 32
NSA_CMP_STRIDE = 16
NSA_CMP_HIDDEN = NSA_HEAD_DIM
NSA_SEL_LEN = 64
NSA_SEL_TOPK = 16
NSA_SEL_LOCAL = 2
NSA_WINDOW = 512
NSA_Q_BLOCK = 32
NSA_FORCE = 1e9
NSA_IN_WIDTH = NSA_HEADS * NSA_HEAD_DIM + 6 * NSA_KV_HEADS * NSA_HEAD_DIM + 3 * NSA_HEADS

CONV_WIDTH = 31
CONV_INNER = D_MODEL

GLA_HEADS = 4
GLA_DK = D_MODEL // 2 // GLA_HEADS
GLA_DV = D_MODEL // GLA_HEADS
GLA_GATE_RANK = 16
GLA_GATE_NORM = 16.0
GLA_CHUNK = 64
GLA_IN_WIDTH = 2 * GLA_HEADS * GLA_DK + 2 * GLA_HEADS * GLA_DV + GLA_GATE_RANK


def rms_norm(x, gain):
    xf = x.astype(jnp.float32)
    y = xf * lax.rsqrt(jnp.mean(xf * xf, axis=-1, keepdims=True) + NORM_EPS)
    return (y * gain.astype(jnp.float32)).astype(x.dtype)

def layer_norm(x, gain, bias):
    xf = x.astype(jnp.float32)
    mu = jnp.mean(xf, axis=-1, keepdims=True)
    xc = xf - mu
    y = xc * lax.rsqrt(jnp.mean(xc * xc, axis=-1, keepdims=True) + LN_EPS)
    return (y * gain.astype(jnp.float32) + bias.astype(jnp.float32)).astype(x.dtype)

def masked_softmax(s, valid):
    s = jnp.where(valid, s.astype(jnp.float32), NEG)
    return jax.nn.softmax(s, axis=-1) * valid

def nsa_mixer(h, w_in, w_out, pos_k, w1_k, w2_k, pos_v, w1_v, w2_v):
    B, S, _ = h.shape
    G, HPG, Dh = NSA_KV_HEADS, NSA_HPG, NSA_HEAD_DIM
    kvw = G * Dh
    proj = h @ w_in
    cuts = [NSA_HEADS * Dh + i * kvw for i in range(7)]
    q, kc, vc, ks, vs, kw, vw, gates = jnp.split(proj, cuts, axis=-1)
    q = q.reshape(B, S, G, HPG, Dh) * (Dh ** -0.5)
    kc, vc, ks, vs, kw, vw = (a.reshape(B, S, G, Dh) for a in (kc, vc, ks, vs, kw, vw))
    gates = jax.nn.sigmoid(gates.reshape(B, S, G, HPG, 3))

    n_cmp = (S - NSA_CMP_LEN) // NSA_CMP_STRIDE + 1
    cmp_idx = np.arange(n_cmp)[:, None] * NSA_CMP_STRIDE + np.arange(NSA_CMP_LEN)[None, :]
    cmp_end = cmp_idx[:, -1]

    def compress(kv, pos, w1, w2):
        blk = kv[:, cmp_idx] + pos[None, None, :, None, :]
        blk = blk.transpose(0, 1, 3, 2, 4).reshape(B, n_cmp, G, NSA_CMP_LEN * Dh)
        return jax.nn.silu(blk @ w1) @ w2

    k_cmp = compress(kc, pos_k, w1_k, w2_k)
    v_cmp = compress(vc, pos_v, w1_v, w2_v)

    n_sel = S // NSA_SEL_LEN
    n_top = min(NSA_SEL_TOPK, n_sel)
    cmp_start = np.arange(n_cmp) * NSA_CMP_STRIDE
    sel_start = np.arange(n_sel) * NSA_SEL_LEN
    overlap = jnp.asarray(((cmp_start[:, None] <= sel_start[None, :] + NSA_SEL_LEN - 1)
                           & (cmp_start[:, None] + NSA_CMP_LEN - 1 >= sel_start[None, :])).astype(np.float32))
    ks_blk = ks.reshape(B, n_sel, NSA_SEL_LEN, G, Dh).transpose(0, 3, 1, 2, 4)
    vs_blk = vs.reshape(B, n_sel, NSA_SEL_LEN, G, Dh).transpose(0, 3, 1, 2, 4)
    b_ix = jnp.arange(B)[:, None, None, None]
    g_ix = jnp.arange(G)[None, :, None, None]
    blk_ids = jnp.arange(n_sel)
    tok_off = jnp.arange(NSA_SEL_LEN)

    pad = ((0, 0), (NSA_WINDOW, 0), (0, 0), (0, 0))
    kw_pad = jnp.pad(kw, pad)
    vw_pad = jnp.pad(vw, pad)
    QB = NSA_Q_BLOCK

    def block(start):
        t = start + jnp.arange(QB)
        qb = lax.dynamic_slice_in_dim(q, start, QB, axis=1)
        gb = lax.dynamic_slice_in_dim(gates, start, QB, axis=1)

        valid_c = cmp_end[None, :] <= t[:, None]
        p_c = masked_softmax(jnp.einsum('bqghd,bngd->bghqn', qb, k_cmp), valid_c)
        o_c = jnp.einsum('bghqn,bngd->bqghd', p_c.astype(v_cmp.dtype), v_cmp)

        imp = jnp.einsum('bghqn,nm->bgqm', p_c, overlap)
        diff = (t // NSA_SEL_LEN)[:, None] - blk_ids[None, :]
        forced = (blk_ids[None, :] == 0) | ((diff >= 0) & (diff < NSA_SEL_LOCAL))
        imp = jnp.where(forced, NSA_FORCE, imp)
        imp = jnp.where(diff >= 0, imp, -NSA_FORCE)
        _, sel = lax.top_k(imp, n_top)
        k_sel = ks_blk[b_ix, g_ix, sel]
        v_sel = vs_blk[b_ix, g_ix, sel]
        tok = sel[..., None] * NSA_SEL_LEN + tok_off
        valid_s = (tok <= t[None, None, :, None, None]).reshape(B, G, 1, QB, n_top * NSA_SEL_LEN)
        s_s = jnp.einsum('bqghd,bgqnld->bghqnl', qb, k_sel).reshape(B, G, HPG, QB, n_top * NSA_SEL_LEN)
        p_s = masked_softmax(s_s, valid_s)
        o_s = jnp.einsum('bghqk,bgqkd->bqghd', p_s.astype(v_sel.dtype),
                         v_sel.reshape(B, G, QB, n_top * NSA_SEL_LEN, Dh))

        kwb = lax.dynamic_slice_in_dim(kw_pad, start, QB + NSA_WINDOW, axis=1)
        vwb = lax.dynamic_slice_in_dim(vw_pad, start, QB + NSA_WINDOW, axis=1)
        kpos = start - NSA_WINDOW + jnp.arange(QB + NSA_WINDOW)
        valid_w = ((kpos[None, :] <= t[:, None]) & (kpos[None, :] > t[:, None] - NSA_WINDOW)
                   & (kpos[None, :] >= 0))
        p_w = masked_softmax(jnp.einsum('bqghd,bkgd->bghqk', qb, kwb), valid_w)
        o_w = jnp.einsum('bghqk,bkgd->bqghd', p_w.astype(vwb.dtype), vwb)

        return gb[..., 0, None] * o_c + gb[..., 1, None] * o_s + gb[..., 2, None] * o_w

    out = lax.map(block, jnp.arange(S // QB) * QB)
    out = out.transpose(1, 0, 2, 3, 4, 5).reshape(B, S, NSA_HEADS * Dh)
    return out @ w_out

def conv_mixer(h, w_in, dw, db, ln_g, ln_b, w_out):
    a, g = jnp.split(h @ w_in, 2, axis=-1)
    u = a * jax.nn.sigmoid(g)
    y = lax.conv_general_dilated(
        u, dw[:, None, :], window_strides=(1,), padding=[(CONV_WIDTH - 1, 0)],
        dimension_numbers=('NWC', 'WIO', 'NWC'), feature_group_count=CONV_INNER) + db
    y = jax.nn.silu(layer_norm(y, ln_g, ln_b))
    return y @ w_out

def gla_mixer(h, w_in, w_gate_up, b_gate, norm_g, w_out):
    B, S, _ = h.shape
    H, dk, dv, C = GLA_HEADS, GLA_DK, GLA_DV, GLA_CHUNK
    nC = S // C
    cuts = [H * dk, 2 * H * dk, 2 * H * dk + H * dv, 2 * H * dk + 2 * H * dv]
    q, k, v, r, gz = jnp.split(h @ w_in, cuts, axis=-1)
    glog = jax.nn.log_sigmoid((gz @ w_gate_up + b_gate).astype(jnp.float32)) / GLA_GATE_NORM
    f32 = jnp.float32
    q = q.astype(f32).reshape(B, nC, C, H, dk) * (dk ** -0.5)
    k = k.astype(f32).reshape(B, nC, C, H, dk)
    v = v.astype(f32).reshape(B, nC, C, H, dv)
    bcum = jnp.cumsum(glog.reshape(B, nC, C, H, dk), axis=2)
    blast = bcum[:, :, -1]
    q_dec = q * jnp.exp(bcum)
    k_intra = k * jnp.exp(-bcum)
    k_state = k * jnp.exp(blast[:, :, None] - bcum)
    causal = jnp.asarray(np.tril(np.ones((C, C), dtype=bool)))
    A = jnp.where(causal, jnp.einsum('bncha,bnsha->bnhcs', q_dec, k_intra), 0.0)
    o_intra = jnp.einsum('bnhcs,bnshv->bnchv', A, v)

    def step(state, xs):
        qd, kst, vv, dl = xs
        o = jnp.einsum('bcha,bhav->bchv', qd, state)
        state = state * jnp.exp(dl)[..., None] + jnp.einsum('bcha,bchv->bhav', kst, vv)
        return state, o

    xs = tuple(jnp.moveaxis(a, 1, 0) for a in (q_dec, k_state, v, blast))
    _, o_inter = lax.scan(step, jnp.zeros((B, H, dk, dv), f32), xs)
    o = (o_intra + jnp.moveaxis(o_inter, 0, 1)).reshape(B, S, H, dv)
    o = o * lax.rsqrt(jnp.mean(o * o, axis=-1, keepdims=True) + NORM_EPS) * norm_g.astype(f32)
    o = o.reshape(B, S, H * dv).astype(h.dtype) * jax.nn.silu(r)
    return o @ w_out

def first_inputs(seed: int = 0) -> dict:
    key = jax.random.key(seed)
    keys = iter(jax.random.split(key, 64))

    def nrm(shape, scale):
        return jax.random.normal(next(keys), shape, jnp.float32) * scale

    def gain(shape):
        return 1.0 + nrm(shape, 0.02)

    n_nsa = len(range(0, DEPTH, N_MIXERS))
    n_conv = len(range(1, DEPTH, N_MIXERS))
    n_gla = len(range(2, DEPTH, N_MIXERS))
    D, Dh, L = D_MODEL, NSA_HEAD_DIM, NSA_CMP_LEN
    return {
        "x": nrm((BATCH, SEQ, D), 1.0),
        "p": nrm((DEPTH, BATCH, SEQ, D_PLE), 1.0),
        "norm_mix": gain((DEPTH, D)),
        "norm_ffn": gain((DEPTH, D)),
        "norm_ple": gain((DEPTH, D)),
        "norm_final": gain((D,)),
        "ffn_w1": nrm((DEPTH, D, D_FF), D ** -0.5),
        "ffn_w2": nrm((DEPTH, D_FF, D), D_FF ** -0.5),
        "ple_w_proj": nrm((DEPTH, D_PLE, D), D_PLE ** -0.5),
        "ple_w_gate": nrm((DEPTH, D, D), D ** -0.5),
        "nsa_w_in": nrm((n_nsa, D, NSA_IN_WIDTH), D ** -0.5),
        "nsa_w_out": nrm((n_nsa, NSA_HEADS * Dh, D), (NSA_HEADS * Dh) ** -0.5),
        "nsa_cmp_pos_k": nrm((n_nsa, L, Dh), 0.02),
        "nsa_cmp_w1_k": nrm((n_nsa, L * Dh, NSA_CMP_HIDDEN), (L * Dh) ** -0.5),
        "nsa_cmp_w2_k": nrm((n_nsa, NSA_CMP_HIDDEN, Dh), NSA_CMP_HIDDEN ** -0.5),
        "nsa_cmp_pos_v": nrm((n_nsa, L, Dh), 0.02),
        "nsa_cmp_w1_v": nrm((n_nsa, L * Dh, NSA_CMP_HIDDEN), (L * Dh) ** -0.5),
        "nsa_cmp_w2_v": nrm((n_nsa, NSA_CMP_HIDDEN, Dh), NSA_CMP_HIDDEN ** -0.5),
        "conv_w_in": nrm((n_conv, D, 2 * CONV_INNER), D ** -0.5),
        "conv_dw": nrm((n_conv, CONV_WIDTH, CONV_INNER), CONV_WIDTH ** -0.5),
        "conv_db": nrm((n_conv, CONV_INNER), 0.01),
        "conv_ln_g": gain((n_conv, CONV_INNER)),
        "conv_ln_b": nrm((n_conv, CONV_INNER), 0.01),
        "conv_w_out": nrm((n_conv, CONV_INNER, D), CONV_INNER ** -0.5),
        "gla_w_in": nrm((n_gla, D, GLA_IN_WIDTH), D ** -0.5),
        "gla_w_gate_up": nrm((n_gla, GLA_GATE_RANK, GLA_HEADS * GLA_DK), GLA_GATE_RANK ** -0.5),
        "gla_b_gate": nrm((n_gla, GLA_HEADS * GLA_DK), 0.01),
        "gla_norm_g": gain((n_gla, GLA_DV)),
        "gla_w_out": nrm((n_gla, GLA_HEADS * GLA_DV, D), (GLA_HEADS * GLA_DV) ** -0.5),
    }

def first_block(x, p, norm_mix, norm_ffn, norm_ple, norm_final, ffn_w1, ffn_w2,
              ple_w_proj, ple_w_gate, nsa_w_in, nsa_w_out, nsa_cmp_pos_k, nsa_cmp_w1_k,
              nsa_cmp_w2_k, nsa_cmp_pos_v, nsa_cmp_w1_v, nsa_cmp_w2_v, conv_w_in, conv_dw,
              conv_db, conv_ln_g, conv_ln_b, conv_w_out, gla_w_in, gla_w_gate_up,
              gla_b_gate, gla_norm_g, gla_w_out):
    h = x
    for i in range(DEPTH):
        m, j = i % N_MIXERS, i // N_MIXERS
        hn = rms_norm(h, norm_mix[i])
        if m == 0:
            y = nsa_mixer(hn, nsa_w_in[j], nsa_w_out[j], nsa_cmp_pos_k[j], nsa_cmp_w1_k[j],
                          nsa_cmp_w2_k[j], nsa_cmp_pos_v[j], nsa_cmp_w1_v[j], nsa_cmp_w2_v[j])
        elif m == 1:
            y = conv_mixer(hn, conv_w_in[j], conv_dw[j], conv_db[j], conv_ln_g[j],
                           conv_ln_b[j], conv_w_out[j])
        else:
            y = gla_mixer(hn, gla_w_in[j], gla_w_gate_up[j], gla_b_gate[j], gla_norm_g[j],
                          gla_w_out[j])
        h = h + y
        hn = rms_norm(h, norm_ffn[i])
        h = h + jnp.square(jax.nn.relu(hn @ ffn_w1[i])) @ ffn_w2[i]
        gate = jax.nn.sigmoid(rms_norm(h, norm_ple[i]) @ ple_w_gate[i])
        h = h + (p[i] @ ple_w_proj[i]) * gate
    return rms_norm(h, norm_final)


MIX_WIDTH = D_MODEL
BLOCK = 128
EPS = 1e-6

SWA_HEADS = 16
SWA_KV_HEADS = 2
SWA_HEAD_DIM = 64
SWA_GROUP = SWA_HEADS // SWA_KV_HEADS
WINDOW = 128

REL_BUCKETS = 32
REL_MAX_DIST = 128

MLA_HEADS = 8
MLA_Q_RANK = 384
MLA_KV_RANK = 128
MLA_NOPE_DIM = 128
MLA_ROPE_DIM = 64
MLA_V_DIM = 128
MLA_QK_DIM = MLA_NOPE_DIM + MLA_ROPE_DIM
ROPE_THETA = 10000.0

D_FF_2 = 4 * D_MODEL

SWA_Q_COLS = SWA_HEADS * SWA_HEAD_DIM
SWA_KV_COLS = SWA_KV_HEADS * SWA_HEAD_DIM
OFF_SWA_Q = 0
OFF_SWA_K = OFF_SWA_Q + SWA_Q_COLS
OFF_SWA_V = OFF_SWA_K + SWA_KV_COLS
OFF_MLA_CQ = OFF_SWA_V + SWA_KV_COLS
OFF_MLA_CKV = OFF_MLA_CQ + MLA_Q_RANK
OFF_MLA_KR = OFF_MLA_CKV + MLA_KV_RANK
IN_COLS = OFF_MLA_KR + MLA_ROPE_DIM
SWA_OUT = SWA_HEADS * SWA_HEAD_DIM
MLA_OUT = MLA_HEADS * MLA_V_DIM


def rmsnorm(x, g):
    x32 = x.astype(jnp.float32)
    y = x32 * lax.rsqrt(jnp.mean(x32 * x32, axis=-1, keepdims=True) + EPS)
    return y.astype(x.dtype) * g

def t5_causal_bucket(dist):
    n = jnp.maximum(dist, 0)
    max_exact = REL_BUCKETS // 2
    is_small = n < max_exact
    nf = jnp.maximum(n, 1).astype(jnp.float32)
    large = max_exact + (jnp.log(nf / max_exact) / math.log(REL_MAX_DIST / max_exact)
                         * (REL_BUCKETS - max_exact)).astype(jnp.int32)
    large = jnp.minimum(large, REL_BUCKETS - 1)
    return jnp.where(is_small, n, large)

def rope(x, positions):
    half = x.shape[-1] // 2
    inv_freq = ROPE_THETA ** (-jnp.arange(half, dtype=jnp.float32) / half)
    ang = positions.astype(jnp.float32)[:, None] * inv_freq[None, :]
    extra = x.ndim - 3
    ang = ang.reshape((1, ang.shape[0]) + (1,) * extra + (half,))
    cos = jnp.cos(ang).astype(x.dtype)
    sin = jnp.sin(ang).astype(x.dtype)
    x1, x2 = x[..., :half], x[..., half:]
    return jnp.concatenate([x1 * cos - x2 * sin, x2 * cos + x1 * sin], axis=-1)

def swa_sink_attention(q, k, v, sinks, rel_bias):
    B, S = q.shape[0], q.shape[1]
    nb = S // BLOCK
    qb = q.reshape(B, nb, BLOCK, SWA_KV_HEADS, SWA_GROUP, SWA_HEAD_DIM)
    kb = k.reshape(B, nb, BLOCK, SWA_KV_HEADS, SWA_HEAD_DIM)
    vb = v.reshape(B, nb, BLOCK, SWA_KV_HEADS, SWA_HEAD_DIM)
    zero = jnp.zeros_like(kb[:, :1])
    k_band = jnp.concatenate([jnp.concatenate([zero, kb[:, :-1]], axis=1), kb], axis=2)
    v_band = jnp.concatenate([jnp.concatenate([zero, vb[:, :-1]], axis=1), vb], axis=2)
    s = jnp.einsum('bnqhgd,bnkhd->bnhgqk', qb, k_band).astype(jnp.float32) * (SWA_HEAD_DIM ** -0.5)

    q_loc = jnp.arange(BLOCK)[:, None]
    k_loc = jnp.arange(2 * BLOCK)[None, :]
    dist = q_loc + BLOCK - k_loc
    in_window = (dist >= 0) & (dist < WINDOW)
    blk = jnp.arange(nb)[:, None]
    key_valid = (blk * BLOCK - BLOCK + k_loc) >= 0
    mask = in_window[None] & key_valid[:, None, :]

    bias = rel_bias.astype(jnp.float32)[t5_causal_bucket(dist)]
    bias = bias.transpose(2, 0, 1).reshape(SWA_KV_HEADS, SWA_GROUP, BLOCK, 2 * BLOCK)
    s = s + bias[None, None]
    s = jnp.where(mask[None, :, None, None], s, -jnp.inf)

    sink = sinks.astype(jnp.float32).reshape(SWA_KV_HEADS, SWA_GROUP)[None, None, :, :, None, None]
    m = jnp.maximum(jnp.max(s, axis=-1, keepdims=True), sink)
    p = jnp.exp(s - m)
    p = p / (jnp.sum(p, axis=-1, keepdims=True) + jnp.exp(sink - m))
    o = jnp.einsum('bnhgqk,bnkhd->bnqhgd', p.astype(v.dtype), v_band)
    return o.reshape(B, S, SWA_OUT)

def mla_attention(q_nope, q_rope, k_nope, k_rope, v):
    B, S = q_nope.shape[0], q_nope.shape[1]
    nb = S // BLOCK
    qn = q_nope.reshape(B, nb, BLOCK, MLA_HEADS, MLA_NOPE_DIM).transpose(1, 0, 2, 3, 4)
    qr = q_rope.reshape(B, nb, BLOCK, MLA_HEADS, MLA_ROPE_DIM).transpose(1, 0, 2, 3, 4)
    key_pos = jnp.arange(S)
    scale = MLA_QK_DIM ** -0.5

    def one_block(args):
        i, qn_i, qr_i = args
        s = (jnp.einsum('bqhd,bkhd->bhqk', qn_i, k_nope)
             + jnp.einsum('bqhd,bkd->bhqk', qr_i, k_rope)).astype(jnp.float32) * scale
        q_pos = i * BLOCK + jnp.arange(BLOCK)
        causal = key_pos[None, :] <= q_pos[:, None]
        s = jnp.where(causal[None, None], s, -jnp.inf)
        p = jax.nn.softmax(s, axis=-1)
        return jnp.einsum('bhqk,bkhd->bqhd', p.astype(v.dtype), v)

    o = lax.map(one_block, (jnp.arange(nb), qn, qr))
    return o.transpose(1, 0, 2, 3, 4).reshape(B, S, MLA_OUT)

def second_inputs(seed: int = 0) -> dict:
    key = jax.random.key(seed)
    ks = jax.random.split(key, 20)
    f32 = jnp.float32
    nrm = lambda k, shape, s: jax.random.normal(k, shape, f32) * s
    return {
        "x": nrm(ks[0], (BATCH, SEQ, D_MODEL), 1.0),
        "c": nrm(ks[1], (BATCH, D_MODEL), 1.0),
        "w_mod": nrm(ks[2], (DEPTH, D_MODEL, 6 * D_MODEL), 0.5 * D_MODEL ** -0.5),
        "b_mod": nrm(ks[3], (DEPTH, 6 * D_MODEL), 0.01),
        "attn_norm_g": 1.0 + nrm(ks[4], (DEPTH, D_MODEL), 0.02),
        "w_in": nrm(ks[5], (DEPTH, D_MODEL, IN_COLS), D_MODEL ** -0.5),
        "swa_sinks": nrm(ks[6], (DEPTH, SWA_HEADS), 1.0),
        "rel_bias": nrm(ks[7], (REL_BUCKETS, SWA_HEADS), 0.5),
        "mla_q_norm_g": 1.0 + nrm(ks[8], (DEPTH, MLA_Q_RANK), 0.02),
        "w_uq": nrm(ks[9], (DEPTH, MLA_Q_RANK, MLA_HEADS * MLA_QK_DIM), MLA_Q_RANK ** -0.5),
        "mla_kv_norm_g": 1.0 + nrm(ks[10], (DEPTH, MLA_KV_RANK), 0.02),
        "w_ukv": nrm(ks[11], (DEPTH, MLA_KV_RANK, MLA_HEADS * (MLA_NOPE_DIM + MLA_V_DIM)), MLA_KV_RANK ** -0.5),
        "w_out": nrm(ks[12], (DEPTH, MIX_WIDTH, D_MODEL), MIX_WIDTH ** -0.5),
        "mlp_norm_g": 1.0 + nrm(ks[13], (DEPTH, D_MODEL), 0.02),
        "w_ff1": nrm(ks[14], (DEPTH, D_MODEL, D_FF_2), D_MODEL ** -0.5),
        "w_ff2": nrm(ks[15], (DEPTH, D_FF_2, D_MODEL), D_FF_2 ** -0.5),
        "final_norm_g": 1.0 + nrm(ks[16], (D_MODEL,), 0.02),
    }

def second_block(x, c, w_mod, b_mod, attn_norm_g, w_in, swa_sinks, rel_bias, mla_q_norm_g, w_uq,
              mla_kv_norm_g, w_ukv, w_out, mlp_norm_g, w_ff1, w_ff2, final_norm_g):
    B, S, _ = x.shape
    positions = jnp.arange(S)
    c_act = jax.nn.silu(c)
    for l in range(DEPTH):
        mod = c_act @ w_mod[l] + b_mod[l]
        sh1, sc1, g1, sh2, sc2, g2 = [m[:, None, :] for m in jnp.split(mod, 6, axis=-1)]

        h = rmsnorm(x, attn_norm_g[l]) * (1.0 + sc1) + sh1
        proj = jnp.einsum('bsd,df->bsf', h, w_in[l])

        q_a = proj[..., OFF_SWA_Q:OFF_SWA_K].reshape(B, S, SWA_HEADS, SWA_HEAD_DIM)
        k_a = proj[..., OFF_SWA_K:OFF_SWA_V].reshape(B, S, SWA_KV_HEADS, SWA_HEAD_DIM)
        v_a = proj[..., OFF_SWA_V:OFF_MLA_CQ].reshape(B, S, SWA_KV_HEADS, SWA_HEAD_DIM)
        o_a = swa_sink_attention(q_a, k_a, v_a, swa_sinks[l], rel_bias)

        c_q = rmsnorm(proj[..., OFF_MLA_CQ:OFF_MLA_CKV], mla_q_norm_g[l])
        c_kv = rmsnorm(proj[..., OFF_MLA_CKV:OFF_MLA_KR], mla_kv_norm_g[l])
        k_rope = rope(proj[..., OFF_MLA_KR:IN_COLS], positions)
        q_b = jnp.einsum('bsr,rf->bsf', c_q, w_uq[l]).reshape(B, S, MLA_HEADS, MLA_QK_DIM)
        q_nope = q_b[..., :MLA_NOPE_DIM]
        q_rope = rope(q_b[..., MLA_NOPE_DIM:], positions)
        kv_b = jnp.einsum('bsr,rf->bsf', c_kv, w_ukv[l]).reshape(B, S, MLA_HEADS, MLA_NOPE_DIM + MLA_V_DIM)
        k_nope = kv_b[..., :MLA_NOPE_DIM]
        v_b = kv_b[..., MLA_NOPE_DIM:]
        o_b = mla_attention(q_nope, q_rope, k_nope, k_rope, v_b)

        mix = jnp.concatenate([o_a, o_b], axis=-1)
        x = x + g1 * jnp.einsum('bsm,md->bsd', mix, w_out[l])

        h = rmsnorm(x, mlp_norm_g[l]) * (1.0 + sc2) + sh2
        u = jax.nn.relu(jnp.einsum('bsd,df->bsf', h, w_ff1[l]))
        x = x + g2 * jnp.einsum('bsf,fd->bsd', u * u, w_ff2[l])
    return rmsnorm(x, final_norm_g)


def setup_inputs(seed=0):
    out = dict(first_inputs(seed))
    for name, value in second_inputs(seed + 1).items():
        if name != "x":
            out[name + "_2"] = value
    return out


def reference(
    x, p, norm_mix, norm_ffn, norm_ple, norm_final, ffn_w1, ffn_w2, ple_w_proj, ple_w_gate,
    nsa_w_in, nsa_w_out, nsa_cmp_pos_k, nsa_cmp_w1_k, nsa_cmp_w2_k, nsa_cmp_pos_v, nsa_cmp_w1_v,
    nsa_cmp_w2_v, conv_w_in, conv_dw, conv_db, conv_ln_g, conv_ln_b, conv_w_out, gla_w_in,
    gla_w_gate_up, gla_b_gate, gla_norm_g, gla_w_out, c_2, w_mod_2, b_mod_2, attn_norm_g_2,
    w_in_2, swa_sinks_2, rel_bias_2, mla_q_norm_g_2, w_uq_2, mla_kv_norm_g_2, w_ukv_2, w_out_2,
    mlp_norm_g_2, w_ff1_2, w_ff2_2, final_norm_g_2,
):
    x = first_block(
        x, p, norm_mix, norm_ffn, norm_ple, norm_final, ffn_w1, ffn_w2, ple_w_proj, ple_w_gate,
        nsa_w_in, nsa_w_out, nsa_cmp_pos_k, nsa_cmp_w1_k, nsa_cmp_w2_k, nsa_cmp_pos_v,
        nsa_cmp_w1_v, nsa_cmp_w2_v, conv_w_in, conv_dw, conv_db, conv_ln_g, conv_ln_b,
        conv_w_out, gla_w_in, gla_w_gate_up, gla_b_gate, gla_norm_g, gla_w_out,
    )
    return second_block(
        x, c_2, w_mod_2, b_mod_2, attn_norm_g_2, w_in_2, swa_sinks_2, rel_bias_2,
        mla_q_norm_g_2, w_uq_2, mla_kv_norm_g_2, w_ukv_2, w_out_2, mlp_norm_g_2, w_ff1_2,
        w_ff2_2, final_norm_g_2,
    )


_drawn_inputs = setup_inputs


def setup_inputs(seed=0):
    import zlib

    import numpy as np

    out = dict(_drawn_inputs(seed))
    spreads = {}
    factors = {'norm_mix': 8.0,
     'norm_ffn': 3.435,
     'norm_ple': 200.0,
     'norm_final': 2.675,
     'nsa_cmp_pos_k': 8.0,
     'nsa_cmp_pos_v': 8.0,
     'b_mod_2': 3.643,
     'attn_norm_g_2': 8.0,
     'swa_sinks_2': 26.67,
     'rel_bias_2': 3.228,
     'mla_q_norm_g_2': 8.0,
     'mla_kv_norm_g_2': 8.0,
     'mlp_norm_g_2': 6.149,
     'final_norm_g_2': 21.9}
    for name, (base, spread) in spreads.items():
        noise = np.random.default_rng([zlib.crc32(name.encode()), seed]).standard_normal(out[name].shape)
        drawn = base * np.exp(spread * noise) if base else spread * noise
        out[name] = __import__('jax').numpy.asarray(drawn.astype(out[name].dtype))
    for name, factor in factors.items():
        out[name] = (out[name] * factor).astype(out[name].dtype)
    return out
```

```python
from contextlib import ExitStack, contextmanager

import concourse.bass as bass
from concourse import mybir
import numpy as np

F32 = mybir.dt.float32
F32R = mybir.dt.float32r
BF16 = mybir.dt.bfloat16
ALU = mybir.AluOpType
ACT = mybir.ActivationFunctionType
AX = mybir.AxisListType

P = 128
S = 256
D = 2048
T = S // P
KC = D // P
BANKS = KC // 2
NW = 512
NG = D // NW
D_FF = 4 * D
QUARTERS = D_FF // D
EPS = 1e-6
NEG = -1e30

NSA_HEADS, NSA_G, DH = 16, 4, 128
HPG = NSA_HEADS // NSA_G
CMP_LEN, CMP_STRIDE = 32, 16
N_CMP = (S - CMP_LEN) // CMP_STRIDE + 1
CPAD = 32

SWA_HEADS, SWA_KV, SWA_D, WINDOW, BUCKETS = 16, 2, 64, 128, 32
MLA_HEADS, Q_RANK, KV_RANK, NOPE, ROPE, VD = 8, 384, 128, 128, 64, 128
QK = NOPE + ROPE
GT = 3 * P

SLOTS = 4
RAW = 2048
SPLIT = 1024
MODS = 6 * KC


class Counts:

    def __init__(self):
        self.n, self.reg, self.per = {}, None, {}

    def at(self, sem, ahead=0):
        v = self.n.get(sem, 0) + ahead
        return self.reg * self.per[sem] + v if self.reg is not None and self.per.get(sem) else v

    def next(self, sem, k=1):
        self.n[sem] = self.n.get(sem, 0) + k
        return self.at(sem)


@contextmanager
def loop(engine, counts, trips, per):
    before = dict(counts.n)
    with engine.Fori(0, trips) as i:
        counts.reg, counts.per = i, per
        yield i
    counts.reg, counts.per = None, {}
    moved = {s: v - before.get(s, 0) for s, v in counts.n.items() if v != before.get(s, 0)}
    assert moved == per, moved
    for s, k in per.items():
        counts.n[s] = before.get(s, 0) + k * trips


def program(nc, a):
    with ExitStack() as ctx:
        base = (nc.sbuf_base + 63) // 64 * 64
        cursor = [base]

        def place(name, shape, dt=F32, at=None):
            size = int(np.prod(shape[1:])) * (2 if dt == BF16 else 4)
            where = cursor[0] if at is None else at
            if at is None:
                cursor[0] += (size + 31) // 32 * 32
            assert where + size <= nc.sbuf_usable_end, (name, where + size)
            return nc.alloc_sbuf_tensor_at(name, shape, dt, offset=where)

        def area(size):
            at = cursor[0]
            cursor[0] += size
            return at

        raw = place("raw", [P, SLOTS, RAW])
        upper = place("upper", [P, SLOTS, SPLIT], F32R)
        lower = place("lower", [P, SLOTS, SPLIT], F32R)
        xs = place("xs", [P, KC, 2, S], F32R)
        h = place("h", [P, T, D])
        work = area(8192)
        half = place("half", [P, 4, S], at=work)
        summed = place("summed", [P, 4, S], at=work + 4096)
        pin = place("pin", [P, 2, 2, S], F32R, at=work + 4096)
        kcmp = place("kcmp", [P, NSA_G, CPAD], at=work + 4096)
        cstat = place("cstat", [P, 3, T * NSA_HEADS], at=work + 4608)
        hid = place("hid", [P, NSA_G, 7 * CPAD], at=work)
        csig = place("csig", [P, NSA_G, N_CMP], at=work + 3584)
        M = area(24576)
        G = area(16384)
        U = area(43008)

        modraw = place("modraw", [P, 2, D], at=M)
        modacc = place("modacc", [P, D], at=M + 16384)
        prob = place("prob", [P, 2, 12 * P], at=M)
        probT = place("probT", [P, 2, 12 * P], at=M + 12288)

        blk = place("blk", [P, CMP_LEN, NSA_G, N_CMP], at=G)
        vcmp = place("vcmp", [P, NSA_HEADS, DH], at=G)
        cprob = place("cprob", [P, T, NSA_HEADS, CPAD], at=G + 8192)
        cprobT = place("cprobT", [P, NSA_G, S], at=G + 12288)

        hidden = place("hidden", [P, KC, 2, S], F32R, at=U)
        heads = place("heads", [P, 32, S], at=U)
        vtok = place("vtok", [P, 2, T, NW], at=U + 32768)
        xn = place("xn", [P, T, D], at=U)
        vrow = place("vrow", [P, 3, P], at=U + 32768)
        gainrow = place("gainrow", [P, D], at=U + 16384)
        embed = place("embed", [P, T, D], at=U + 24576)
        prow = place("prow", [P, T, 2 * P], at=U + 40960)

        qa = place("qa", [P, 8, S], at=U)
        ka = place("ka", [P, SWA_KV, 2, S], at=U + 8192)
        qn = place("qn", [P, MLA_HEADS, S], at=U + 12288)
        qr = place("qr", [P, MLA_HEADS // 2, S], at=U + 20480)
        kr = place("kr", [P, 2, S], at=U + 24576)
        kn = place("kn", [P, MLA_HEADS, S], at=U + 26624)
        vb = place("vb", [P, T, MLA_HEADS, VD], at=U + 34816)
        tok = place("tok", [P, T, 832], at=G)
        cqs = place("cqs", [P, 3, 2, S], F32R, at=G + 6656)
        ckvs = place("ckvs", [P, 1, 2, S], F32R, at=G + 12800)
        qb = place("qb", [P, T, MLA_HEADS, QK], at=M)
        qrope = place("qrope", [P, T, MLA_HEADS, ROPE], at=M + 12288)
        rope_t = place("rope_t", [P, 2, MLA_HEADS, ROPE // 2], at=M + 16384)
        krope = place("krope", [P, T, 2, 2, ROPE], at=M + 18432)
        kpad = place("kpad", [P, T, SWA_KV, 2, 2, SWA_D], at=M + 20480)
        gain1 = place("gain1", [P, D], at=G)
        gain2 = place("gain2", [P, D], at=G + 8192)
        toe = [half, summed]

        ident = place("ident", [P, P])
        flip = place("flip", [P, P])
        ones = place("ones", [P, P])
        ident_b = place("ident_b", [P, P], BF16)
        causal_b = place("causal_b", [P, P], BF16)
        vcol = place("vcol", [P, 2 * P + CMP_LEN])
        modcol = place("modcol", [P, 6, KC])
        silu_c = place("silu_c", [P, KC])
        gates = place("gates", [P, T, 3 * NSA_HEADS])
        cmask = place("cmask", [P, 2, T, N_CMP])
        stat = place("stat", [P, 5, 2, 8])
        norm = place("norm", [P, 3, 4])
        affine = place("affine", [P, KC])
        angle = place("angle", [P, 2, T, ROPE // 2])
        sinks = place("sinks", [P, SWA_HEADS])
        eps = place("eps", [P, 1])
        COL = dict(mix=0, ffn=16, ple=32, attn=48, mlp=64, c=80, q=96, kv=99, b=P, k=P + 96, v=2 * P)
        onehot = place("onehot", [BUCKETS, P], at=U + 40960)
        relb = place("relb", [BUCKETS, SWA_HEADS], at=U + 41472)
        table = place("table", [SWA_HEADS, GT], at=G)
        tmp = place("tmp", [P, 2, S], at=work)

        ps = ctx.enter_context(nc.psum_tensor("ps", [P, 8, 512], F32))
        scratch = nc.dram_tensor("bias_by_distance", [SWA_HEADS, GT], F32).ap()

        def sem(name):
            return ctx.enter_context(nc.semaphore(name))

        landed = [sem(f"landed{i}") for i in range(SLOTS)]
        upper_ready, lower_ready, step_used = sem("upper_ready"), sem("lower_ready"), sem("step_used")
        direct_used = sem("direct_used")
        half_copied, evacuated = sem("half_copied"), sem("evacuated")
        squared, hidden_upper, hidden_ready = sem("squared"), sem("hidden_upper"), sem("hidden_ready")
        mod_landed = [sem(f"mod_landed{i}") for i in range(2)]
        mod_added, mod_summed, mod_stored = sem("mod_added"), sem("mod_summed"), sem("mod_stored")
        x_landed = [sem(f"x_landed{i}") for i in range(T)]
        rows_landed, aux_landed, consts = sem("rows_landed"), sem("aux_landed"), sem("consts")
        rows_turned, cols_ready, c_sigmoid, c_ready = sem("rows_turned"), sem("cols_ready"), sem("c_sigmoid"), sem("c_ready")
        bias_placed, bias_sum, bias_table, bias_stored = sem("bias_placed"), sem("bias_sum"), sem("bias_table"), sem("bias_stored")
        h_ready, squares, rms_ready, rstd_ready = sem("h_ready"), sem("squares"), sem("rms_ready"), sem("rstd_ready")
        scaled_a, scaled_v, turned, x_upper, x_ready = sem("scaled_a"), sem("scaled_v"), sem("turned"), sem("x_upper"), sem("x_ready")
        mod_cols = sem("mod_cols")
        gain_landed, p_landed, p_turned, p_upper, p_ready = sem("gain_landed"), sem("p_landed"), sem("p_turned"), sem("p_upper"), sem("p_ready")
        pv_done = sem("pv_done")
        ple_gate = sem("ple_gate")
        diag_ready, diag_spread, gain_row = sem("diag_ready"), sem("diag_spread"), sem("gain_row")
        blk_ready, cmp_hidden, cmp_sigmoid, hid_ready = sem("blk_ready"), sem("cmp_hidden"), sem("cmp_sigmoid"), sem("hid_ready")
        cmp_out, cmp_stored = sem("cmp_out"), sem("cmp_stored")
        gate_logits, gate_ready = sem("gate_logits"), sem("gate_ready")
        c_scores, c_shifted, c_exp, c_scaled, c_turned, c_prob = sem("c_scores"), sem("c_shifted"), sem("c_exp"), sem("c_scaled"), sem("c_turned"), sem("c_prob")
        scores, bias_ready, exps, prob_ready = sem("scores"), sem("bias_ready"), sem("exps"), sem("prob_ready")
        prob_turned, probT_ready, mixed, mix_upper, mix_ready = sem("prob_turned"), sem("probT_ready"), sem("mixed"), sem("mix_upper"), sem("mix_ready")
        toe_landed = [sem(f"toe_landed{i}") for i in range(2)]
        sink_gap = sem("sink_gap")
        lat_squares, lat_rms, lat_scaled, lat_turned, lat_upper, lat_ready = sem("lat_squares"), sem("lat_rms"), sem("lat_scaled"), sem("lat_turned"), sem("lat_upper"), sem("lat_ready")
        v_stored = sem("v_stored")
        roped, heads_turned, heads_copied = sem("roped"), sem("heads_turned"), sem("heads_copied")
        act_step, dve_step, pool_step = sem("act_step"), sem("dve_step"), sem("pool_step")
        stored = sem("stored")

        def chunks(w):
            return w.rearrange("(k p) n -> p k n", p=P)

        w_in, w_out = chunks(a["nsa_w_in"][0]), chunks(a["nsa_w_out"][0])
        ffn1, ffn2 = chunks(a["ffn_w1"][0]), chunks(a["ffn_w2"][0])
        w_gate, w_embed = chunks(a["ple_w_gate"][0]), chunks(a["ple_w_proj"][0])
        w_mod = a["w_mod_2"][0]
        w_in2, w_out2 = chunks(a["w_in_2"][0]), chunks(a["w_out_2"][0])
        ffn1b, ffn2b = chunks(a["w_ff1_2"][0]), chunks(a["w_ff2_2"][0])
        w_uq, w_ukv = chunks(a["w_uq_2"][0]), chunks(a["w_ukv_2"][0])
        NSA_Q = NSA_HEADS * DH
        KV_COLS = {"vs": NSA_Q + 3 * NW, "kw": NSA_Q + 4 * NW, "vw": NSA_Q + 5 * NW, "gates": NSA_Q + 6 * NW}
        STEPS_FFN = 8 * (10 + NG + 2 * NG * QUARTERS) + 1
        STEPS_FFN2 = STEPS_FFN + 4 + 8 * NG + 8 * 4 + 3 * 2 + 2 + 8 * NG + 8 * 2 * NG * QUARTERS
        GROUPS_UKV = 11 + NG + 2 * NG * QUARTERS + NG + NG + 4 + 3 + 2

        def slot_view(t, slot, k, n):
            return t[:, slot, 0:k * n].rearrange("p (k n) -> p k n", n=n)

        def std_steps(n):
            return [(0, 2, 0, n), (2, 2, 0, n)]

        def gate_view(t, g, branch):
            return gates[:, t, :].rearrange("p (h b) -> p h b", b=3)[:, HPG * g:HPG * g + HPG, branch]

        NSA_JOBS = [("nsa", g, b) for g in range(NSA_G) for b in range(2)]
        LATE_JOBS = [("swa", i, 0) for i in range(4)] + [("mla", i, 0) for i in range(2)]

        block = ctx.enter_context(nc.Block())

        @block.sync
        def _(sp):
            c = Counts()
            st = dict(unit=0, mod=0)
            release = []

            def free_slot():
                if len(release) >= SLOTS:
                    s, k = release.pop(0)
                    sp.wait_ge(s, c.next(s, k))

            def unit(src, K, N, frees=(lower_ready, 2)):
                free_slot()
                release.append(frees)
                slot = st["unit"] % SLOTS
                st["unit"] += 1
                dst = raw[:, slot, 0:K * N].rearrange("p (k n) -> p k n", n=N)
                sp.dma_start(dst, src).then_inc(landed[slot], 16)

            def mod_unit(row, col):
                slot = st["mod"] % 2
                if st["mod"] >= 2:
                    sp.wait_ge(mod_added, c.next(mod_added))
                st["mod"] += 1
                sp.dma_start(modraw[:, slot, :], w_mod[row, col]).then_inc(mod_landed[slot], 16)

            def section_rows(k, m):
                return [(bass.ds((k + j) * P, P), slice(m * D, (m + 1) * D)) for j in range(2)]

            def mods_of(u):
                return (slice(u % KC * P, (u % KC + 1) * P), slice(u // KC * D, (u // KC + 1) * D))

            def group(w, col, row=0, n=NW, mods=None):
                for j in range(4):
                    k = row + 4 * j
                    rows = bass.ds(k, 4) if not isinstance(row, int) else slice(k, k + 4)
                    cols = bass.ds(col, n) if not isinstance(col, int) else slice(col, col + n)
                    unit(w[:, rows, cols], 4, n)
                    if mods and j >= 2:
                        mod_unit(*mods[j - 2])

            for t in range(T):
                sp.dma_start(h[:, t, :], a["x"][0, t * P:(t + 1) * P, :]).then_inc(x_landed[t], 16)
            vecs = [(a["norm_mix"][0], 0, 0), (a["norm_ffn"][0], 16, 0), (a["norm_ple"][0], 32, 0),
                    (a["attn_norm_g_2"][0], 48, 0), (a["mlp_norm_g_2"][0], 64, 0), (a["c_2"][0], 80, 0),
                    (a["mla_q_norm_g_2"][0], 96, 0), (a["mla_kv_norm_g_2"][0], 99, 0),
                    (a["b_mod_2"][0], 0, 1)]
            for v, r, j in vecs:
                n = v.shape[0] // P
                sp.dma_start(vrow[r:r + n, j, :], v.rearrange("(r c) -> r c", c=P)).then_inc(rows_landed, 16)
            sp.dma_start(vrow[96:128, 1, :], a["nsa_cmp_pos_k"][0]).then_inc(rows_landed, 16)
            sp.dma_start(vrow[0:32, 2, :], a["nsa_cmp_pos_v"][0]).then_inc(rows_landed, 16)

            group(w_in, 0, mods=[mods_of(0), mods_of(1)])
            group(w_in, NW, mods=section_rows(2, 0))
            with loop(sp, c, 5, {lower_ready: 8, mod_added: 2}) as i:
                group(w_in, i * NW + 2 * NW, mods=section_rows(i * 2 + 4, 0))
            group(w_in, KV_COLS["kw"], mods=[mods_of(14), mods_of(15)])
            group(w_in, KV_COLS["vs"])
            group(w_in, KV_COLS["vw"])
            unit(w_in[:, :, KV_COLS["gates"]:KV_COLS["gates"] + 48], KC, 48, (lower_ready, 1))
            for name in ("k", "v"):
                w1 = a[f"nsa_cmp_w1_{name}"][0].rearrange("(l p) n -> p l n", p=P)
                for u in range(2):
                    unit(w1[:, 16 * u:16 * u + 16, :], 16, P, (direct_used, 1))
                unit(a[f"nsa_cmp_w2_{name}"][0].rearrange("p (k n) -> p k n", k=1), 1, P, (direct_used, 1))
            group(w_out, 0)
            sp.wait_ge(pv_done, len(NSA_JOBS))
            for rows_cols in section_rows(0, 1):
                mod_unit(*rows_cols)
            with loop(sp, c, NG - 1, {lower_ready: 8, mod_added: 2}) as i:
                group(w_out, i * NW + NW, mods=section_rows(i * 2 + 2, 1))

            def quarter(w1, w2, q, mods):
                for g in range(NG):
                    group(w1, q * D + g * NW, mods=mods and mods[2 * g:2 * g + 2])
                for g in range(NG):
                    group(w2, g * NW, row=q * KC, mods=mods and mods[8 + 2 * g:10 + 2 * g])

            def quarter_mods(q):
                rows = [slice((8 + j) % KC * P, ((8 + j) % KC + 1) * P) for j in range(KC)]
                return [(rows[j], bass.ds((q + (1 if j < 8 else 2)) * D, D) if not isinstance(q, int)
                         else slice((q + (1 if j < 8 else 2)) * D, (q + (1 if j < 8 else 2) + 1) * D))
                        for j in range(KC)]

            quarter(ffn1, ffn2, 0, quarter_mods(0))
            with loop(sp, c, QUARTERS - 1, {lower_ready: 64, mod_added: 16}) as i:
                quarter(ffn1, ffn2, i + 1, quarter_mods(i + 1))
            for u in range(2):
                unit(w_embed[:, 0:2, u * 1024:(u + 1) * 1024], 2, 1024)
            with loop(sp, c, NG, {lower_ready: 8, mod_added: 2}) as i:
                group(w_gate, i * NW, mods=section_rows(i * 2 + 8, 5))
            for g in range(3):
                group(w_in2, g * NW)
            group(w_in2, 3 * NW, n=320)
            for g in range(3):
                unit(w_uq[:, 0:3, g * NW:(g + 1) * NW], 3, NW)
            unit(w_ukv[:, 0:1, :], 1, D)
            group(w_out2, 0)
            with loop(sp, c, NG - 1, {lower_ready: 8}) as i:
                group(w_out2, i * NW + NW)
            quarter(ffn1b, ffn2b, 0, None)
            with loop(sp, c, QUARTERS - 1, {lower_ready: 64}) as i:
                quarter(ffn1b, ffn2b, i + 1, None)
            for t in range(T):
                sp.wait_ge(h_ready, T + t + 1)
                sp.dma_start(a["out"][0, t * P:(t + 1) * P, :], h[:, t, :]).then_inc(stored, 16)
            sp.wait_ge(stored, 16 * T)

        @block.gpsimd
        def _(pool):
            c = Counts()

            def link(op):
                op.then_inc(pool_step, 1)
                pool.wait_ge(pool_step, c.next(pool_step))

            nc.gpsimd.memset(ident[:], 0.0)
            nc.gpsimd.memset(flip[:], 0.0)
            nc.gpsimd.memset(causal_b[:], 0.0)
            nc.gpsimd.memset(cmask[:, 0], 0.0)
            nc.gpsimd.memset(cmask[:, 1], 1.0)
            nc.gpsimd.memset(eps[:], EPS)
            link(nc.gpsimd.memset(ones[:], 1.0))
            nc.gpsimd.affine_select(out=flip[:], in_=flip[:], compare_op=ALU.not_equal, fill=1.0,
                                    base=-(P - 1), pattern=[[1, P]], channel_multiplier=1)
            link(nc.gpsimd.affine_select(out=ident[:], in_=ident[:], compare_op=ALU.not_equal, fill=1.0,
                                         base=0, pattern=[[-1, P]], channel_multiplier=1))
            nc.gpsimd.affine_select(out=causal_b[:], in_=causal_b[:], compare_op=ALU.is_ge, fill=NEG,
                                    base=0, pattern=[[-1, P]], channel_multiplier=1)
            for m, fill in ((0, NEG), (1, 0.0)):
                nc.gpsimd.affine_select(out=cmask[:, m], in_=cmask[:, m], compare_op=ALU.is_ge, fill=fill,
                                        base=-(CMP_LEN - 1), pattern=[[P, T], [-CMP_STRIDE, N_CMP]],
                                        channel_multiplier=1)
            nc.gpsimd.tensor_copy(ident_b[:], ident[:]).then_inc(consts, 1)
            pool.dma_start(angle[:, 0], a["cos"].rearrange("(t p) f -> p t f", p=P)).then_inc(aux_landed, 16)
            pool.dma_start(angle[:, 1], a["sin"].rearrange("(t p) f -> p t f", p=P)).then_inc(aux_landed, 16)
            pool.dma_start(sinks[:], a["swa_sinks_2"][0].partition_broadcast(P)).then_inc(aux_landed, 16)
            pool.dma_start(onehot[:], a["bucket_onehot"]).then_inc(aux_landed, 16)
            pool.dma_start(relb[:], a["rel_bias_2"]).then_inc(aux_landed, 16)
            link(nc.gpsimd.memset(table[:], NEG))
            nc.gpsimd.memset(eps[:], EPS).then_inc(bias_placed, 1)
            pool.wait_ge(bias_table, 1)
            pool.dma_start(scratch, table[:]).then_inc(bias_stored, 16)
            pool.wait_ge(bias_stored, 16)
            pool.wait_ge(step_used, STEPS_FFN)
            pool.dma_start(prow[:], a["p"][0, 0].rearrange("(t p) f -> p t f", p=P)).then_inc(p_landed, 16)
            pool.dma_start(gainrow[:], a["norm_final"].partition_broadcast(P)).then_inc(gain_landed, 16)
            pool.wait_ge(evacuated, GROUPS_UKV)
            for i in range(4):
                if i >= 2:
                    pool.wait_ge(scores, len(NSA_JOBS) + i - 1)
                src = bass.AP(scratch.tensor, 4 * i * GT, [[1, P], [GT, 4], [1, 2 * P]])
                pool.dma_start(toe[i % 2][:], src).then_inc(toe_landed[i % 2], 16)
            pool.wait_ge(step_used, STEPS_FFN2)
            pool.dma_start(gainrow[:], a["final_norm_g_2"].partition_broadcast(P)).then_inc(gain_landed, 16)

        @block.scalar
        def _(act):
            c = Counts()
            st = dict(unit=0, step=0)

            def link(op):
                op.then_inc(act_step, 1)
                act.wait_ge(act_step, c.next(act_step))

            def split(K, N, spec, first):
                k0, nk, n0, nn = spec
                if first:
                    slot = st["unit"] % SLOTS
                    act.wait_ge(landed[slot], c.next(landed[slot], 16))
                    st["unit"] += 1
                slot = (st["unit"] - 1) % SLOTS
                if st["step"] >= SLOTS:
                    act.wait_ge(step_used, c.at("steps", 1 - SLOTS))
                src = slot_view(raw, slot, K, N)[:, k0:k0 + nk, n0:n0 + nn]
                dst = slot_view(upper, st["step"] % SLOTS, nk, nn)
                nc.scalar.activation(dst, src, ACT.Copy).then_inc(upper_ready, 1)
                st["step"] += 1
                c.next("steps")

            def group(before=(), n=NW):
                for s in range(8):
                    split(4, n, std_steps(n)[s % 2], s % 2 == 0)
                    if 2 <= s < 2 + len(before):
                        before[s - 2](s + 1)

            def group_summed(ahead):
                act.wait_ge(step_used, c.at("steps", -ahead))

            def none(ahead):
                c.next("groups")

            def copy_half(parity):
                def f(ahead):
                    group_summed(ahead)
                    act.wait_ge(evacuated, c.at("groups"))
                    nc.scalar.activation(half[:], ps[:, 4 * parity:4 * parity + 4, S:2 * S],
                                         ACT.Copy).then_inc(half_copied, 1)
                    c.next("groups")
                return f

            def first_half(ahead):
                group_summed(ahead)
                nc.scalar.activation(half[:], ps[:, 0:4, S:2 * S], ACT.Copy).then_inc(half_copied, 1)
                c.next("groups")

            def upper_hidden(g):
                def f(ahead):
                    act.wait_ge(squared, c.next(squared))
                    nc.scalar.activation(hidden[:, 4 * g:4 * g + 4, 0, :], summed[:],
                                         ACT.Copy).then_inc(hidden_upper, 1)
                return f

            def root_mean(n, first):
                first()
                nc.scalar.activation(xn[:, 0, :], h[:, 0, :], ACT.Square,
                                     accum_out=norm[:, 0, 0:1]).then_inc(act_step, 1)
                act.wait_ge(act_step, c.next(act_step))
                act.wait_ge(squares, c.next(squares))
                nc.scalar.activation(norm[:, 1, 0:2], norm[:, 0, 0:2], ACT.Sqrt, bias=eps[:, 0:1],
                                     scale=1.0 / n).then_inc(rms_ready, 1)
                c.next(rstd_ready)

            def to_features(first, gain, shift=None):
                root_mean(D, first)
                act.wait_ge(rstd_ready, c.at(rstd_ready))
                nc.scalar.activation(xn[:, 0, :], h[:, 0, :], ACT.Copy,
                                     scale=norm[:, 2, 0:1]).then_inc(scaled_a, 1)
                b0 = 4 * (st_groups() % 2)
                if shift is not None:
                    act.wait_ge(mod_cols, c.next(mod_cols))
                for k in range(KC):
                    src = ps[:, (b0 + k // 2) % 8, S * (k % 2):S * (k % 2) + S]
                    if k % 2 == 0:
                        act.wait_ge(turned, c.next(turned))
                    if shift is None:
                        op = nc.scalar.activation(xs[:, k, 0, :], src, ACT.Copy, scale=gain[:, k:k + 1])
                    else:
                        op = nc.scalar.activation(xs[:, k, 0, :], src, ACT.Identity, scale=gain[:, k:k + 1],
                                                  bias=shift[:, k:k + 1])
                    if k % 2:
                        op.then_inc(x_upper, 1)

            def st_groups():
                return c.n.get("groups", 0)

            def all_evacuated():
                act.wait_ge(evacuated, c.at("groups"))

            act.wait_ge(cols_ready, 1)
            nc.scalar.activation(silu_c[:], vcol[:, COL["c"]:COL["c"] + KC], ACT.Sigmoid).then_inc(c_sigmoid, 1)

            act.wait_ge(consts, 1)
            to_features(lambda: act.wait_ge(x_landed[0], 16), vcol[:, COL["mix"]:COL["mix"] + KC])
            group()
            group([first_half])
            with loop(act, c, 3, {"steps": 16, "groups": 2, **{l: 32 for l in landed}}):
                group([copy_half(1)])
                group([copy_half(0)])
            group([copy_half(1)])
            group([none])
            split(KC, 48, (0, KC, 0, 48), True)
            none(1)
            none(1)
            act.wait_ge(gate_logits, 1)
            nc.scalar.activation(gates[:], gates[:], ACT.Sigmoid).then_inc(gate_ready, 1)
            for i in range(2):
                for _ in range(3):
                    c.next(landed[st["unit"] % SLOTS], 16)
                    st["unit"] += 1
                act.wait_ge(direct_used, 3 * i + 2)
                nc.scalar.activation(csig[:], ps[:, 3 * i, 0:NSA_G * N_CMP], ACT.Sigmoid).then_inc(cmp_sigmoid, 1)
            act.wait_ge(c_shifted, 1)
            cp = cprob[:].rearrange("p t h n -> p (t h) n")[:, :, 0:N_CMP]
            nc.scalar.activation(cp, cp, ACT.Exp).then_inc(c_exp, 1)
            act.wait_ge(c_turned, 1)
            nc.scalar.activation(cprobT[:].rearrange("p g s -> p (g s)"), ps[:, 5:7, :].rearrange("p b n -> p (b n)"),
                                 ACT.Copy).then_inc(c_prob, 1)

            def job_exps(n, kind, scale):
                act.wait_ge(bias_ready, c.next(bias_ready))
                if kind == "swa":
                    nc.scalar.activation(stat[:, 4, n % 2, :], stat[:, 4, n % 2, :], ACT.Exp)
                for t in range(T):
                    for j in range(HPG):
                        w = P * (t + 1)
                        src = ps[:, 0, P * j:P * j + P] if t == 0 else ps[:, 1 + j // 2, S * (j % 2):S * (j % 2) + S]
                        o = P * HPG * t + w * j
                        col = HPG * t + j
                        op = nc.scalar.activation(prob[:, n % 2, o:o + w], src, ACT.Exp,
                                                  bias=stat[:, 1, n % 2, col:col + 1], scale=scale,
                                                  accum_out=stat[:, 2, n % 2, col:col + 1])
                op.then_inc(exps, 1)

            def job_turned(n):
                act.wait_ge(prob_turned, c.next(prob_turned))
                if n >= 2:
                    act.wait_ge(pv_done, c.next(pv_done))
                nc.scalar.activation(probT[:, n % 2, :], ps[:, 3:6, :].rearrange("p b n -> p (b n)"),
                                     ACT.Copy).then_inc(probT_ready, 1)

            def mix_parts(jobs, n, base):
                kind, i, b = jobs[n]
                if kind == "nsa":
                    return (4 * i, 4, ps[:, 6:8, :].rearrange("p b (c s) -> p (b c) s", s=S)) if b else None
                if kind == "swa":
                    return 2 * i, 2, ps[:, 6 + i % 2, :].rearrange("p (c s) -> p c s", s=S)
                return 8 + 4 * i, 4, ps[:, 6:8, :].rearrange("p b (c s) -> p (b c) s", s=S)

            def attention(jobs, base, scale_of):
                for n in range(len(jobs) + 1):
                    if n < len(jobs):
                        job_exps(base + n, jobs[n][0], scale_of(jobs[n][0]))
                    if n >= 1:
                        part = mix_parts(jobs, n - 1, base)
                        if part:
                            k, m, src = part
                            act.wait_ge(pv_done, base + n)
                            nc.scalar.activation(xs[:, k:k + m, 0, :], src, ACT.Copy).then_inc(mix_upper, 1)
                    if n < len(jobs):
                        job_turned(base + n)

            SCALE = {"nsa": DH ** -0.5, "swa": 1.0, "mla": QK ** -0.5}
            attention(NSA_JOBS, 0, SCALE.get)
            group()
            for g in range(1, NG):
                group([none])
            none(0)

            def quarter(pending, p0):
                for g in range(NG):
                    group(pending)
                    pending = [copy_half((p0 + g) % 2), upper_hidden(g)]
                for g in range(NG):
                    group(pending)
                    pending = [none]

            def ffn():
                p0 = st_groups() % 2
                quarter([], p0)
                with loop(act, c, QUARTERS - 1, {"steps": 64, "groups": 8, squared: 4,
                                                 **{l: 128 for l in landed}}):
                    quarter([none], p0)
                none(0)

            to_features(all_evacuated, vcol[:, COL["ffn"]:COL["ffn"] + KC])
            ffn()

            for k in range(2):
                act.wait_ge(p_turned, k + 1)
                nc.scalar.activation(pin[:, k, 0, :], ps[:, k, 0:S], ACT.Copy).then_inc(p_upper, 1)
            for u in range(2):
                for s in range(2):
                    split(2, 1024, (0, 2, 512 * s, 512), s == 0)
            for g in range(NG):
                none(0)
            to_features(all_evacuated, vcol[:, COL["ple"]:COL["ple"] + KC])

            def gate_of(g):
                def f(ahead):
                    group_summed(ahead)
                    act.wait_ge(evacuated, c.at("groups"))
                    b = 4 * (c.n["groups"] % 2)
                    nc.scalar.activation(half[:].rearrange("p (t a) s -> p t (a s)", t=T), ps[:, b:b + 2, :],
                                         ACT.Sigmoid).then_inc(ple_gate, 1)
                    c.next("groups")
                return f

            group()
            for g in range(1, NG):
                group([gate_of(g - 1)])
            gate_of(NG - 1)(0)
            root_mean(D, all_evacuated)

            to_features(lambda: act.wait_ge(h_ready, T), affine[:], modcol[:, 0, :])
            p0 = st_groups() % 2
            group()
            group([copy_half(p0)])
            group([copy_half(1 - p0)])
            group([none], n=320)
            none(0)
            act.wait_ge(evacuated, c.at("groups"))
            act.wait_ge(lat_squares, 1)
            nc.scalar.activation(norm[:, 1, 0:2], norm[:, 0, 0:2], ACT.Sqrt, bias=eps[:, 0:1], scale=1.0 / Q_RANK)
            nc.scalar.activation(norm[:, 1, 2:4], norm[:, 0, 2:4], ACT.Sqrt, bias=eps[:, 0:1],
                                 scale=1.0 / KV_RANK).then_inc(lat_rms, 1)
            for k in range(4):
                act.wait_ge(lat_turned, k // 2 + 1)
                dst = cqs[:, k, 0, :] if k < 3 else ckvs[:, 0, 0, :]
                op = nc.scalar.activation(dst, ps[:, 4 + k // 2, S * (k % 2):S * (k % 2) + S], ACT.Copy,
                                          scale=vcol[:, COL["q"] + k:COL["q"] + k + 1])
                if k % 2:
                    op.then_inc(lat_upper, 1)
            for g in range(3):
                split(3, NW, (0, 2, 0, NW), True)
                split(3, NW, (2, 1, 0, NW), False)
                none(0)
            for s in range(2):
                split(1, D, (0, 1, 1024 * s, 1024), s == 0)
                group_summed(0)
                act.wait_ge(evacuated, c.at("groups"))
                nc.scalar.activation(half[:], ps[:, 0:4, S:2 * S], ACT.Copy).then_inc(half_copied, 1)
                none(0)
            for i, (dst, b, n) in enumerate(((qn[:].rearrange("p h s -> p (h s)"), 0, 4),
                                             (qr[:].rearrange("p h s -> p (h s)"), 4, 2),
                                             (ka[:].rearrange("p v a s -> p (v a s)"), 6, 2),
                                             (kr[:].rearrange("p a s -> p (a s)"), 0, 1))):
                act.wait_ge(heads_turned, i + 1)
                src = ps[:, b:b + n, :].rearrange("p b n -> p (b n)")
                nc.scalar.activation(dst, src, ACT.Copy).then_inc(heads_copied, 1)
            attention(LATE_JOBS, len(NSA_JOBS), SCALE.get)
            group()
            for g in range(1, NG):
                group([none])
            none(0)
            to_features(all_evacuated, affine[:], modcol[:, 3, :])
            ffn()
            root_mean(D, all_evacuated)

        @block.vector
        def _(dve):
            c = Counts()
            st = dict(unit=0, step=0, mod=0)

            def link(op):
                op.then_inc(dve_step, 1)
                dve.wait_ge(dve_step, c.next(dve_step))

            def split(K, N, spec, first):
                k0, nk, n0, nn = spec
                st["unit"] += first
                slot = (st["unit"] - 1) % SLOTS
                dve.wait_ge(upper_ready, c.next(upper_ready))
                src = slot_view(raw, slot, K, N)[:, k0:k0 + nk, n0:n0 + nn]
                up, low = (slot_view(x, st["step"] % SLOTS, nk, nn) for x in (upper, lower))
                nc.vector.tensor_tensor(low, src, up, ALU.subtract).then_inc(lower_ready, 1)
                st["step"] += 1
                c.next("steps")

            def add_mod(k):
                slot = st["mod"] % 2
                dve.wait_ge(mod_landed[slot], c.next(mod_landed[slot], 16))
                if st["mod"]:
                    dve.wait_ge(mod_added, c.at(mod_added))
                w, s = modraw[:, slot, :], silu_c[:, bass.ds(k, 1)]
                if isinstance(k, int) and k == 0:
                    op = nc.vector.tensor_scalar(modacc[:], w, s, None, ALU.mult)
                else:
                    op = nc.vector.scalar_tensor_tensor(modacc[:], w, s, modacc[:], ALU.mult, ALU.add)
                op.then_inc(mod_added, 1)
                c.next(mod_added)
                st["mod"] += 1

            def store_mod(m):
                dve.wait_ge(mod_summed, c.next(mod_summed))
                if isinstance(m, int):
                    dst, b = modcol[:, m, :], vcol[:, COL["b"] + KC * m:COL["b"] + KC * (m + 1)]
                else:
                    dst, b = modcol[:, bass.ds(m, 1), :].rearrange("p a k -> p (a k)"), vcol[:, bass.ds(m * KC + COL["b"], KC)]
                nc.vector.tensor_tensor(dst, ps[:, 6, 0:KC], b, ALU.add).then_inc(mod_stored, 1)

            def group(before=(), n=NW, mods=None, store=None, at=(3, 6)):
                for s in range(8):
                    split(4, n, std_steps(n)[s % 2], s % 2 == 0)
                    if 2 <= s < 2 + len(before):
                        before[s - 2](s + 1)
                    if s == 3 and store is not None:
                        store_mod(store)
                    if mods is not None and s in at:
                        add_mod(mods + (s == at[1]))

            def group_summed(ahead):
                dve.wait_ge(step_used, c.at("steps", -ahead))

            def done(op):
                op.then_inc(evacuated, 1)
                c.next("groups")

            def own_before():
                if c.n.get("groups", 0):
                    dve.wait_ge(evacuated, c.at("groups"))

            def columns_out(parity, dst):
                def f(ahead):
                    dve.wait_ge(half_copied, c.next(half_copied))
                    done(nc.vector.tensor_tensor(dst, ps[:, 4 * parity:4 * parity + 4, 0:S], half[:], ALU.add))
                return f

            def square(parity):
                def f(ahead):
                    dve.wait_ge(half_copied, c.next(half_copied))
                    done(nc.vector.tensor_tensor(summed[:], ps[:, 4 * parity:4 * parity + 4, 0:S], half[:], ALU.add))
                    own_before()
                    nc.vector.scalar_tensor_tensor(summed[:], summed[:], 0.0, summed[:], ALU.max,
                                                   ALU.mult).then_inc(squared, 1)
                return f

            def lower_hidden(g):
                def f(ahead):
                    dve.wait_ge(hidden_upper, c.next(hidden_upper))
                    nc.vector.tensor_tensor(hidden[:, 4 * g:4 * g + 4, 1, :], summed[:],
                                            hidden[:, 4 * g:4 * g + 4, 0, :], ALU.subtract).then_inc(hidden_ready, 1)
                return f

            def rows_of(parity):
                return ps[:, 4 * parity:4 * parity + 2, :]

            def add_rows(parity, g, gain=None):
                def f(ahead):
                    group_summed(ahead)
                    hv = h[:, :, g * NW:(g + 1) * NW]
                    own_before()
                    if gain is None:
                        done(nc.vector.tensor_tensor(hv, rows_of(parity), hv, ALU.add))
                        return
                    gv = gain[:, g * NW:(g + 1) * NW].unsqueeze(1).to_broadcast([P, T, NW])
                    sv = half[:].rearrange("p (t a) s -> p t (a s)", t=T)
                    link(nc.vector.tensor_tensor(sv, rows_of(parity), gv, ALU.mult))
                    done(nc.vector.tensor_tensor(hv, sv, hv, ALU.add))
                return f

            def copy_rows(parity, dst):
                def f(ahead):
                    group_summed(ahead)
                    done(nc.vector.tensor_copy(dst, rows_of(parity)[:, :, 0:dst.shape[-1]]))
                return f

            def root_mean(first):
                first()
                nc.vector.tensor_tensor_reduce(xn[:, 1, :], h[:, 1, :], h[:, 1, :], 1.0, 0.0, ALU.mult, ALU.add,
                                               norm[:, 0, 1:2]).then_inc(squares, 1)
                c.next(squares)
                dve.wait_ge(rms_ready, c.next(rms_ready))
                nc.vector.reciprocal(norm[:, 2, 0:2], norm[:, 1, 0:2]).then_inc(rstd_ready, 1)
                dve.wait_ge(rstd_ready, c.next(rstd_ready))
                dve.wait_ge(squares, c.at(squares))

            def to_features(first, gain, shift=None):
                root_mean(first)
                nc.vector.tensor_scalar(xn[:, 1, :], h[:, 1, :], norm[:, 2, 1:2], None, ALU.mult).then_inc(scaled_v, 1)
                if shift is not None:
                    nc.vector.scalar_tensor_tensor(affine[:], shift[1], 1.0, gain, ALU.add, ALU.mult).then_inc(mod_cols, 1)
                    dve.wait_ge(mod_cols, c.next(mod_cols))
                b0 = 4 * (c.n.get("groups", 0) % 2)
                for k in range(KC):
                    src = ps[:, (b0 + k // 2) % 8, S * (k % 2):S * (k % 2) + S]
                    if k % 2 == 0:
                        dve.wait_ge(x_upper, c.next(x_upper))
                    if shift is None:
                        op = nc.vector.scalar_tensor_tensor(xs[:, k, 1, :], src, gain[:, k:k + 1], xs[:, k, 0, :],
                                                            ALU.mult, ALU.subtract)
                    else:
                        link(nc.vector.tensor_scalar(tmp[:, k % 2, :], src, affine[:, k:k + 1],
                                                     shift[0][:, k:k + 1], ALU.mult, ALU.add))
                        op = nc.vector.tensor_tensor(xs[:, k, 1, :], tmp[:, k % 2, :], xs[:, k, 0, :], ALU.subtract)
                    if k % 2:
                        op.then_inc(x_ready, 1)

            def final_norm(gain_wait):
                root_mean(own_before)
                dve.wait_ge(gain_landed, gain_wait)
                for t in range(T):
                    nc.vector.scalar_tensor_tensor(h[:, t, :], h[:, t, :], norm[:, 2, t:t + 1], gainrow[:],
                                                   ALU.mult, ALU.mult).then_inc(h_ready, 1)
                dve.wait_ge(h_ready, c.next(h_ready, T))

            dve.wait_ge(rows_turned, 1)
            nc.vector.tensor_copy(vcol[:, 0:100], ps[:, 0, 0:100])
            nc.vector.tensor_copy(vcol[:, P:], ps[:, 0, P:2 * P + CMP_LEN]).then_inc(cols_ready, 1)
            dve.wait_ge(cols_ready, 1)
            dve.wait_ge(bias_sum, 1)
            dve.wait_ge(bias_placed, 1)
            nc.vector.tensor_copy(table[:, P - 1:2 * P - 1], ps[0:SWA_HEADS, 1, 0:P]).then_inc(bias_table, 1)
            dve.wait_ge(c_sigmoid, 1)
            link(nc.vector.tensor_tensor(silu_c[:], silu_c[:], vcol[:, COL["c"]:COL["c"] + KC], ALU.mult))

            to_features(lambda: dve.wait_ge(x_landed[1], 16), vcol[:, COL["mix"]:COL["mix"] + KC])
            def heads_out(parity, i):
                return columns_out(parity, heads[:, bass.ds(i * 4, 4), :])

            group(mods=0)
            group([heads_out(0, 0)], mods=2)
            per = {"steps": 16, "groups": 2, upper_ready: 16, half_copied: 2, mod_added: 4,
                   mod_landed[0]: 32, mod_landed[1]: 32}
            with loop(dve, c, 3, per) as i:
                group([heads_out(1, i * 2 + 1)], mods=i * 4 + 4)
                group([heads_out(0, i * 2 + 2)], mods=i * 4 + 6)
            group([heads_out(1, 7)], store=0)
            group([copy_rows(0, vtok[:, 0])])
            split(KC, 48, (0, KC, 0, 48), True)
            copy_rows(1, vtok[:, 1])(1)
            group_summed(0)
            done(nc.vector.tensor_copy(gates[:], rows_of(0)[:, :, 0:48]))
            own_before()
            nc.vector.tensor_copy(norm[:, 0, 2:3], gates[:, 0, 0:1]).then_inc(gate_logits, 1)
            dve.wait_ge(bias_stored, 16)
            nc.vector.memset(hid[:], 0.0)
            link(nc.vector.memset(cprob[:], 0.0))
            for i, name in enumerate("kv"):
                if i:
                    dve.wait_ge(direct_used, 2)
                src = heads[:, 16 + 4 * i:20 + 4 * i, :].rearrange("p g (m b) -> p g m b", b=CMP_STRIDE)
                for half_ in range(CMP_LEN // CMP_STRIDE):
                    dst = blk[:, CMP_STRIDE * half_:CMP_STRIDE * (half_ + 1)].rearrange("p l g n -> p g n l")
                    pos = vcol[:, COL[name] + CMP_STRIDE * half_:COL[name] + CMP_STRIDE * (half_ + 1)]
                    for g in range(NSA_G):
                        op = nc.vector.tensor_tensor(dst[:, g], src[:, g, half_:half_ + N_CMP],
                                                     pos.unsqueeze(1).to_broadcast([P, N_CMP, CMP_STRIDE]), ALU.add)
                op.then_inc(blk_ready, 1)
                dve.wait_ge(cmp_sigmoid, i + 1)
                if i:
                    dve.wait_ge(direct_used, 3)
                nc.vector.tensor_tensor(hid[:, :, 3 * CPAD:3 * CPAD + N_CMP], ps[:, 3 * i, 0:NSA_G * N_CMP].rearrange("p (g n) -> p g n", n=N_CMP),
                                        csig[:], ALU.mult).then_inc(hid_ready, 1)
                dve.wait_ge(direct_used, 3 * i + 3)
                if i == 0:
                    nc.vector.tensor_copy(kcmp[:].rearrange("p g n -> p (g n)"), ps[:, 1, 0:P]).then_inc(cmp_stored, 1)
                else:
                    nc.vector.tensor_copy(vcmp[:].rearrange("p h n -> p (h n)"),
                                          ps[:, 3:7, :].rearrange("p b n -> p (b n)")).then_inc(cmp_stored, 1)
            dve.wait_ge(c_scores, 1)
            flat = cprob[:].rearrange("p t h n -> p (t h) n")[:, :, 0:N_CMP]
            for t in range(T):
                op = nc.vector.scalar_tensor_tensor(
                    cprob[:, t, :, 0:N_CMP], ps[:, 7, S * t:S * t + S].rearrange("p (h n) -> p h n", n=16)[:, :, 0:N_CMP],
                    DH ** -0.5, cmask[:, 0, t].unsqueeze(1).to_broadcast([P, NSA_HEADS, N_CMP]), ALU.mult, ALU.add)
            link(op)
            link(nc.vector.tensor_reduce(cstat[:, 0, :], flat, AX.X, ALU.max))
            nc.vector.tensor_tensor(flat, flat, cstat[:, 0, :].unsqueeze(2).to_broadcast([P, T * NSA_HEADS, N_CMP]),
                                    ALU.subtract).then_inc(c_shifted, 1)
            dve.wait_ge(c_exp, 1)
            link(nc.vector.tensor_reduce(cstat[:, 1, :], flat, AX.X, ALU.add))
            link(nc.vector.reciprocal(cstat[:, 2, :], cstat[:, 1, :]))
            dve.wait_ge(gate_ready, 1)
            link(nc.vector.tensor_tensor(cstat[:, 2, :].rearrange("p (t h) -> p t h", t=T),
                                         cstat[:, 2, :].rearrange("p (t h) -> p t h", t=T),
                                         gates[:].rearrange("p t (h b) -> p t h b", b=3)[:, :, :, 0], ALU.mult))
            for t in range(T):
                op = nc.vector.tensor_tensor(cprob[:, t, :, 0:N_CMP], cprob[:, t, :, 0:N_CMP],
                                             cmask[:, 1, t].unsqueeze(1).to_broadcast([P, NSA_HEADS, N_CMP]), ALU.mult)
            link(op)
            nc.vector.tensor_tensor(flat, flat, cstat[:, 2, :].unsqueeze(2).to_broadcast([P, T * NSA_HEADS, N_CMP]),
                                    ALU.mult).then_inc(c_scaled, 1)

            def wide(n):
                return ps[:, 1:3, :].rearrange("p b (h k) -> p (b h) k", k=S)

            def attention(jobs, base):
                for n in range(len(jobs) + 1):
                    if n < len(jobs):
                        kind, i, b = jobs[n]
                        m, par = base + n, (base + n) % 2
                        dve.wait_ge(scores, m + 1)
                        nc.vector.tensor_reduce(stat[:, 0, par, 0:4], ps[:, 0, :].rearrange("p (h k) -> p h k", k=P), AX.X, ALU.max)
                        link(nc.vector.tensor_reduce(stat[:, 0, par, 4:8], wide(n), AX.X, ALU.max))
                        if kind == "swa":
                            sk = sinks[:, 4 * i:4 * i + 4].unsqueeze(1).to_broadcast([P, T, 4])
                            v = stat[:, 0, par, :].rearrange("p (t h) -> p t h", t=T)
                            link(nc.vector.tensor_tensor(v, v, sk, ALU.max))
                            nc.vector.tensor_tensor(stat[:, 4, par, :].rearrange("p (t h) -> p t h", t=T), sk, v, ALU.subtract)
                        scale = {"nsa": DH ** -0.5, "swa": 1.0, "mla": QK ** -0.5}[kind]
                        nc.vector.tensor_scalar(stat[:, 1, par, :], stat[:, 0, par, :], -scale, None,
                                                ALU.mult).then_inc(bias_ready, 1)
                        dve.wait_ge(exps, m + 1)
                        if kind == "swa":
                            link(nc.vector.tensor_tensor(stat[:, 2, par, :], stat[:, 2, par, :], stat[:, 4, par, :], ALU.add))
                        link(nc.vector.reciprocal(stat[:, 3, par, :], stat[:, 2, par, :]))
                        if kind == "nsa":
                            for t in range(T):
                                v = stat[:, 3, par, 4 * t:4 * t + 4]
                                op = nc.vector.tensor_tensor(v, v, gate_view(t, i, 1 + b), ALU.mult)
                            link(op)
                        for t in range(T):
                            w = P * (t + 1)
                            v = prob[:, par, 512 * t:512 * t + 4 * w].rearrange("p (h k) -> p h k", k=w)
                            r = stat[:, 3, par, 4 * t:4 * t + 4].unsqueeze(2).to_broadcast([P, 4, w])
                            op = nc.vector.tensor_tensor(v, v, r, ALU.mult)
                        op.then_inc(prob_ready, 1)
                    if n >= 1:
                        kind, i, b = jobs[n - 1]
                        if kind == "nsa" and not b:
                            continue
                        dve.wait_ge(mix_upper, c.next(mix_upper))
                        if kind == "swa":
                            k, w, src = 2 * i, 2, ps[:, 6 + i % 2, :].rearrange("p (c s) -> p c s", s=S)
                        else:
                            k, w = (4 * i if kind == "nsa" else 8 + 4 * i), 4
                            src = ps[:, 6:8, :].rearrange("p b (c s) -> p (b c) s", s=S)
                        nc.vector.tensor_tensor(xs[:, k:k + w, 1, :], src, xs[:, k:k + w, 0, :],
                                                ALU.subtract).then_inc(mix_ready, 1)

            attention(NSA_JOBS, 0)
            st["unit"] += 6
            st_par = lambda: c.n["groups"] % 2

            def project(gain=None, mods=None):
                p0 = st_par()
                for g in range(NG):
                    group([add_rows((p0 + g - 1) % 2, g - 1, gain)] if g else (),
                          mods=None if mods is None else mods + 2 * g, at=(3, 6) if g else (6, 7))
                add_rows((p0 + NG - 1) % 2, NG - 1, gain)(0)

            project(mods=0)

            def quarter(pending, p0, gain, m):
                for g in range(NG):
                    group(pending, mods=None if m is None else 8 + 2 * g)
                    pending = [square((p0 + g) % 2), lower_hidden(g)]
                for g in range(NG):
                    group(pending, mods=None if m is None else 2 * g, store=m if g == 0 else None)
                    pending = [add_rows((p0 + g) % 2, g, gain)]

            def ffn(gain, modulated):
                p0 = st_par()
                last = add_rows((p0 + 1) % 2, NG - 1, gain)
                quarter([], p0, gain, 1 if modulated else None)
                per = {"steps": 64, "groups": 8, upper_ready: 64, half_copied: 4, hidden_upper: 4}
                if gain is not None:
                    per[dve_step] = 4
                if modulated:
                    per.update({mod_landed[0]: 128, mod_landed[1]: 128, mod_added: 16, mod_summed: 1})
                with loop(dve, c, QUARTERS - 1, per) as i:
                    quarter([last], p0, gain, i + 2 if modulated else None)
                last(0)

            to_features(own_before, vcol[:, COL["ffn"]:COL["ffn"] + KC])
            ffn(None, True)

            for k in range(2):
                dve.wait_ge(p_upper, k + 1)
                nc.vector.tensor_tensor(pin[:, k, 1, :], ps[:, k, 0:S], pin[:, k, 0, :], ALU.subtract).then_inc(p_ready, 1)
            for g in range(NG):
                split(2, 1024, (0, 2, 512 * (g % 2), 512), g % 2 == 0)
                copy_rows(st_par(), embed[:, :, g * NW:(g + 1) * NW])(0)
            to_features(own_before, vcol[:, COL["ple"]:COL["ple"] + KC])

            def gated(g):
                def f(ahead):
                    sv, hv = half[:].rearrange("p (t a) s -> p t (a s)", t=T), h[:, :, g * NW:(g + 1) * NW]
                    dve.wait_ge(ple_gate, c.next(ple_gate))
                    link(nc.vector.tensor_tensor(sv, sv, embed[:, :, g * NW:(g + 1) * NW], ALU.mult))
                    done(nc.vector.tensor_tensor(hv, sv, hv, ALU.add))
                return f

            for g in range(NG):
                group([gated(g - 1)] if g else (), mods=8 + 2 * g)
            gated(NG - 1)(0)
            store_mod(5)
            final_norm(16)

            dve.wait_ge(mod_stored, 6)
            to_features(lambda: None, vcol[:, COL["attn"]:COL["attn"] + KC], (modcol[:, 0, :], modcol[:, 1, :]))

            def scaled_queries(parity, dst):
                def f(ahead):
                    dve.wait_ge(half_copied, c.next(half_copied))
                    done(nc.vector.tensor_tensor(dst, ps[:, 4 * parity:4 * parity + 4, 0:S], half[:], ALU.add))
                    own_before()
                    link(nc.vector.tensor_scalar(dst, dst, SWA_D ** -0.5, None, ALU.mult))
                return f

            p0 = st_par()
            group()
            group([scaled_queries(p0, qa[:, 0:4, :])])
            group([scaled_queries(1 - p0, qa[:, 4:8, :])])
            group([copy_rows(p0, tok[:, :, 0:NW])], n=320)
            copy_rows(1 - p0, tok[:, :, NW:832])(0)
            own_before()
            for t in range(T):
                for i, (o, n) in enumerate(((256, Q_RANK), (640, KV_RANK))):
                    link(nc.vector.tensor_tensor_reduce(half[:].rearrange("p a s -> p (a s)")[:, 0:n], tok[:, t, o:o + n],
                                                        tok[:, t, o:o + n], 1.0, 0.0, ALU.mult, ALU.add,
                                                        norm[:, 0, 2 * i + t:2 * i + t + 1]))
            nc.vector.memset(krope[:], 0.0)
            link(nc.vector.memset(kpad[:], 0.0))
            for t in range(T):
                v = tok[:, t, 0:P].rearrange("p (v d) -> p v d", v=SWA_KV)
                for i in range(2):
                    op = nc.vector.tensor_copy(kpad[:, t, :, i, i, :], v)
            op.then_inc(lat_squares, 1)
            dve.wait_ge(lat_rms, 1)
            link(nc.vector.reciprocal(norm[:, 2, :], norm[:, 1, :]))
            for i, (o, n) in enumerate(((256, Q_RANK), (640, KV_RANK))):
                for t in range(T):
                    v = tok[:, t, o:o + n]
                    op = nc.vector.tensor_scalar(v, v, norm[:, 2, 2 * i + t:2 * i + t + 1], None, ALU.mult)
            op.then_inc(lat_scaled, 1)
            for k in range(4):
                dve.wait_ge(lat_upper, k // 2 + 1)
                up, low = (cqs[:, k, j, :] if k < 3 else ckvs[:, 0, j, :] for j in range(2))
                nc.vector.scalar_tensor_tensor(low, ps[:, 4 + k // 2, S * (k % 2):S * (k % 2) + S],
                                               vcol[:, COL["q"] + k:COL["q"] + k + 1], up,
                                               ALU.mult, ALU.subtract).then_inc(lat_ready, 1)
            for g in range(3):
                split(3, NW, (0, 2, 0, NW), True)
                split(3, NW, (2, 1, 0, NW), False)
                copy_rows(st_par(), qb[:].rearrange("p t h d -> p t (h d)")[:, :, g * NW:(g + 1) * NW])(0)
            own_before()

            def rotate(x1, x2, o1, o2, cos, sin, t1, t2):
                nc.vector.tensor_tensor(t1, x1, cos, ALU.mult)
                link(nc.vector.tensor_tensor(t2, x2, sin, ALU.mult))
                link(nc.vector.tensor_tensor(o1, t1, t2, ALU.subtract))
                nc.vector.tensor_tensor(t1, x2, cos, ALU.mult)
                link(nc.vector.tensor_tensor(t2, x1, sin, ALU.mult))
                return nc.vector.tensor_tensor(o2, t1, t2, ALU.add)

            R = ROPE // 2
            dve.wait_ge(aux_landed, 16 * 5)
            for t in range(T):
                cos, sin = (angle[:, j, t].unsqueeze(1).to_broadcast([P, MLA_HEADS, R]) for j in range(2))
                link(rotate(qb[:, t, :, NOPE:NOPE + R], qb[:, t, :, NOPE + R:QK], qrope[:, t, :, 0:R],
                            qrope[:, t, :, R:ROPE], cos, sin, rope_t[:, 0], rope_t[:, 1]))
            for t in range(T):
                link(rotate(tok[:, t, 768:768 + R], tok[:, t, 768 + R:832], krope[:, t, 0, 0, 0:R], krope[:, t, 0, 0, R:ROPE],
                            angle[:, 0, t], angle[:, 1, t], rope_t[:, 0, 0], rope_t[:, 1, 0]))
            nc.vector.tensor_copy(krope[:, :, 1, 1, :], krope[:, :, 0, 0, :]).then_inc(roped, 1)
            for s in range(2):
                split(1, D, (0, 1, 1024 * s, 1024), s == 0)
                columns_out(0, kn[:, 4 * s:4 * s + 4, :])(0)
                c.n["groups"] -= 1
                dve.wait_ge(evacuated, c.at("groups", 1))
                nc.vector.tensor_copy(vb[:, :, 4 * s:4 * s + 4, :],
                                      ps[:, 4:6, :].rearrange("p t (h d) -> p t h d", d=VD)).then_inc(v_stored, 1)
                c.next("groups")
            attention(LATE_JOBS, len(NSA_JOBS))
            st["unit"] += 0

            def spread_gain(m, dst):
                for q in range(4):
                    dg = summed[:].rearrange("p a s -> p (a s)")[:, 0:512].rearrange("p (k n) -> p k n", n=P)
                    nc.vector.tensor_tensor(dg, ident[:].unsqueeze(1).to_broadcast([P, 4, P]),
                                            modcol[:, m, 4 * q:4 * q + 4].unsqueeze(2).to_broadcast([P, 4, P]),
                                            ALU.mult).then_inc(diag_ready, 1)
                    dve.wait_ge(diag_spread, c.next(diag_spread))
                    op = nc.vector.tensor_copy(dst[:, q * NW:(q + 1) * NW], ps[:, 7, :])
                    op.then_inc(gain_row, 1)

            spread_gain(2, gain1)
            spread_gain(5, gain2)
            dve.wait_ge(gain_row, 8)
            project(gain1)
            to_features(own_before, vcol[:, COL["mlp"]:COL["mlp"] + KC], (modcol[:, 3, :], modcol[:, 4, :]))
            ffn(gain2, False)
            final_norm(32)

        @block.tensor
        def _(pe):
            c = Counts()
            st = dict(step=0)
            mm = nc.tensor.matmul

            def parity():
                return c.n.get("groups", 0) % 2

            def bank_free(p):
                if c.reg is not None or c.n.get("groups", 0) >= 2:
                    pe.wait_ge(evacuated, c.at("groups", -1))
                c.next("groups")

            def step(nk, nn, ready=None):
                if ready:
                    pe.wait_ge(*ready)
                pe.wait_ge(lower_ready, c.next(lower_ready))
                slot = st["step"] % SLOTS
                st["step"] += 1
                return slot_view(upper, slot, nk, nn), slot_view(lower, slot, nk, nn)

            def rows(x, par, k, kk, up, low, first, last):
                n = up.shape[-1]
                for t in range(T):
                    out = ps[:, 4 * par + t, 0:n]
                    xu, xl = (x[:, k, j, t * P:(t + 1) * P] for j in range(2))
                    mm(out, xu, up[:, kk, :], start=first, stop=False)
                    mm(out, xu, low[:, kk, :], start=False, stop=False)
                    op = mm(out, xl, up[:, kk, :], start=False, stop=last)
                return op

            def columns(x, par, k, kk, up, low, first, last):
                for f in range(4):
                    both = x[:, k].rearrange("p j s -> p (j s)")
                    mm(ps[:, 4 * par + f, :], up[:, kk, f * P:(f + 1) * P], both, start=first, stop=False,
                       skip_group_check=True)
                    op = mm(ps[:, 4 * par + f, 0:S], low[:, kk, f * P:(f + 1) * P], x[:, k, 0, :],
                            start=False, stop=last, skip_group_check=True)
                return op

            def group(form, x, n=NW, ready=None, between=None):
                p = st["par"] = (st["par"] + 1) % 2
                bank_free(p)
                for s in range(8):
                    if ready:
                        ready(s)
                    up, low = step(2, n)
                    for kk in range(2):
                        k = 2 * s + kk
                        op = form(x, p, k, kk, up, low, k == 0, k == KC - 1)
                    op.then_inc(step_used, 1)
                    if s == 1 and between:
                        between()

            st["par"] = 1

            def norm_parts(base):
                def ready(s):
                    pe.wait_ge(x_ready, base + max(4, s + 1))
                return ready

            def turn(norms):
                b0 = 4 * ((st["par"] + 1) % 2)
                for t, s in enumerate((scaled_a, scaled_v)):
                    pe.wait_ge(s, norms + 1)
                    for k in range(KC):
                        o = S * (k % 2) + t * P
                        op = nc.tensor.transpose(ps[:, (b0 + k // 2) % 8, o:o + P], xn[:, t, k * P:(k + 1) * P], ident[:])
                        if t and k % 2:
                            op.then_inc(turned, 1)

            def sum_mod(wait, before=-1):
                pe.wait_ge(mod_added, wait)
                pe.wait_ge(evacuated, c.at("groups", before))
                for k in range(KC):
                    op = mm(ps[:, 6, k:k + 1], modacc[:, k * P:(k + 1) * P], ones[:, 0:1], start=True, stop=True)
                op.then_inc(mod_summed, 1)

            pe.wait_ge(consts, 1)
            pe.wait_ge(rows_landed, 16 * 11)
            for j, n in ((0, 100), (1, P), (2, CMP_LEN)):
                op = nc.tensor.transpose(ps[:, 0, j * P:j * P + n], vrow[0:n, j, :], ident[0:n, 0:n])
            op.then_inc(rows_turned, 1)
            pe.wait_ge(aux_landed, 16 * 5)
            mm(ps[0:SWA_HEADS, 1, 0:P], relb[:], onehot[:], start=True, stop=True).then_inc(bias_sum, 1)
            pe.wait_ge(bias_table, 1)
            pe.wait_ge(cols_ready, 1)

            turn(0)
            group(columns, xs, ready=norm_parts(0))
            group(columns, xs)
            with loop(pe, c, 3, {lower_ready: 16, "groups": 2}):
                group(columns, xs)
                group(columns, xs)
            group(rows, xs, between=lambda: sum_mod(KC))
            group(rows, xs)
            st["par"] = 0
            bank_free(0)
            up, low = step(KC, 48)
            for k in range(KC):
                op = rows(xs, 0, k, k, up, low, k == 0, k == KC - 1)
            op.then_inc(step_used, 1)
            pe.wait_ge(evacuated, c.at("groups"))
            U0 = 4 * 10 + 1
            for i in range(2):
                pe.wait_ge(blk_ready, i + 1)
                for l in range(CMP_LEN):
                    u = U0 + 3 * i + l // 16
                    if l % 16 == 0:
                        pe.wait_ge(landed[u % SLOTS], 16 * (u // SLOTS + 1))
                    w = raw[:, u % SLOTS, (l % 16) * P:(l % 16 + 1) * P]
                    op = mm(ps[:, 3 * i, 0:NSA_G * N_CMP], w, blk[:, l].rearrange("p g n -> p (g n)"),
                            start=(l == 0), stop=(l == CMP_LEN - 1))
                    if l % 16 == 15:
                        op.then_inc(direct_used, 1)
                u = U0 + 3 * i + 2
                pe.wait_ge(landed[u % SLOTS], 16 * (u // SLOTS + 1))
                pe.wait_ge(hid_ready, i + 1)
                w = raw[:, u % SLOTS, 0:P]
                if i == 0:
                    op = mm(ps[:, 1, 0:P], w, hid[:, :, 3 * CPAD:4 * CPAD], start=True, stop=True)
                    op.then_inc(direct_used, 1)
                    pe.wait_ge(cmp_stored, 1)
                    for t in range(T):
                        for hh in range(NSA_HEADS):
                            op = mm(ps[:, 7, S * t + 16 * hh:S * t + 16 * hh + N_CMP], heads[:, hh, t * P:(t + 1) * P],
                                    kcmp[:, hh // HPG, 0:N_CMP], start=True, stop=True)
                    op.then_inc(c_scores, 1)
                else:
                    for g in range(NSA_G):
                        for j in range(HPG):
                            op = mm(ps[:, 3 + g, j * DH:(j + 1) * DH], hid[:, g, (3 - j) * CPAD:(7 - j) * CPAD], w,
                                    start=True, stop=True)
                    op.then_inc(direct_used, 1)
            pe.wait_ge(cmp_stored, 2)

            def score(n, kind, i, b):
                if n:
                    pe.wait_ge(exps, n)
                if kind == "swa":
                    pe.wait_ge(toe_landed[i % 2], 16 * (i // 2 + 1))
                for t in range(T):
                    w = P * (t + 1)
                    for j in range(HPG):
                        out = ps[:, 0, P * j:P * j + P] if t == 0 else ps[:, 1 + j // 2, S * (j % 2):S * (j % 2) + S]
                        first = j == 0 if t == 0 else j % 2 == 0
                        hh = HPG * i + j
                        if kind == "nsa":
                            pairs = [(heads[:, hh, t * P:(t + 1) * P], heads[:, 24 + 4 * b + i, 0:w])]
                        elif kind == "swa":
                            pairs = [(qa[:, hh // 2, t * P:(t + 1) * P], ka[:, i // 2, hh % 2, 0:w])]
                        else:
                            pairs = [(qn[:, hh, t * P:(t + 1) * P], kn[:, hh, 0:w]),
                                     (qr[:, hh // 2, t * P:(t + 1) * P], kr[:, hh % 2, 0:w])]
                        for q, k in pairs:
                            op = mm(out, q, k, start=first, stop=False, skip_group_check=True)
                            first = False
                        if kind == "swa":
                            for kt in range(t + 1):
                                x0 = P * (t - kt)
                                op = mm(out[:, P * kt:P * kt + P], toe[i % 2][:, j, x0:x0 + P], flip[:], start=False,
                                        stop=True, skip_group_check=True)
                if kind != "swa":
                    mask = causal_b[:].unsqueeze(1)
                    mm(ps[:, 0, :], ident_b[:], mask.to_broadcast([P, 4, P]), start=False, stop=True, skip_group_check=True)
                    for b_ in (1, 2):
                        out = ps[:, b_, :].rearrange("p (h k) -> p h k", k=S)[:, :, P:S]
                        op = mm(out, ident_b[:], mask.to_broadcast([P, 2, P]), start=False, stop=True, skip_group_check=True)
                op.then_inc(scores, 1)

            def turn_probs(n):
                pe.wait_ge(prob_ready, n + 1)
                if n:
                    pe.wait_ge(probT_ready, n)
                for j in range(HPG):
                    bank, o = 3 + j // 2, S * (j % 2)
                    p = prob[:, n % 2, :]
                    nc.tensor.transpose(ps[:, bank, o:o + P], p[:, P * j:P * j + P], ident[:])
                    nc.tensor.transpose(ps[:, bank, o + P:o + S], p[:, 512 + S * j:512 + S * j + P], ident[:])
                    op = nc.tensor.transpose(ps[:, 5, P * j:P * j + P], p[:, 512 + S * j + P:512 + S * j + S], ident[:])
                op.then_inc(prob_turned, 1)

            def mix(n, kind, i, b):
                pe.wait_ge(probT_ready, n + 1)
                if kind != "nsa" or not b:
                    if c.n.get(mix_ready, 0):
                        pe.wait_ge(mix_ready, c.at(mix_ready))
                    c.next(mix_ready)
                for j in range(HPG):
                    hh = HPG * i + j
                    if kind == "swa":
                        r = slice(64 * (j % 2), 64 * (j % 2) + 64)
                        out = ps[r, 6 + i % 2, S * (j // 2):S * (j // 2) + S]
                        v = [tok[:, kt, P + 64 * (i // 2):P + 64 * (i // 2) + 64] for kt in range(T)]
                        first = j < 2
                    else:
                        out = ps[:, 6 + j // 2, S * (j % 2):S * (j % 2) + S]
                        first = j % 2 == 0 and not b
                        v = [vtok[:, b, kt, i * DH:(i + 1) * DH] if kind == "nsa" else vb[:, kt, hh, :] for kt in range(T)]
                    if kind == "nsa" and not b:
                        mm(out, vcmp[:, hh, :], cprobT[:, i, :], start=first, stop=False, skip_group_check=True)
                        first = False
                    mm(out, v[0], probT[:, n % 2, S * j:S * j + S], start=first, stop=False, skip_group_check=True)
                    op = mm(out[:, P:S], v[1], probT[:, n % 2, 1024 + P * j:1024 + P * j + P], start=False, stop=True,
                            skip_group_check=True)
                op.then_inc(pv_done, 1)

            def attention(jobs, base, after_first=None):
                score(base, *jobs[0])
                if after_first:
                    after_first()
                for n in range(len(jobs)):
                    if n + 1 < len(jobs):
                        score(base + n + 1, *jobs[n + 1])
                    if n:
                        mix(base + n - 1, *jobs[n - 1])
                    turn_probs(base + n)
                mix(base + len(jobs) - 1, *jobs[-1])

            def turn_compressed():
                pe.wait_ge(c_scaled, 1)
                for g in range(NSA_G):
                    for t in range(T):
                        op = nc.tensor.transpose(ps[:, 5 + g // 2, S * (g % 2) + P * t:S * (g % 2) + P * t + P],
                                                 cprob[:, t, HPG * g:HPG * g + HPG, :].rearrange("p h n -> p (h n)"), ident[:])
                op.then_inc(c_turned, 1)
                pe.wait_ge(c_prob, 1)

            attention(NSA_JOBS, 0, turn_compressed)

            def mixed_parts(per_step):
                def ready(s):
                    pe.wait_ge(mix_ready, per_step(s))
                return ready

            pe.wait_ge(mix_ready, NSA_G)
            for g in range(NG):
                group(rows, xs)

            def quarter(first_ready, between):
                for g in range(NG):
                    group(columns, xs, ready=first_ready if g == 0 else None)
                for g in range(NG):
                    def ready(s, g=g):
                        if g == 0 and s in (0, 6):
                            pe.wait_ge(hidden_ready, c.next(hidden_ready, 3 if s == 0 else 1))
                    group(rows, hidden, ready=ready, between=between if g == 0 else None)

            def ffn(base, modulated):
                def between():
                    sum_mod(c.at("mods", 0))
                    c.next("mods", KC)
                if modulated:
                    c.n["mods"] = 2 * KC
                quarter(norm_parts(base), between if modulated else None)
                per = {lower_ready: 64, "groups": 8, hidden_ready: 4}
                if modulated:
                    per["mods"] = KC
                with loop(pe, c, QUARTERS - 1, per):
                    quarter(None, between if modulated else None)

            turn(1)
            ffn(BANKS, True)
            pe.wait_ge(p_landed, 16)
            pe.wait_ge(evacuated, c.at("groups"))
            for k in range(2):
                for t in range(T):
                    op = nc.tensor.transpose(ps[:, k, t * P:(t + 1) * P], prow[:, t, k * P:(k + 1) * P], ident[:])
                op.then_inc(p_turned, 1)
            pe.wait_ge(p_ready, 2)
            for g in range(NG):
                st["par"] = (st["par"] + 1) % 2
                bank_free(st["par"])
                up, low = step(2, NW)
                for k in range(2):
                    op = rows(pin, st["par"], k, k, up, low, k == 0, k == 1)
                op.then_inc(step_used, 1)
            turn(2)
            group(rows, xs, ready=norm_parts(2 * BANKS))
            for g in range(1, NG):
                group(rows, xs)
            pe.wait_ge(evacuated, c.at("groups"))
            sum_mod(6 * KC, 0)
            pe.wait_ge(mod_stored, 6)

            turn(3)
            group(columns, xs, ready=norm_parts(3 * BANKS))
            group(columns, xs)
            group(rows, xs)
            group(rows, xs, n=320)
            pe.wait_ge(evacuated, c.at("groups"))
            pe.wait_ge(lat_scaled, 1)
            for k in range(4):
                for t in range(T):
                    op = nc.tensor.transpose(ps[:, 4 + k // 2, S * (k % 2) + t * P:S * (k % 2) + (t + 1) * P],
                                             tok[:, t, 256 + k * P:256 + (k + 1) * P], ident[:])
                if k % 2:
                    op.then_inc(lat_turned, 1)
            pe.wait_ge(lat_ready, 4)
            for g in range(3):
                st["par"] = (st["par"] + 1) % 2
                bank_free(st["par"])
                for nk in (2, 1):
                    up, low = step(nk, NW)
                    for kk in range(nk):
                        k = kk + 2 * (nk == 1)
                        op = rows(cqs, st["par"], k, kk, up, low, k == 0, k == 2)
                    op.then_inc(step_used, 1)
            for s in range(2):
                pe.wait_ge(evacuated, c.at("groups"))
                if s:
                    pe.wait_ge(v_stored, s)
                c.next("groups")
                up, low = step(1, 1024)
                kv = [x.rearrange("p a (h d) -> p (a h) d", d=NOPE + VD) for x in (up, low)]
                both = ckvs[:, 0].rearrange("p j s -> p (j s)")
                for j in range(4):
                    mm(ps[:, j, :], kv[0][:, j, 0:NOPE], both, start=True, stop=False, skip_group_check=True)
                    mm(ps[:, j, 0:S], kv[1][:, j, 0:NOPE], ckvs[:, 0, 0, :], start=False, stop=True, skip_group_check=True)
                for t in range(T):
                    xu, xl = (ckvs[:, 0, j, t * P:(t + 1) * P] for j in range(2))
                    vu, vl = (x[:, :, NOPE:] for x in kv)
                    out = ps[:, 4 + t, :]
                    mm(out, xu, vu, start=True, stop=False)
                    mm(out, xu, vl, start=False, stop=False)
                    op = mm(out, xl, vu, start=False, stop=True)
                op.then_inc(step_used, 1)
            pe.wait_ge(evacuated, c.at("groups"))
            pe.wait_ge(v_stored, 2)
            pe.wait_ge(roped, 1)
            for hh in range(MLA_HEADS):
                for t in range(T):
                    o = S * (hh % 2) + t * P
                    op = nc.tensor.transpose(ps[:, hh // 2, o:o + P], qb[:, t, hh, 0:NOPE], ident[:])
            op.then_inc(heads_turned, 1)
            for j in range(MLA_HEADS // 2):
                for t in range(T):
                    o = S * (j % 2) + t * P
                    op = nc.tensor.transpose(ps[:, 4 + j // 2, o:o + P],
                                             qrope[:, t, 2 * j:2 * j + 2, :].rearrange("p h d -> p (h d)"), ident[:])
            op.then_inc(heads_turned, 1)
            for j in range(SWA_KV):
                for i in range(2):
                    for t in range(T):
                        o = S * i + t * P
                        op = nc.tensor.transpose(ps[:, 6 + j, o:o + P], kpad[:, t, j, i].rearrange("p a d -> p (a d)"), ident[:])
            op.then_inc(heads_turned, 1)
            pe.wait_ge(heads_copied, 1)
            for i in range(2):
                for t in range(T):
                    o = S * i + t * P
                    op = nc.tensor.transpose(ps[:, 0, o:o + P], krope[:, t, i].rearrange("p a d -> p (a d)"), ident[:])
            op.then_inc(heads_turned, 1)
            pe.wait_ge(heads_copied, 4)
            attention(LATE_JOBS, len(NSA_JOBS))
            pe.wait_ge(mix_ready, NSA_G + len(LATE_JOBS))
            for q in range(8):
                pe.wait_ge(diag_ready, q + 1)
                if q:
                    pe.wait_ge(gain_row, q)
                mm(ps[:, 7, :], ones[:], summed[:].rearrange("p a s -> p (a s)")[:, 0:512], start=True,
                   stop=True).then_inc(diag_spread, 1)
            pe.wait_ge(gain_row, 8)
            for g in range(NG):
                group(rows, xs)
            turn(4)
            ffn(4 * BANKS, False)


_INS = ["x", "p", "norm_mix", "norm_ffn", "norm_ple", "norm_final", "ffn_w1", "ffn_w2", "ple_w_proj", "ple_w_gate",
        "nsa_w_in", "nsa_w_out", "nsa_cmp_pos_k", "nsa_cmp_w1_k", "nsa_cmp_w2_k", "nsa_cmp_pos_v", "nsa_cmp_w1_v",
        "nsa_cmp_w2_v", "c_2", "w_mod_2", "b_mod_2", "attn_norm_g_2", "w_in_2", "swa_sinks_2", "rel_bias_2",
        "mla_q_norm_g_2", "w_uq_2", "mla_kv_norm_g_2", "w_ukv_2", "w_out_2", "mlp_norm_g_2", "w_ff1_2", "w_ff2_2",
        "final_norm_g_2"]


def shape_constants():
    half_ = ROPE // 2
    freq = np.float32(10000.0) ** (-np.arange(half_, dtype=np.float32) / np.float32(half_))
    ang = np.arange(S, dtype=np.float32)[:, None] * freq[None, :].astype(np.float32)
    exact = BUCKETS // 2
    dist = np.arange(P)
    far = exact + (np.log(np.maximum(dist, 1).astype(np.float32) / exact) / np.log(P / exact)
                   * (BUCKETS - exact)).astype(np.int32)
    bucket = np.where(dist < exact, dist, np.minimum(far, BUCKETS - 1))
    onehot = (bucket[None, :] == np.arange(BUCKETS)[:, None]).astype(np.float32)
    return {"cos": np.cos(ang).astype(np.float32), "sin": np.sin(ang).astype(np.float32), "bucket_onehot": onehot}


def kernel(**inputs):
    import numpy as _np
    import concourse.bacc as _bacc
    from concourse import mybir as _mybir
    from concourse.bass_utils import run_bass_kernel_spmd as _run

    nc = _bacc.Bacc("TRN2", target_bir_lowering=False, num_devices=1)
    arrays, args = {}, {}
    for name, a in [(n, inputs[n]) for n in _INS] + list(shape_constants().items()):
        a = _np.ascontiguousarray(a)
        arrays[f"in_{name}_dram"] = a
        args[name] = nc.dram_tensor(f"in_{name}_dram", a.shape, _mybir.dt.from_np(a.dtype), kind="ExternalInput").ap()
    args["out"] = nc.dram_tensor("out_0_dram", (1, S, D), _mybir.dt.float32, kind="ExternalOutput").ap()
    program(nc, args)
    r = _run(nc, [arrays], core_ids=[0])
    return r.results[0]["out_0_dram"]
```

```python
from contextlib import ExitStack, contextmanager

import concourse.bass as bass
from concourse import mybir
import numpy as np

F32 = mybir.dt.float32
F32R = mybir.dt.float32r
BF16 = mybir.dt.bfloat16
ALU = mybir.AluOpType
ACT = mybir.ActivationFunctionType
AX = mybir.AxisListType

P = 128
S = 256
D = 2048
T = S // P
KC = D // P
BANKS = KC // 2
NW = 512
NG = D // NW
D_FF = 4 * D
QUARTERS = D_FF // D
EPS = 1e-6
NEG = -1e30

NSA_HEADS, NSA_G, DH = 16, 4, 128
HPG = NSA_HEADS // NSA_G
CMP_LEN, CMP_STRIDE = 32, 16
N_CMP = (S - CMP_LEN) // CMP_STRIDE + 1
CPAD = 32

SWA_HEADS, SWA_KV, SWA_D, WINDOW, BUCKETS = 16, 2, 64, 128, 32
MLA_HEADS, Q_RANK, KV_RANK, NOPE, ROPE, VD = 8, 384, 128, 128, 64, 128
QK = NOPE + ROPE
GT = 3 * P

SLOTS = 4
RAW = 2048
SPLIT = 1024
MODS = 6 * KC


class Counts:

    def __init__(self):
        self.n, self.reg, self.per = {}, None, {}

    def at(self, sem, ahead=0):
        v = self.n.get(sem, 0) + ahead
        return self.reg * self.per[sem] + v if self.reg is not None and self.per.get(sem) else v

    def next(self, sem, k=1):
        self.n[sem] = self.n.get(sem, 0) + k
        return self.at(sem)


@contextmanager
def loop(engine, counts, trips, per):
    before = dict(counts.n)
    with engine.Fori(0, trips) as i:
        counts.reg, counts.per = i, per
        yield i
    counts.reg, counts.per = None, {}
    moved = {s: v - before.get(s, 0) for s, v in counts.n.items() if v != before.get(s, 0)}
    assert moved == per, moved
    for s, k in per.items():
        counts.n[s] = before.get(s, 0) + k * trips


def program(nc, a):
    with ExitStack() as ctx:
        base = (nc.sbuf_base + 63) // 64 * 64
        cursor = [base]

        def place(name, shape, dt=F32, at=None):
            size = int(np.prod(shape[1:])) * (2 if dt == BF16 else 4)
            where = cursor[0] if at is None else at
            if at is None:
                cursor[0] += (size + 31) // 32 * 32
            assert where + size <= nc.sbuf_usable_end, (name, where + size)
            return nc.alloc_sbuf_tensor_at(name, shape, dt, offset=where)

        def area(size):
            at = cursor[0]
            cursor[0] += size
            return at

        raw = place("raw", [P, SLOTS, RAW])
        upper = place("upper", [P, SLOTS, SPLIT], F32R)
        lower = place("lower", [P, SLOTS, SPLIT], F32R)
        xs = place("xs", [P, KC, 2, S], F32R)
        h = place("h", [P, T, D])
        work = area(8192)
        half = place("half", [P, 4, S], at=work)
        summed = place("summed", [P, 4, S], at=work + 4096)
        kcmp = place("kcmp", [P, NSA_G, CPAD], at=work + 4096)
        cstat = place("cstat", [P, 3, T * NSA_HEADS], at=work + 4608)
        hid = place("hid", [P, NSA_G, 7 * CPAD], at=work)
        gsum = place("gsum", [3 * NSA_HEADS, 2, S], at=work + 5120)
        csig = place("csig", [P, NSA_G, N_CMP], at=work + 3584)
        M = area(24576)
        G = area(16384)
        U = area(43008)

        modraw = place("modraw", [P, 2, D], at=M)
        modacc = place("modacc", [P, D], at=M + 16384)
        prob = place("prob", [P, 2, 12 * P], at=M)
        probT = place("probT", [P, 2, 12 * P], at=M + 12288)

        blk = place("blk", [P, CMP_LEN, NSA_G, N_CMP], at=G)
        vcmp = place("vcmp", [P, NSA_HEADS, DH], at=G)
        cprob = place("cprob", [P, T, NSA_HEADS, CPAD], at=G + 8192)
        cprobT = place("cprobT", [P, NSA_G, S], at=G + 12288)

        pin = place("pin", [P, 2, 2, S], F32R, at=G)

        hidden = place("hidden", [P, KC, 2, S], F32R, at=U)
        heads = place("heads", [P, 32, S], at=U)
        vtok = place("vtok", [P, 2, T, NW], at=U + 32768)
        xn = place("xn", [P, T, D], at=U)
        vrow = place("vrow", [P, 3, P], at=U + 32768)
        gainrow = place("gainrow", [P, D], at=U + 16384)
        embed = place("embed", [P, T, D], at=U + 24576)
        prow = place("prow", [P, T, 2 * P], at=U + 40960)

        qa = place("qa", [P, 8, S], at=U)
        ka = place("ka", [P, SWA_KV, 2, S], at=U + 8192)
        qn = place("qn", [P, MLA_HEADS, S], at=U + 12288)
        qr = place("qr", [P, MLA_HEADS // 2, S], at=U + 20480)
        kr = place("kr", [P, 2, S], at=U + 24576)
        kn = place("kn", [P, MLA_HEADS, S], at=U + 26624)
        vb = place("vb", [P, T, MLA_HEADS, VD], at=U + 34816)
        tok = place("tok", [P, T, 832], at=G)
        cqs = place("cqs", [P, 3, 2, S], F32R, at=G + 6656)
        ckvs = place("ckvs", [P, 1, 2, S], F32R, at=G + 12800)
        qb = place("qb", [P, T, MLA_HEADS, QK], at=M)
        qrope = place("qrope", [P, T, MLA_HEADS, ROPE], at=M + 12288)
        rope_t = place("rope_t", [P, 2, MLA_HEADS, ROPE // 2], at=M + 16384)
        krope = place("krope", [P, T, 2, 2, ROPE], at=M + 18432)
        kpad = place("kpad", [P, T, SWA_KV, 2, 2, SWA_D], at=M + 20480)
        gain1 = place("gain1", [P, D], at=G)
        gain2 = place("gain2", [P, D], at=G + 8192)
        toe = [half, summed]

        ident = place("ident", [P, P])
        flip = place("flip", [P, P])
        ones = place("ones", [P, P])
        ident_b = place("ident_b", [P, P], BF16)
        causal_b = place("causal_b", [P, P], BF16)
        vcol = place("vcol", [P, 2 * P + CMP_LEN])
        modcol = place("modcol", [P, 6, KC])
        silu_c = place("silu_c", [P, KC])
        gates = place("gates", [P, T, 3 * NSA_HEADS])
        cmask = place("cmask", [P, 2, T, N_CMP])
        stat = place("stat", [P, 5, 2, 8])
        sumsq = place("sumsq", [P, T, 4])
        norm = place("norm", [P, 3, 4])
        affine = place("affine", [P, KC])
        angle = place("angle", [P, 2, T, ROPE // 2])
        sinks = place("sinks", [P, SWA_HEADS])
        eps = place("eps", [P, 1])
        COL = dict(mix=0, ffn=16, ple=32, attn=48, mlp=64, c=80, q=96, kv=99, b=P, k=P + 96, v=2 * P)
        onehot = place("onehot", [BUCKETS, P], at=U + 40960)
        relb = place("relb", [BUCKETS, SWA_HEADS], at=U + 41472)
        table = place("table", [SWA_HEADS, GT], at=G + 12288)
        tmp = place("tmp", [P, 2, S], at=work)

        ps = ctx.enter_context(nc.psum_tensor("ps", [P, 8, 512], F32))
        modrow = place("modrow", [6 * KC, P], at=work + 4096)
        rows_scratch = nc.dram_tensor("modulation_rows", [6 * KC, P], F32).ap()
        scratch = nc.dram_tensor("bias_by_distance", [SWA_HEADS, GT], F32).ap()

        def sem(name):
            return ctx.enter_context(nc.semaphore(name))

        landed = [sem(f"landed{i}") for i in range(SLOTS)]
        upper_ready, lower_ready, step_used = sem("upper_ready"), sem("lower_ready"), sem("step_used")
        direct_used = sem("direct_used")
        half_copied, evacuated = sem("half_copied"), sem("evacuated")
        squared, hidden_upper, hidden_ready = sem("squared"), sem("hidden_upper"), sem("hidden_ready")
        mod_landed = [sem(f"mod_landed{i}") for i in range(2)]
        mod_added, mod_summed, mod_stored = sem("mod_added"), sem("mod_summed"), sem("mod_stored")
        x_landed = [sem(f"x_landed{i}") for i in range(T)]
        rows_landed, aux_landed, consts = sem("rows_landed"), sem("aux_landed"), sem("consts")
        rows_turned, cols_ready, c_sigmoid, c_ready = sem("rows_turned"), sem("cols_ready"), sem("c_sigmoid"), sem("c_ready")
        bias_placed, bias_sum, bias_table, bias_stored = sem("bias_placed"), sem("bias_sum"), sem("bias_table"), sem("bias_stored")
        h_ready, squares, squares_v, mean_ready = sem("h_ready"), sem("squares"), sem("squares_v"), sem("mean_ready")
        rms_ready, rstd_ready = sem("rms_ready"), sem("rstd_ready")
        scaled_a, scaled_v, turned, x_upper, x_ready = sem("scaled_a"), sem("scaled_v"), sem("turned"), sem("x_upper"), sem("x_ready")
        mod_cols = sem("mod_cols")
        gain_landed, p_landed, p_turned, p_upper, p_ready = sem("gain_landed"), sem("p_landed"), sem("p_turned"), sem("p_upper"), sem("p_ready")
        pv_done = sem("pv_done")
        ple_gate = sem("ple_gate")
        mod_turned, mod_rows, mod_rows_stored, gain_row = sem("mod_turned"), sem("mod_rows"), sem("mod_rows_stored"), sem("gain_row")
        blk_ready, cmp_hidden, cmp_sigmoid, hid_ready = sem("blk_ready"), sem("cmp_hidden"), sem("cmp_sigmoid"), sem("hid_ready")
        cmp_out, cmp_stored = sem("cmp_out"), sem("cmp_stored")
        gate_half, gate_sum, gate_turned, gate_ready = sem("gate_half"), sem("gate_sum"), sem("gate_turned"), sem("gate_ready")
        c_scores, c_shifted, c_exp, c_scaled, c_turned, c_prob = sem("c_scores"), sem("c_shifted"), sem("c_exp"), sem("c_scaled"), sem("c_turned"), sem("c_prob")
        scores, bias_ready, exps, prob_ready = sem("scores"), sem("bias_ready"), sem("exps"), sem("prob_ready")
        prob_turned, probT_ready, mixed, mix_upper, mix_ready = sem("prob_turned"), sem("probT_ready"), sem("mixed"), sem("mix_upper"), sem("mix_ready")
        toe_landed = [sem(f"toe_landed{i}") for i in range(2)]
        sink_gap = sem("sink_gap")
        lat_squares, lat_rms, lat_scaled, lat_turned, lat_upper, lat_ready = sem("lat_squares"), sem("lat_rms"), sem("lat_scaled"), sem("lat_turned"), sem("lat_upper"), sem("lat_ready")
        v_stored = sem("v_stored")
        roped, heads_turned, heads_copied = sem("roped"), sem("heads_turned"), sem("heads_copied")
        act_step, dve_step, pool_step = sem("act_step"), sem("dve_step"), sem("pool_step")
        stored = sem("stored")

        def chunks(w):
            return w.rearrange("(k p) n -> p k n", p=P)

        w_in, w_out = chunks(a["nsa_w_in"][0]), chunks(a["nsa_w_out"][0])
        ffn1, ffn2 = chunks(a["ffn_w1"][0]), chunks(a["ffn_w2"][0])
        w_gate, w_embed = chunks(a["ple_w_gate"][0]), chunks(a["ple_w_proj"][0])
        w_mod = a["w_mod_2"][0]
        w_in2, w_out2 = chunks(a["w_in_2"][0]), chunks(a["w_out_2"][0])
        ffn1b, ffn2b = chunks(a["w_ff1_2"][0]), chunks(a["w_ff2_2"][0])
        w_uq, w_ukv = chunks(a["w_uq_2"][0]), chunks(a["w_ukv_2"][0])
        NSA_Q = NSA_HEADS * DH
        KV_COLS = {"vs": NSA_Q + 3 * NW, "kw": NSA_Q + 4 * NW, "vw": NSA_Q + 5 * NW, "gates": NSA_Q + 6 * NW}
        STEPS_FFN = 8 * (10 + NG + 2 * NG * QUARTERS) + 1
        STEPS_FFN2 = STEPS_FFN + 4 + 8 * NG + 8 * 4 + 3 * 2 + 2 + 8 * NG + 8 * 2 * NG * QUARTERS
        GROUPS_UKV = 11 + NG + 2 * NG * QUARTERS + NG + NG + 4 + 3 + 2

        PIECES = [(0, 2 * NW), (2 * NW, NW), (3 * NW, NW)]
        HALVES = [(0, 2 * NW), (2 * NW, 2 * NW)]

        def slot_view(t, slot, k, n):
            return t[:, slot, 0:k * n].rearrange("p (k n) -> p k n", n=n)

        def std_steps(n):
            return [(0, 2, 0, n), (2, 2, 0, n)]

        def gate_view(t, g, branch):
            return gates[:, t, :].rearrange("p (h b) -> p h b", b=3)[:, HPG * g:HPG * g + HPG, branch]

        NSA_JOBS = [("nsa", g, b) for g in range(NSA_G) for b in range(2)]
        LATE_JOBS = [("swa", i, 0) for i in range(4)] + [("mla", i, 0) for i in range(2)]

        block = ctx.enter_context(nc.Block())

        @block.sync
        def _(sp):
            c = Counts()
            st = dict(unit=0, mod=0)
            release = []

            def free_slot():
                if len(release) >= SLOTS:
                    s, k = release.pop(0)
                    sp.wait_ge(s, c.next(s, k))

            def unit(src, K, N, frees=(lower_ready, 2)):
                free_slot()
                release.append(frees)
                slot = st["unit"] % SLOTS
                st["unit"] += 1
                dst = raw[:, slot, 0:K * N].rearrange("p (k n) -> p k n", n=N)
                sp.dma_start(dst, src).then_inc(landed[slot], 16)

            def mod_unit(row, col):
                slot = st["mod"] % 2
                if st["mod"] >= 2:
                    sp.wait_ge(mod_added, c.next(mod_added))
                st["mod"] += 1
                sp.dma_start(modraw[:, slot, :], w_mod[row, col]).then_inc(mod_landed[slot], 16)

            def section_rows(k, m):
                return [(bass.ds((k + j) * P, P), slice(m * D, (m + 1) * D)) for j in range(2)]

            def mods_of(u):
                return (slice(u % KC * P, (u % KC + 1) * P), slice(u // KC * D, (u // KC + 1) * D))

            def group(w, col, row=0, n=NW, mods=None):
                for j in range(4):
                    k = row + 4 * j
                    rows = bass.ds(k, 4) if not isinstance(row, int) else slice(k, k + 4)
                    cols = bass.ds(col, n) if not isinstance(col, int) else slice(col, col + n)
                    unit(w[:, rows, cols], 4, n)
                    if mods and j >= 2:
                        mod_unit(*mods[j - 2])

            for t in range(T):
                sp.dma_start(h[:, t, :], a["x"][0, t * P:(t + 1) * P, :]).then_inc(x_landed[t], 16)
            vecs = [(a["norm_mix"][0], 0, 0), (a["norm_ffn"][0], 16, 0), (a["norm_ple"][0], 32, 0),
                    (a["attn_norm_g_2"][0], 48, 0), (a["mlp_norm_g_2"][0], 64, 0), (a["c_2"][0], 80, 0),
                    (a["mla_q_norm_g_2"][0], 96, 0), (a["mla_kv_norm_g_2"][0], 99, 0),
                    (a["b_mod_2"][0], 0, 1)]
            for v, r, j in vecs:
                n = v.shape[0] // P
                sp.dma_start(vrow[r:r + n, j, :], v.rearrange("(r c) -> r c", c=P)).then_inc(rows_landed, 16)
            sp.dma_start(vrow[96:128, 1, :], a["nsa_cmp_pos_k"][0]).then_inc(rows_landed, 16)
            sp.dma_start(vrow[0:32, 2, :], a["nsa_cmp_pos_v"][0]).then_inc(rows_landed, 16)

            group(w_in, 0, mods=[mods_of(0), mods_of(1)])
            group(w_in, NW, mods=section_rows(2, 0))
            with loop(sp, c, 5, {lower_ready: 8, mod_added: 2}) as i:
                group(w_in, i * NW + 2 * NW, mods=section_rows(i * 2 + 4, 0))
            group(w_in, KV_COLS["kw"], mods=[mods_of(14), mods_of(15)])
            for name, values in (("k", "vs"), ("v", "vw")):
                group(w_in, KV_COLS[values])
                w1 = a[f"nsa_cmp_w1_{name}"][0].rearrange("(l p) n -> p l n", p=P)
                for u in range(2):
                    unit(w1[:, 16 * u:16 * u + 16, :], 16, P, (direct_used, 1))
                unit(a[f"nsa_cmp_w2_{name}"][0].rearrange("p (k n) -> p k n", k=1), 1, P, (direct_used, 1))
            unit(w_in[:, :, KV_COLS["gates"]:KV_COLS["gates"] + 48], KC, 48, (lower_ready, 1))
            group(w_out, 0)
            sp.wait_ge(pv_done, len(NSA_JOBS))
            for rows_cols in section_rows(0, 1):
                mod_unit(*rows_cols)
            with loop(sp, c, NG - 1, {lower_ready: 8, mod_added: 2}) as i:
                group(w_out, i * NW + NW, mods=section_rows(i * 2 + 2, 1))

            def quarter(w1, w2, q, mods):
                for g in range(NG):
                    group(w1, q * D + g * NW, mods=mods and mods[2 * g:2 * g + 2])
                for g in range(NG):
                    group(w2, g * NW, row=q * KC, mods=mods and mods[8 + 2 * g:10 + 2 * g])

            def quarter_mods(q):
                rows = [slice((8 + j) % KC * P, ((8 + j) % KC + 1) * P) for j in range(KC)]
                return [(rows[j], bass.ds((q + (1 if j < 8 else 2)) * D, D) if not isinstance(q, int)
                         else slice((q + (1 if j < 8 else 2)) * D, (q + (1 if j < 8 else 2) + 1) * D))
                        for j in range(KC)]

            quarter(ffn1, ffn2, 0, quarter_mods(0))
            with loop(sp, c, QUARTERS - 1, {lower_ready: 64, mod_added: 16}) as i:
                quarter(ffn1, ffn2, i + 1, quarter_mods(i + 1))
            for u in range(2):
                unit(w_embed[:, 0:2, u * 1024:(u + 1) * 1024], 2, 1024)
            with loop(sp, c, NG, {lower_ready: 8, mod_added: 2}) as i:
                group(w_gate, i * NW, mods=section_rows(i * 2 + 8, 5))
            for g in range(3):
                group(w_in2, g * NW)
            group(w_in2, 3 * NW, n=320)
            for g in range(3):
                unit(w_uq[:, 0:3, g * NW:(g + 1) * NW], 3, NW)
            unit(w_ukv[:, 0:1, :], 1, D)
            group(w_out2, 0)
            with loop(sp, c, NG - 1, {lower_ready: 8}) as i:
                group(w_out2, i * NW + NW)
            quarter(ffn1b, ffn2b, 0, None)
            with loop(sp, c, QUARTERS - 1, {lower_ready: 64}) as i:
                quarter(ffn1b, ffn2b, i + 1, None)
            for t, (j, (o, n)) in [(t, x) for t in range(T) for x in enumerate(HALVES)]:
                sp.wait_ge(h_ready, 2 * T + 2 * t + j + 1)
                sp.dma_start(a["out"][0, t * P:(t + 1) * P, o:o + n], h[:, t, o:o + n]).then_inc(stored, 16)
            sp.wait_ge(stored, 16 * 2 * T)

        @block.gpsimd
        def _(pool):
            c = Counts()

            def link(op):
                op.then_inc(pool_step, 1)
                pool.wait_ge(pool_step, c.next(pool_step))

            nc.gpsimd.memset(ident[:], 0.0)
            nc.gpsimd.memset(flip[:], 0.0)
            nc.gpsimd.memset(causal_b[:], 0.0)
            nc.gpsimd.memset(cmask[:, 0], 0.0)
            nc.gpsimd.memset(cmask[:, 1], 1.0)
            nc.gpsimd.memset(eps[:], EPS)
            link(nc.gpsimd.memset(ones[:], 1.0))
            nc.gpsimd.affine_select(out=flip[:], in_=flip[:], compare_op=ALU.not_equal, fill=1.0,
                                    base=-(P - 1), pattern=[[1, P]], channel_multiplier=1)
            link(nc.gpsimd.affine_select(out=ident[:], in_=ident[:], compare_op=ALU.not_equal, fill=1.0,
                                         base=0, pattern=[[-1, P]], channel_multiplier=1))
            nc.gpsimd.affine_select(out=causal_b[:], in_=causal_b[:], compare_op=ALU.is_ge, fill=NEG,
                                    base=0, pattern=[[-1, P]], channel_multiplier=1)
            for m, fill in ((0, NEG), (1, 0.0)):
                nc.gpsimd.affine_select(out=cmask[:, m], in_=cmask[:, m], compare_op=ALU.is_ge, fill=fill,
                                        base=-(CMP_LEN - 1), pattern=[[P, T], [-CMP_STRIDE, N_CMP]],
                                        channel_multiplier=1)
            nc.gpsimd.tensor_copy(ident_b[:], ident[:]).then_inc(consts, 1)
            pool.dma_start(angle[:, 0], a["cos"].rearrange("(t p) f -> p t f", p=P)).then_inc(aux_landed, 16)
            pool.dma_start(angle[:, 1], a["sin"].rearrange("(t p) f -> p t f", p=P)).then_inc(aux_landed, 16)
            pool.dma_start(sinks[:], a["swa_sinks_2"][0].partition_broadcast(P)).then_inc(aux_landed, 16)
            pool.dma_start(onehot[:], a["bucket_onehot"]).then_inc(aux_landed, 16)
            pool.dma_start(relb[:], a["rel_bias_2"]).then_inc(aux_landed, 16)
            nc.gpsimd.memset(table[:], NEG).then_inc(bias_placed, 1)
            pool.wait_ge(bias_table, 1)
            pool.dma_start(scratch, table[:]).then_inc(bias_stored, 16)
            pool.wait_ge(bias_stored, 16)
            pool.dma_start(prow[:], a["p"][0, 0].rearrange("(t p) f -> p t f", p=P)).then_inc(p_landed, 16)
            pool.wait_ge(step_used, STEPS_FFN)
            pool.dma_start(gainrow[:], a["norm_final"].partition_broadcast(P)).then_inc(gain_landed, 16)
            pool.wait_ge(mod_rows, 1)
            pool.dma_start(rows_scratch, modrow[:]).then_inc(mod_rows_stored, 16)
            pool.wait_ge(mod_rows_stored, 16)
            pool.wait_ge(evacuated, GROUPS_UKV)
            for i in range(4):
                if i >= 2:
                    pool.wait_ge(scores, len(NSA_JOBS) + i - 1)
                src = bass.AP(scratch.tensor, 4 * i * GT, [[1, P], [GT, 4], [1, 2 * P]])
                pool.dma_start(toe[i % 2][:], src).then_inc(toe_landed[i % 2], 16)
            pool.wait_ge(pv_done, len(NSA_JOBS) + 4)
            for m, gain in ((2, gain1), (5, gain2)):
                src = bass.AP(rows_scratch.tensor, m * D, [[0, P], [1, D]])
                pool.dma_start(gain[:], src).then_inc(gain_row, 16)
            pool.wait_ge(step_used, STEPS_FFN2)
            pool.dma_start(gainrow[:], a["final_norm_g_2"].partition_broadcast(P)).then_inc(gain_landed, 16)

        @block.scalar
        def _(act):
            c = Counts()
            st = dict(unit=0, step=0)

            def link(op):
                op.then_inc(act_step, 1)
                act.wait_ge(act_step, c.next(act_step))

            def split(K, N, spec, first):
                k0, nk, n0, nn = spec
                if first:
                    slot = st["unit"] % SLOTS
                    act.wait_ge(landed[slot], c.next(landed[slot], 16))
                    st["unit"] += 1
                slot = (st["unit"] - 1) % SLOTS
                if st["step"] >= SLOTS:
                    act.wait_ge(step_used, c.at("steps", 1 - SLOTS))
                src = slot_view(raw, slot, K, N)[:, k0:k0 + nk, n0:n0 + nn]
                dst = slot_view(upper, st["step"] % SLOTS, nk, nn)
                nc.scalar.activation(dst, src, ACT.Copy).then_inc(upper_ready, 1)
                st["step"] += 1
                c.next("steps")

            def split_ahead():
                for s in range(SLOTS):
                    split(4, NW, std_steps(NW)[s % 2], s % 2 == 0)

            def group(before=(), n=NW, start=0):
                for s in range(start, 8):
                    split(4, n, std_steps(n)[s % 2], s % 2 == 0)
                    if 2 <= s < 2 + len(before):
                        before[s - 2](s + 1)

            def group_summed(ahead):
                act.wait_ge(step_used, c.at("steps", -ahead))

            def none(ahead):
                c.next("groups")

            def copy_half(parity):
                def f(ahead):
                    group_summed(ahead)
                    act.wait_ge(evacuated, c.at("groups"))
                    nc.scalar.activation(half[:], ps[:, 4 * parity:4 * parity + 4, S:2 * S],
                                         ACT.Copy).then_inc(half_copied, 1)
                    c.next("groups")
                return f

            def first_half(ahead):
                group_summed(ahead)
                nc.scalar.activation(half[:], ps[:, 0:4, S:2 * S], ACT.Copy).then_inc(half_copied, 1)
                c.next("groups")

            def upper_hidden(g):
                def f(ahead):
                    act.wait_ge(squared, c.next(squared))
                    nc.scalar.activation(hidden[:, 4 * g:4 * g + 4, 0, :], summed[:],
                                         ACT.Copy).then_inc(hidden_upper, 1)
                return f

            def square(t, i, o, n, sem_):
                out = summed[:].rearrange("p a s -> p (a s)")[:, 0:n]
                nc.scalar.activation(out, h[:, t, o:o + n], ACT.Square,
                                     accum_out=sumsq[:, t, i:i + 1]).then_inc(sem_, 1)
                act.wait_ge(sem_, c.next(sem_))

            def squares_ahead():
                link(nc.scalar.activation(norm[:, 1, 2:3], eps[:, 0:1], ACT.Sqrt))
                if st_groups():
                    act.wait_ge(evacuated, c.at("groups"))
                for i, (o, n) in enumerate(PIECES[:-1]):
                    square(0, i, o, n, act_step)

            def root():
                act.wait_ge(mean_ready, c.next(mean_ready))
                nc.scalar.activation(norm[:, 1, 0:2], norm[:, 0, 0:2], ACT.Sqrt, bias=eps[:, 0:1],
                                     scale=1.0 / D).then_inc(rms_ready, 1)
                c.next(rstd_ready)

            def root_mean(first):
                first()
                square(0, len(PIECES) - 1, *PIECES[-1], squares)
                root()

            def root_mean_rescaled():
                for t in range(T):
                    for i, (o, n) in enumerate(HALVES):
                        act.wait_ge(h_ready, 2 * t + i + 1)
                        square(t, i, o, n, act_step if (t, i) != (T - 1, 1) else squares)
                root()

            def to_features(gain, shift=None, ahead=True):
                act.wait_ge(rstd_ready, c.at(rstd_ready))
                b0 = 4 * ((st_groups() + 1) % 2)

                def scale(q):
                    nc.scalar.activation(xn[:, 0, q * NW:(q + 1) * NW], h[:, 0, q * NW:(q + 1) * NW], ACT.Copy,
                                         scale=norm[:, 2, 0:1]).then_inc(scaled_a, 1)

                scale(0)
                scale(1)
                for b in range(BANKS):
                    if b in (1, 3):
                        scale((b + 3) // 2)
                    if b == 0 and shift is not None:
                        act.wait_ge(mod_cols, c.next(mod_cols))
                    act.wait_ge(turned, c.next(turned))
                    for k in (2 * b, 2 * b + 1):
                        src = ps[:, b0 + b % 4, S * (k % 2):S * (k % 2) + S]
                        if shift is None:
                            op = nc.scalar.activation(xs[:, k, 0, :], src, ACT.Copy, scale=gain[:, k:k + 1])
                        else:
                            op = nc.scalar.activation(xs[:, k, 0, :], src, ACT.Identity, scale=gain[:, k:k + 1],
                                                      bias=shift[:, k:k + 1])
                    op.then_inc(x_upper, 1)
                    if b >= SLOTS or not ahead:
                        split(4, NW, std_steps(NW)[b % 2], b % 2 == 0)

            def st_groups():
                return c.n.get("groups", 0)

            def all_evacuated():
                act.wait_ge(evacuated, c.at("groups"))

            act.wait_ge(consts, 1)
            act.wait_ge(x_landed[0], 16)
            squares_ahead()
            root_mean(lambda: None)
            split_ahead()
            act.wait_ge(cols_ready, 1)
            to_features(vcol[:, COL["mix"]:COL["mix"] + KC])
            nc.scalar.activation(silu_c[:], vcol[:, COL["c"]:COL["c"] + KC], ACT.Sigmoid).then_inc(c_sigmoid, 1)
            group([first_half])
            with loop(act, c, 3, {"steps": 16, "groups": 2, **{l: 32 for l in landed}}):
                group([copy_half(1)])
                group([copy_half(0)])
            def direct_units():
                for _ in range(3):
                    c.next(landed[st["unit"] % SLOTS], 16)
                    st["unit"] += 1

            def hidden_sigmoid(i):
                def f(ahead):
                    act.wait_ge(direct_used, 3 * i + 2)
                    nc.scalar.activation(csig[:], ps[:, 2 + i, 0:NSA_G * N_CMP], ACT.Sigmoid).then_inc(cmp_sigmoid, 1)
                return f

            group([copy_half(1)])
            direct_units()
            group([hidden_sigmoid(0)])
            direct_units()
            split(KC, 48, (0, KC, 0, 48), True)
            for _ in range(3):
                none(0)
            hidden_sigmoid(1)(0)
            group_summed(0)
            nc.scalar.activation(gsum[:, 0, :], ps[0:48, 0, S:2 * S], ACT.Copy).then_inc(gate_half, 1)
            act.wait_ge(gate_turned, 1)
            nc.scalar.activation(gates[:], ps[:, 1, 0:2 * P].rearrange("p (t n) -> p t n", t=T)[:, :, 0:48],
                                 ACT.Sigmoid).then_inc(gate_ready, 1)
            act.wait_ge(c_shifted, 1)
            cp = cprob[:].rearrange("p t h n -> p (t h) n")[:, :, 0:N_CMP]
            nc.scalar.activation(cp, cp, ACT.Exp).then_inc(c_exp, 1)

            def compressed_turned():
                act.wait_ge(c_turned, 1)
                nc.scalar.activation(cprobT[:].rearrange("p g s -> p (g s)"), ps[:, 5:7, :].rearrange("p b n -> p (b n)"),
                                     ACT.Copy).then_inc(c_prob, 1)

            def job_exps(n, kind, scale):
                act.wait_ge(bias_ready, c.next(bias_ready))
                if kind == "swa":
                    nc.scalar.activation(stat[:, 4, n % 2, :], stat[:, 4, n % 2, :], ACT.Exp)
                for t in range(T):
                    for j in range(HPG):
                        w = P * (t + 1)
                        src = ps[:, 0, P * j:P * j + P] if t == 0 else ps[:, 1 + j // 2, S * (j % 2):S * (j % 2) + S]
                        o = P * HPG * t + w * j
                        col = HPG * t + j
                        op = nc.scalar.activation(prob[:, n % 2, o:o + w], src, ACT.Exp,
                                                  bias=stat[:, 1, n % 2, col:col + 1], scale=scale,
                                                  accum_out=stat[:, 2, n % 2, col:col + 1])
                op.then_inc(exps, 1)

            def job_turned(n):
                act.wait_ge(prob_turned, c.next(prob_turned))
                if n >= 2:
                    act.wait_ge(pv_done, c.next(pv_done))
                nc.scalar.activation(probT[:, n % 2, :], ps[:, 3:6, :].rearrange("p b n -> p (b n)"),
                                     ACT.Copy).then_inc(probT_ready, 1)

            def mix_parts(jobs, n, base):
                kind, i, b = jobs[n]
                if kind == "nsa":
                    return (4 * i, 4, ps[:, 6:8, :].rearrange("p b (c s) -> p (b c) s", s=S)) if b else None
                if kind == "swa":
                    return 2 * i, 2, ps[:, 6 + i % 2, :].rearrange("p (c s) -> p c s", s=S)
                return 8 + 4 * i, 4, ps[:, 6:8, :].rearrange("p b (c s) -> p (b c) s", s=S)

            def attention(jobs, base, scale_of, after_first=None):
                for n in range(len(jobs) + 1):
                    if n < len(jobs):
                        job_exps(base + n, jobs[n][0], scale_of(jobs[n][0]))
                    if n == 0 and after_first:
                        after_first()
                    if n >= 1:
                        part = mix_parts(jobs, n - 1, base)
                        if part:
                            k, m, src = part
                            act.wait_ge(pv_done, base + n)
                            nc.scalar.activation(xs[:, k:k + m, 0, :], src, ACT.Copy).then_inc(mix_upper, 1)
                    if n < len(jobs):
                        job_turned(base + n)

            SCALE = {"nsa": DH ** -0.5, "swa": 1.0, "mla": QK ** -0.5}
            attention(NSA_JOBS, 0, SCALE.get, compressed_turned)

            def pin_upper(ahead):
                act.wait_ge(p_turned, 1)
                nc.scalar.activation(pin[:, :, 0, :], ps[:, 2, :].rearrange("p (k s) -> p k s", s=S),
                                     ACT.Copy).then_inc(p_upper, 1)

            group([pin_upper])
            for g in range(1, NG):
                group([none])

            def norm_behind(pending=none):
                squares_ahead()
                split_ahead()
                pending(SLOTS)
                root_mean(all_evacuated)

            norm_behind()

            def quarter(pending, p0, start):
                for g in range(NG):
                    if g or not start:
                        group(pending)
                    pending = [copy_half((p0 + g) % 2), upper_hidden(g)]
                for g in range(NG):
                    group(pending)
                    pending = [none]

            def ffn():
                p0 = st_groups() % 2
                quarter([], p0, 8)
                with loop(act, c, QUARTERS - 1, {"steps": 64, "groups": 8, squared: 4,
                                                 **{l: 128 for l in landed}}):
                    quarter([none], p0, 0)

            to_features(vcol[:, COL["ffn"]:COL["ffn"] + KC])
            ffn()

            squares_ahead()
            for u in range(2):
                for s in range(2):
                    split(2, 1024, (0, 2, 512 * s, 512), s == 0)
            none(0)
            root_mean(all_evacuated)
            for g in range(NG):
                none(0)
            to_features(vcol[:, COL["ple"]:COL["ple"] + KC], ahead=False)

            def gate_of(g):
                def f(ahead):
                    group_summed(ahead)
                    act.wait_ge(evacuated, c.at("groups"))
                    b = 4 * (c.n["groups"] % 2)
                    nc.scalar.activation(half[:].rearrange("p (t a) s -> p t (a s)", t=T), ps[:, b:b + 2, :],
                                         ACT.Sigmoid).then_inc(ple_gate, 1)
                    c.next("groups")
                return f

            for g in range(1, NG):
                group([gate_of(g - 1)])
            norm_behind(gate_of(NG - 1))

            root_mean_rescaled()
            p0 = st_groups() % 2
            to_features(affine[:], modcol[:, 0, :])
            group([copy_half(p0)])
            group([copy_half(1 - p0)])
            group([none], n=320)
            none(0)
            act.wait_ge(evacuated, c.at("groups"))
            act.wait_ge(lat_squares, 1)
            nc.scalar.activation(norm[:, 1, 0:2], norm[:, 0, 0:2], ACT.Sqrt, bias=eps[:, 0:1], scale=1.0 / Q_RANK)
            nc.scalar.activation(norm[:, 1, 2:4], norm[:, 0, 2:4], ACT.Sqrt, bias=eps[:, 0:1],
                                 scale=1.0 / KV_RANK).then_inc(lat_rms, 1)
            for k in range(4):
                act.wait_ge(lat_turned, k // 2 + 1)
                dst = cqs[:, k, 0, :] if k < 3 else ckvs[:, 0, 0, :]
                op = nc.scalar.activation(dst, ps[:, 4 + k // 2, S * (k % 2):S * (k % 2) + S], ACT.Copy,
                                          scale=vcol[:, COL["q"] + k:COL["q"] + k + 1])
                if k % 2:
                    op.then_inc(lat_upper, 1)
            for g in range(3):
                split(3, NW, (0, 2, 0, NW), True)
                split(3, NW, (2, 1, 0, NW), False)
                none(0)
            for s in range(2):
                split(1, D, (0, 1, 1024 * s, 1024), s == 0)
                group_summed(0)
                act.wait_ge(evacuated, c.at("groups"))
                nc.scalar.activation(half[:], ps[:, 0:4, S:2 * S], ACT.Copy).then_inc(half_copied, 1)
                none(0)
            for i, (dst, b, n) in enumerate(((qn[:].rearrange("p h s -> p (h s)"), 0, 4),
                                             (qr[:].rearrange("p h s -> p (h s)"), 4, 2),
                                             (ka[:].rearrange("p v a s -> p (v a s)"), 6, 2),
                                             (kr[:].rearrange("p a s -> p (a s)"), 0, 1))):
                act.wait_ge(heads_turned, i + 1)
                src = ps[:, b:b + n, :].rearrange("p b n -> p (b n)")
                nc.scalar.activation(dst, src, ACT.Copy).then_inc(heads_copied, 1)
            attention(LATE_JOBS, len(NSA_JOBS), SCALE.get)
            group()
            for g in range(1, NG):
                group([none])
            norm_behind()
            to_features(affine[:], modcol[:, 3, :])
            ffn()
            squares_ahead()
            none(0)
            root_mean(all_evacuated)

        @block.vector
        def _(dve):
            c = Counts()
            st = dict(unit=0, step=0, mod=0)

            def link(op):
                op.then_inc(dve_step, 1)
                dve.wait_ge(dve_step, c.next(dve_step))

            def split(K, N, spec, first):
                k0, nk, n0, nn = spec
                st["unit"] += first
                slot = (st["unit"] - 1) % SLOTS
                dve.wait_ge(upper_ready, c.next(upper_ready))
                src = slot_view(raw, slot, K, N)[:, k0:k0 + nk, n0:n0 + nn]
                up, low = (slot_view(x, st["step"] % SLOTS, nk, nn) for x in (upper, lower))
                nc.vector.tensor_tensor(low, src, up, ALU.subtract).then_inc(lower_ready, 1)
                st["step"] += 1
                c.next("steps")

            def add_mod(k):
                slot = st["mod"] % 2
                dve.wait_ge(mod_landed[slot], c.next(mod_landed[slot], 16))
                if st["mod"]:
                    dve.wait_ge(mod_added, c.at(mod_added))
                w, s = modraw[:, slot, :], silu_c[:, bass.ds(k, 1)]
                if isinstance(k, int) and k == 0:
                    op = nc.vector.tensor_scalar(modacc[:], w, s, None, ALU.mult)
                else:
                    op = nc.vector.scalar_tensor_tensor(modacc[:], w, s, modacc[:], ALU.mult, ALU.add)
                op.then_inc(mod_added, 1)
                c.next(mod_added)
                st["mod"] += 1

            def store_mod(m):
                dve.wait_ge(mod_summed, c.next(mod_summed))
                if isinstance(m, int):
                    dst, b = modcol[:, m, :], vcol[:, COL["b"] + KC * m:COL["b"] + KC * (m + 1)]
                else:
                    dst, b = modcol[:, bass.ds(m, 1), :].rearrange("p a k -> p (a k)"), vcol[:, bass.ds(m * KC + COL["b"], KC)]
                nc.vector.tensor_tensor(dst, ps[:, 6, 0:KC], b, ALU.add).then_inc(mod_stored, 1)

            def split_ahead(first, last):
                for s in range(first, last):
                    split(4, NW, std_steps(NW)[s % 2], s % 2 == 0)

            def group(before=(), n=NW, mods=None, store=None, at=(3, 6)):
                for s in range(8):
                    split(4, n, std_steps(n)[s % 2], s % 2 == 0)
                    if 2 <= s < 2 + len(before):
                        before[s - 2](s + 1)
                    if s == 3 and store is not None:
                        store_mod(store)
                    if mods is not None and s in at:
                        add_mod(mods + (s == at[1]))

            def group_summed(ahead):
                dve.wait_ge(step_used, c.at("steps", -ahead))

            def done(op):
                op.then_inc(evacuated, 1)
                c.next("groups")

            def own_before():
                if c.n.get("groups", 0):
                    dve.wait_ge(evacuated, c.at("groups"))

            def columns_out(parity, dst):
                def f(ahead):
                    dve.wait_ge(half_copied, c.next(half_copied))
                    done(nc.vector.tensor_tensor(dst, ps[:, 4 * parity:4 * parity + 4, 0:S], half[:], ALU.add))
                return f

            def square(parity):
                def f(ahead):
                    dve.wait_ge(half_copied, c.next(half_copied))
                    done(nc.vector.tensor_tensor(summed[:], ps[:, 4 * parity:4 * parity + 4, 0:S], half[:], ALU.add))
                    own_before()
                    nc.vector.scalar_tensor_tensor(summed[:], summed[:], 0.0, summed[:], ALU.max,
                                                   ALU.mult).then_inc(squared, 1)
                return f

            def lower_hidden(g):
                def f(ahead):
                    dve.wait_ge(hidden_upper, c.next(hidden_upper))
                    nc.vector.tensor_tensor(hidden[:, 4 * g:4 * g + 4, 1, :], summed[:],
                                            hidden[:, 4 * g:4 * g + 4, 0, :], ALU.subtract).then_inc(hidden_ready, 1)
                return f

            def rows_of(parity):
                return ps[:, 4 * parity:4 * parity + 2, :]

            def add_rows(parity, g, gain=None):
                def f(ahead):
                    group_summed(ahead)
                    hv = h[:, :, g * NW:(g + 1) * NW]
                    own_before()
                    if gain is None:
                        done(nc.vector.tensor_tensor(hv, rows_of(parity), hv, ALU.add))
                        return
                    gv = gain[:, g * NW:(g + 1) * NW].unsqueeze(1).to_broadcast([P, T, NW])
                    sv = half[:].rearrange("p (t a) s -> p t (a s)", t=T)
                    link(nc.vector.tensor_tensor(sv, rows_of(parity), gv, ALU.mult))
                    done(nc.vector.tensor_tensor(hv, sv, hv, ALU.add))
                return f

            def copy_rows(parity, dst):
                def f(ahead):
                    group_summed(ahead)
                    done(nc.vector.tensor_copy(dst, rows_of(parity)[:, :, 0:dst.shape[-1]]))
                return f

            def square_piece(i, junk, sem_):
                o, n = PIECES[i]
                v = h[:, 1, o:o + n]
                nc.vector.tensor_tensor_reduce(junk[:, 0:n], v, v, 1.0, 0.0, ALU.mult, ALU.add,
                                               sumsq[:, 1, i:i + 1]).then_inc(sem_, 1)
                dve.wait_ge(sem_, c.next(sem_))

            half_flat = half[:].rearrange("p a s -> p (a s)")

            def squares_ahead(junk=half_flat):
                own_before()
                for i in range(len(PIECES) - 1):
                    square_piece(i, junk, squares_v)

            def mean(pieces):
                dve.wait_ge(squares, c.next(squares))
                nc.vector.tensor_reduce(norm[:, 0, 0:2], sumsq[:, :, 0:pieces], AX.X, ALU.add).then_inc(mean_ready, 1)
                dve.wait_ge(rms_ready, c.next(rms_ready))
                nc.vector.reciprocal(norm[:, 2, 0:2], norm[:, 1, 0:2]).then_inc(rstd_ready, 1)
                dve.wait_ge(rstd_ready, c.next(rstd_ready))

            def root_mean(first, junk=half_flat):
                first()
                square_piece(len(PIECES) - 1, junk, squares_v)
                mean(len(PIECES))

            def scale_tile(shift=None, gain=None):
                for q in range(4):
                    nc.vector.tensor_scalar(xn[:, 1, q * NW:(q + 1) * NW], h[:, 1, q * NW:(q + 1) * NW],
                                            norm[:, 2, 1:2], None, ALU.mult).then_inc(scaled_v, 1)
                if shift is not None:
                    nc.vector.scalar_tensor_tensor(affine[:], shift[1], 1.0, gain, ALU.add, ALU.mult).then_inc(mod_cols, 1)
                    dve.wait_ge(mod_cols, c.next(mod_cols))

            def to_features(gain, shift=None, ahead=True, mods=None):
                b0 = 4 * ((c.n.get("groups", 0) + 1) % 2)
                for b in range(BANKS):
                    dve.wait_ge(x_upper, c.next(x_upper))
                    for k in (2 * b, 2 * b + 1):
                        src = ps[:, b0 + b % 4, S * (k % 2):S * (k % 2) + S]
                        if shift is None:
                            op = nc.vector.scalar_tensor_tensor(xs[:, k, 1, :], src, gain[:, k:k + 1], xs[:, k, 0, :],
                                                                ALU.mult, ALU.subtract)
                        else:
                            op = nc.vector.tensor_scalar(tmp[:, k % 2, :], src, affine[:, k:k + 1],
                                                         shift[0][:, k:k + 1], ALU.mult, ALU.add)
                    if shift is not None:
                        link(op)
                        op = nc.vector.tensor_tensor(xs[:, 2 * b:2 * b + 2, 1, :], tmp[:], xs[:, 2 * b:2 * b + 2, 0, :],
                                                     ALU.subtract)
                    op.then_inc(x_ready, 1)
                    if shift is not None:
                        dve.wait_ge(x_ready, c.at(x_ready, b + 1))
                    if b >= SLOTS or not ahead:
                        split(4, NW, std_steps(NW)[b % 2], b % 2 == 0)
                    if mods is not None and b in (5, 7):
                        add_mod(mods + (b == 7))
                c.next(x_ready, BANKS)

            def final_norm(gain_wait):
                dve.wait_ge(gain_landed, gain_wait)
                for t in range(T):
                    for o, n in HALVES:
                        nc.vector.scalar_tensor_tensor(h[:, t, o:o + n], h[:, t, o:o + n], norm[:, 2, t:t + 1],
                                                       gainrow[:, o:o + n], ALU.mult, ALU.mult).then_inc(h_ready, 1)
                dve.wait_ge(h_ready, c.next(h_ready, 2 * T))

            dve.wait_ge(x_landed[1], 16)
            squares_ahead()
            root_mean(lambda: None)
            scale_tile()
            dve.wait_ge(rows_turned, 1)
            nc.vector.tensor_copy(vcol[:, 0:100], ps[:, 0, 0:100])
            nc.vector.tensor_copy(vcol[:, P:], ps[:, 0, P:2 * P + CMP_LEN]).then_inc(cols_ready, 1)
            dve.wait_ge(cols_ready, 1)
            split_ahead(0, SLOTS)
            to_features(vcol[:, COL["mix"]:COL["mix"] + KC])
            dve.wait_ge(c_sigmoid, 1)
            link(nc.vector.tensor_tensor(silu_c[:], silu_c[:], vcol[:, COL["c"]:COL["c"] + KC], ALU.mult))
            add_mod(0)
            add_mod(1)

            def nothing(ahead):
                pass

            def bias_table_out(ahead):
                dve.wait_ge(bias_sum, 1)
                dve.wait_ge(bias_placed, 1)
                nc.vector.tensor_copy(table[:, P - 1:2 * P - 1], ps[0:SWA_HEADS, 7, 0:P]).then_inc(bias_table, 1)

            def heads_out(parity, i):
                return columns_out(parity, heads[:, bass.ds(i * 4, 4), :])

            group([heads_out(0, 0)], mods=2)
            per = {"steps": 16, "groups": 2, upper_ready: 16, half_copied: 2, mod_added: 4,
                   mod_landed[0]: 32, mod_landed[1]: 32}
            with loop(dve, c, 3, per) as i:
                group([heads_out(1, i * 2 + 1)], mods=i * 4 + 4)
                group([heads_out(0, i * 2 + 2)], mods=i * 4 + 6)
            def clear(what):
                def f(ahead):
                    own_before()
                    link(nc.vector.memset(what, 0.0))
                return f

            def blocks(i, half_):
                def f(ahead):
                    src = heads[:, 16 + 4 * i:20 + 4 * i, :].rearrange("p g (m b) -> p g m b", b=CMP_STRIDE)
                    dst = blk[:, CMP_STRIDE * half_:CMP_STRIDE * (half_ + 1)].rearrange("p l g n -> p g n l")
                    o = COL["kv"[i]] + CMP_STRIDE * half_
                    for g in range(NSA_G):
                        op = nc.vector.tensor_tensor(dst[:, g], src[:, g, half_:half_ + N_CMP],
                                                     vcol[:, o:o + CMP_STRIDE].unsqueeze(1).to_broadcast([P, N_CMP, CMP_STRIDE]),
                                                     ALU.add)
                    if half_:
                        op.then_inc(blk_ready, 1)
                return f

            def hidden_silu(i):
                def f(ahead):
                    dve.wait_ge(cmp_sigmoid, i + 1)
                    nc.vector.tensor_tensor(hid[:, :, 3 * CPAD:3 * CPAD + N_CMP],
                                            ps[:, 2 + i, 0:NSA_G * N_CMP].rearrange("p (g n) -> p g n", n=N_CMP),
                                            csig[:], ALU.mult).then_inc(hid_ready, 1)
                return f

            def keys_out(ahead):
                dve.wait_ge(direct_used, 3)
                nc.vector.tensor_copy(kcmp[:].rearrange("p g n -> p (g n)"), ps[:, 3, 0:P]).then_inc(cmp_stored, 1)

            group([heads_out(1, 7), clear(hid[:]), clear(cprob[:]), bias_table_out, blocks(0, 0), blocks(0, 1)],
                  store=0)
            st["unit"] += 3
            group([copy_rows(0, vtok[:, 0]), hidden_silu(0), keys_out, blocks(1, 0), blocks(1, 1)])
            st["unit"] += 3
            split(KC, 48, (0, KC, 0, 48), True)
            copy_rows(1, vtok[:, 1])(1)
            dve.wait_ge(c_scores, 1)
            flat = cprob[:].rearrange("p t h n -> p (t h) n")[:, :, 0:N_CMP]
            for t in range(T):
                op = nc.vector.scalar_tensor_tensor(
                    cprob[:, t, :, 0:N_CMP], ps[:, 7, S * t:S * t + S].rearrange("p (h n) -> p h n", n=16)[:, :, 0:N_CMP],
                    DH ** -0.5, cmask[:, 0, t].unsqueeze(1).to_broadcast([P, NSA_HEADS, N_CMP]), ALU.mult, ALU.add)
            link(op)
            link(nc.vector.tensor_reduce(cstat[:, 0, :], flat, AX.X, ALU.max))
            nc.vector.tensor_tensor(flat, flat, cstat[:, 0, :].unsqueeze(2).to_broadcast([P, T * NSA_HEADS, N_CMP]),
                                    ALU.subtract).then_inc(c_shifted, 1)
            hidden_silu(1)(0)
            dve.wait_ge(gate_half, 1)
            done(nc.vector.tensor_tensor(gsum[:, 1, :], ps[0:48, 0, 0:S], gsum[:, 0, :], ALU.add))
            own_before()
            nc.vector.tensor_copy(gsum[:, 0, :], gsum[:, 1, :]).then_inc(gate_sum, 1)
            dve.wait_ge(direct_used, 6)
            nc.vector.tensor_copy(vcmp[:].rearrange("p h n -> p (h n)"),
                                  ps[:, 3:7, :].rearrange("p b n -> p (b n)")).then_inc(cmp_stored, 1)
            dve.wait_ge(c_exp, 1)
            link(nc.vector.tensor_reduce(cstat[:, 1, :], flat, AX.X, ALU.add))
            link(nc.vector.reciprocal(cstat[:, 2, :], cstat[:, 1, :]))
            dve.wait_ge(gate_ready, 1)
            dve.wait_ge(bias_stored, 16)
            link(nc.vector.tensor_tensor(cstat[:, 2, :].rearrange("p (t h) -> p t h", t=T),
                                         cstat[:, 2, :].rearrange("p (t h) -> p t h", t=T),
                                         gates[:].rearrange("p t (h b) -> p t h b", b=3)[:, :, :, 0], ALU.mult))
            for t in range(T):
                op = nc.vector.tensor_tensor(cprob[:, t, :, 0:N_CMP], cprob[:, t, :, 0:N_CMP],
                                             cmask[:, 1, t].unsqueeze(1).to_broadcast([P, NSA_HEADS, N_CMP]), ALU.mult)
            link(op)
            nc.vector.tensor_tensor(flat, flat, cstat[:, 2, :].unsqueeze(2).to_broadcast([P, T * NSA_HEADS, N_CMP]),
                                    ALU.mult).then_inc(c_scaled, 1)

            def wide(n):
                return ps[:, 1:3, :].rearrange("p b (h k) -> p (b h) k", k=S)

            def attention(jobs, base):
                for n in range(len(jobs) + 1):
                    if n < len(jobs):
                        kind, i, b = jobs[n]
                        m, par = base + n, (base + n) % 2
                        dve.wait_ge(scores, m + 1)
                        nc.vector.tensor_reduce(stat[:, 0, par, 0:4], ps[:, 0, :].rearrange("p (h k) -> p h k", k=P), AX.X, ALU.max)
                        link(nc.vector.tensor_reduce(stat[:, 0, par, 4:8], wide(n), AX.X, ALU.max))
                        if kind == "swa":
                            sk = sinks[:, 4 * i:4 * i + 4].unsqueeze(1).to_broadcast([P, T, 4])
                            v = stat[:, 0, par, :].rearrange("p (t h) -> p t h", t=T)
                            link(nc.vector.tensor_tensor(v, v, sk, ALU.max))
                            nc.vector.tensor_tensor(stat[:, 4, par, :].rearrange("p (t h) -> p t h", t=T), sk, v, ALU.subtract)
                        scale = {"nsa": DH ** -0.5, "swa": 1.0, "mla": QK ** -0.5}[kind]
                        nc.vector.tensor_scalar(stat[:, 1, par, :], stat[:, 0, par, :], -scale, None,
                                                ALU.mult).then_inc(bias_ready, 1)
                        dve.wait_ge(exps, m + 1)
                        if kind == "swa":
                            link(nc.vector.tensor_tensor(stat[:, 2, par, :], stat[:, 2, par, :], stat[:, 4, par, :], ALU.add))
                        link(nc.vector.reciprocal(stat[:, 3, par, :], stat[:, 2, par, :]))
                        if kind == "nsa":
                            for t in range(T):
                                v = stat[:, 3, par, 4 * t:4 * t + 4]
                                op = nc.vector.tensor_tensor(v, v, gate_view(t, i, 1 + b), ALU.mult)
                            link(op)
                        for t in range(T):
                            w = P * (t + 1)
                            v = prob[:, par, 512 * t:512 * t + 4 * w].rearrange("p (h k) -> p h k", k=w)
                            r = stat[:, 3, par, 4 * t:4 * t + 4].unsqueeze(2).to_broadcast([P, 4, w])
                            op = nc.vector.tensor_tensor(v, v, r, ALU.mult)
                        op.then_inc(prob_ready, 1)
                    if n >= 1:
                        kind, i, b = jobs[n - 1]
                        if kind == "nsa" and not b:
                            continue
                        dve.wait_ge(mix_upper, c.next(mix_upper))
                        if kind == "swa":
                            k, w, src = 2 * i, 2, ps[:, 6 + i % 2, :].rearrange("p (c s) -> p c s", s=S)
                        else:
                            k, w = (4 * i if kind == "nsa" else 8 + 4 * i), 4
                            src = ps[:, 6:8, :].rearrange("p b (c s) -> p (b c) s", s=S)
                        nc.vector.tensor_tensor(xs[:, k:k + w, 1, :], src, xs[:, k:k + w, 0, :],
                                                ALU.subtract).then_inc(mix_ready, 1)

            attention(NSA_JOBS, 0)
            st_par = lambda: c.n["groups"] % 2

            def norm_behind(pending, junk, shift=None, gain_cols=None):
                squares_ahead(junk)
                split_ahead(0, SLOTS - 1)
                pending(SLOTS - 1)
                root_mean(own_before, junk)
                scale_tile(shift, gain_cols)
                split_ahead(SLOTS - 1, SLOTS)

            def project(gain=None, mods=None, first=(), **norm_args):
                p0 = st_par()
                for g in range(NG):
                    group([add_rows((p0 + g - 1) % 2, g - 1, gain)] if g else first,
                          mods=None if mods is None else mods + 2 * g, at=(3, 6) if g else (6, 7))
                norm_behind(add_rows((p0 + NG - 1) % 2, NG - 1, gain), junk=xn[:, 1, :], **norm_args)

            def pin_lower(ahead):
                dve.wait_ge(p_upper, 1)
                nc.vector.tensor_tensor(pin[:, :, 1, :], ps[:, 2, :].rearrange("p (k s) -> p k s", s=S), pin[:, :, 0, :],
                                        ALU.subtract).then_inc(p_ready, 1)

            project(mods=0, first=[pin_lower])

            def quarter(pending, p0, gain, m, first_split=False):
                for g in range(NG):
                    if g or not first_split:
                        group(pending, mods=None if m is None else 8 + 2 * g)
                    pending = [square((p0 + g) % 2), lower_hidden(g)]
                for g in range(NG):
                    group(pending, mods=None if m is None else 2 * g, store=m if g == 0 else None)
                    pending = [add_rows((p0 + g) % 2, g, gain)]

            def ffn(gain, modulated):
                p0 = st_par()
                last = add_rows((p0 + 1) % 2, NG - 1, gain)
                quarter([], p0, gain, 1 if modulated else None, first_split=True)
                per = {"steps": 64, "groups": 8, upper_ready: 64, half_copied: 4, hidden_upper: 4}
                if gain is not None:
                    per[dve_step] = 4
                if modulated:
                    per.update({mod_landed[0]: 128, mod_landed[1]: 128, mod_added: 16, mod_summed: 1})
                with loop(dve, c, QUARTERS - 1, per) as i:
                    quarter([last], p0, gain, i + 2 if modulated else None)
                return last

            to_features(vcol[:, COL["ffn"]:COL["ffn"] + KC], mods=8)
            last = ffn(None, True)

            squares_ahead()
            for g in range(NG - 1):
                split(2, 1024, (0, 2, 512 * (g % 2), 512), g % 2 == 0)
            last(NG - 1)
            split(2, 1024, (0, 2, 512, 512), False)
            root_mean(own_before)
            scale_tile()
            for g in range(NG):
                copy_rows(st_par(), embed[:, :, g * NW:(g + 1) * NW])(NG - 1 - g)
            to_features(vcol[:, COL["ple"]:COL["ple"] + KC], ahead=False, mods=8)

            def gated(g):
                def f(ahead):
                    sv, hv = half[:].rearrange("p (t a) s -> p t (a s)", t=T), h[:, :, g * NW:(g + 1) * NW]
                    dve.wait_ge(ple_gate, c.next(ple_gate))
                    link(nc.vector.tensor_tensor(sv, sv, embed[:, :, g * NW:(g + 1) * NW], ALU.mult))
                    done(nc.vector.tensor_tensor(hv, sv, hv, ALU.add))
                return f

            for g in range(1, NG):
                group([gated(g - 1)], mods=8 + 2 * g)
            squares_ahead(xn[:, 1, :])
            split_ahead(0, SLOTS - 1)
            gated(NG - 1)(SLOTS - 1)
            root_mean(own_before, xn[:, 1, :])
            final_norm(16)

            store_mod(5)
            dve.wait_ge(mod_stored, 6)
            mean(len(HALVES))
            scale_tile((modcol[:, 0, :], modcol[:, 1, :]), vcol[:, COL["attn"]:COL["attn"] + KC])
            split_ahead(SLOTS - 1, SLOTS)
            p0 = st_par()
            to_features(None, (modcol[:, 0, :], modcol[:, 1, :]))

            def scaled_queries(parity, dst):
                def f(ahead):
                    dve.wait_ge(half_copied, c.next(half_copied))
                    done(nc.vector.tensor_tensor(dst, ps[:, 4 * parity:4 * parity + 4, 0:S], half[:], ALU.add))
                    own_before()
                    link(nc.vector.tensor_scalar(dst, dst, SWA_D ** -0.5, None, ALU.mult))
                return f

            group([scaled_queries(p0, qa[:, 0:4, :])])
            group([scaled_queries(1 - p0, qa[:, 4:8, :])])
            group([copy_rows(p0, tok[:, :, 0:NW])], n=320)
            dve.wait_ge(mod_turned, 1)
            nc.vector.tensor_copy(modrow[:], ps[0:6 * KC, 6, 0:P]).then_inc(mod_rows, 1)
            copy_rows(1 - p0, tok[:, :, NW:832])(0)
            own_before()
            for t in range(T):
                for i, (o, n) in enumerate(((256, Q_RANK), (640, KV_RANK))):
                    link(nc.vector.tensor_tensor_reduce(half[:].rearrange("p a s -> p (a s)")[:, 0:n], tok[:, t, o:o + n],
                                                        tok[:, t, o:o + n], 1.0, 0.0, ALU.mult, ALU.add,
                                                        norm[:, 0, 2 * i + t:2 * i + t + 1]))
            nc.vector.memset(krope[:], 0.0)
            link(nc.vector.memset(kpad[:], 0.0))
            for t in range(T):
                v = tok[:, t, 0:P].rearrange("p (v d) -> p v d", v=SWA_KV)
                for i in range(2):
                    op = nc.vector.tensor_copy(kpad[:, t, :, i, i, :], v)
            op.then_inc(lat_squares, 1)
            dve.wait_ge(lat_rms, 1)
            link(nc.vector.reciprocal(norm[:, 2, :], norm[:, 1, :]))
            for i, (o, n) in enumerate(((256, Q_RANK), (640, KV_RANK))):
                for t in range(T):
                    v = tok[:, t, o:o + n]
                    op = nc.vector.tensor_scalar(v, v, norm[:, 2, 2 * i + t:2 * i + t + 1], None, ALU.mult)
            op.then_inc(lat_scaled, 1)
            for k in range(4):
                dve.wait_ge(lat_upper, k // 2 + 1)
                up, low = (cqs[:, k, j, :] if k < 3 else ckvs[:, 0, j, :] for j in range(2))
                nc.vector.scalar_tensor_tensor(low, ps[:, 4 + k // 2, S * (k % 2):S * (k % 2) + S],
                                               vcol[:, COL["q"] + k:COL["q"] + k + 1], up,
                                               ALU.mult, ALU.subtract).then_inc(lat_ready, 1)
            for g in range(3):
                split(3, NW, (0, 2, 0, NW), True)
                split(3, NW, (2, 1, 0, NW), False)
                copy_rows(st_par(), qb[:].rearrange("p t h d -> p t (h d)")[:, :, g * NW:(g + 1) * NW])(0)
            own_before()

            def rotate(x1, x2, o1, o2, cos, sin, t1, t2):
                nc.vector.tensor_tensor(t1, x1, cos, ALU.mult)
                link(nc.vector.tensor_tensor(t2, x2, sin, ALU.mult))
                link(nc.vector.tensor_tensor(o1, t1, t2, ALU.subtract))
                nc.vector.tensor_tensor(t1, x2, cos, ALU.mult)
                link(nc.vector.tensor_tensor(t2, x1, sin, ALU.mult))
                return nc.vector.tensor_tensor(o2, t1, t2, ALU.add)

            R = ROPE // 2
            dve.wait_ge(aux_landed, 16 * 5)
            for t in range(T):
                cos, sin = (angle[:, j, t].unsqueeze(1).to_broadcast([P, MLA_HEADS, R]) for j in range(2))
                link(rotate(qb[:, t, :, NOPE:NOPE + R], qb[:, t, :, NOPE + R:QK], qrope[:, t, :, 0:R],
                            qrope[:, t, :, R:ROPE], cos, sin, rope_t[:, 0], rope_t[:, 1]))
            for t in range(T):
                link(rotate(tok[:, t, 768:768 + R], tok[:, t, 768 + R:832], krope[:, t, 0, 0, 0:R], krope[:, t, 0, 0, R:ROPE],
                            angle[:, 0, t], angle[:, 1, t], rope_t[:, 0, 0], rope_t[:, 1, 0]))
            nc.vector.tensor_copy(krope[:, :, 1, 1, :], krope[:, :, 0, 0, :]).then_inc(roped, 1)
            for s in range(2):
                split(1, D, (0, 1, 1024 * s, 1024), s == 0)
                columns_out(0, kn[:, 4 * s:4 * s + 4, :])(0)
                c.n["groups"] -= 1
                dve.wait_ge(evacuated, c.at("groups", 1))
                nc.vector.tensor_copy(vb[:, :, 4 * s:4 * s + 4, :],
                                      ps[:, 4:6, :].rearrange("p t (h d) -> p t h d", d=VD)).then_inc(v_stored, 1)
                c.next("groups")
            attention(LATE_JOBS, len(NSA_JOBS))
            st["unit"] += 0

            dve.wait_ge(gain_row, 16 * 2)
            shift = (modcol[:, 3, :], modcol[:, 4, :])
            project(gain1, shift=shift, gain_cols=vcol[:, COL["mlp"]:COL["mlp"] + KC])
            to_features(None, shift)
            last = ffn(gain2, False)
            squares_ahead()
            last(0)
            root_mean(own_before)
            final_norm(32)

        @block.tensor
        def _(pe):
            c = Counts()
            st = dict(step=0)
            mm = nc.tensor.matmul

            def parity():
                return c.n.get("groups", 0) % 2

            def bank_free(p):
                if c.reg is not None or c.n.get("groups", 0) >= 2:
                    pe.wait_ge(evacuated, c.at("groups", -1))
                c.next("groups")

            def step(nk, nn, ready=None):
                if ready:
                    pe.wait_ge(*ready)
                pe.wait_ge(lower_ready, c.next(lower_ready))
                slot = st["step"] % SLOTS
                st["step"] += 1
                return slot_view(upper, slot, nk, nn), slot_view(lower, slot, nk, nn)

            def rows(x, par, k, kk, up, low, first, last):
                n = up.shape[-1]
                for t in range(T):
                    out = ps[:, 4 * par + t, 0:n]
                    xu, xl = (x[:, k, j, t * P:(t + 1) * P] for j in range(2))
                    mm(out, xu, up[:, kk, :], start=first, stop=False)
                    mm(out, xu, low[:, kk, :], start=False, stop=False)
                    op = mm(out, xl, up[:, kk, :], start=False, stop=last)
                return op

            def columns(x, par, k, kk, up, low, first, last):
                for f in range(4):
                    both = x[:, k].rearrange("p j s -> p (j s)")
                    mm(ps[:, 4 * par + f, :], up[:, kk, f * P:(f + 1) * P], both, start=first, stop=False,
                       skip_group_check=True)
                    op = mm(ps[:, 4 * par + f, 0:S], low[:, kk, f * P:(f + 1) * P], x[:, k, 0, :],
                            start=False, stop=last, skip_group_check=True)
                return op

            def group(form, x, n=NW, ready=None, between=None):
                p = st["par"] = (st["par"] + 1) % 2
                bank_free(p)
                for s in range(8):
                    if ready:
                        ready(s)
                    up, low = step(2, n)
                    for kk in range(2):
                        k = 2 * s + kk
                        op = form(x, p, k, kk, up, low, k == 0, k == KC - 1)
                    op.then_inc(step_used, 1)
                    if between and s in between:
                        between[s]()

            st["par"] = 1

            def group_turned(form, norms):
                p = st["par"] = (st["par"] + 1) % 2
                b0 = 4 * (1 - p)
                if c.n.get("groups", 0):
                    pe.wait_ge(evacuated, c.at("groups"))
                c.next("groups")

                def turn(b):
                    if b % 2 == 0:
                        pe.wait_ge(scaled_a, 4 * norms + b // 2 + 1)
                        pe.wait_ge(scaled_v, 4 * norms + b // 2 + 1)
                    for k in (2 * b, 2 * b + 1):
                        for t in range(T):
                            o = S * (k % 2) + t * P
                            op = nc.tensor.transpose(ps[:, b0 + b % 4, o:o + P], xn[:, t, k * P:(k + 1) * P], ident[:])
                    op.then_inc(turned, 1)

                for b in range(4):
                    turn(b)
                for s in range(8):
                    pe.wait_ge(x_ready, BANKS * norms + s + 1)
                    up, low = step(2, NW)
                    for kk in range(2):
                        k = 2 * s + kk
                        op = form(xs, p, k, kk, up, low, k == 0, k == KC - 1)
                    op.then_inc(step_used, 1)
                    if s + 4 < BANKS:
                        turn(s + 4)

            def sum_mod(wait, before=-1):
                pe.wait_ge(mod_added, wait)
                pe.wait_ge(evacuated, c.at("groups", before))
                for k in range(KC):
                    op = mm(ps[:, 6, k:k + 1], modacc[:, k * P:(k + 1) * P], ones[:, 0:1], start=True, stop=True)
                op.then_inc(mod_summed, 1)

            pe.wait_ge(consts, 1)
            pe.wait_ge(rows_landed, 16 * 11)
            for j, n in ((0, 100), (1, P), (2, CMP_LEN)):
                op = nc.tensor.transpose(ps[:, 0, j * P:j * P + n], vrow[0:n, j, :], ident[0:n, 0:n])
            op.then_inc(rows_turned, 1)
            pe.wait_ge(cols_ready, 1)

            group_turned(columns, 0)
            group(columns, xs)
            with loop(pe, c, 3, {lower_ready: 16, "groups": 2}):
                group(columns, xs)
                group(columns, xs)

            def sums_and_bias():
                sum_mod(KC)
                pe.wait_ge(aux_landed, 16 * 5)
                mm(ps[0:SWA_HEADS, 7, 0:P], relb[:], onehot[:], start=True, stop=True).then_inc(bias_sum, 1)

            UNITS = [(36, 37, 38), (43, 44, 45)]

            def raw_weights(u, l):
                if l == 0:
                    pe.wait_ge(landed[u % SLOTS], 16 * (u // SLOTS + 1))
                return raw[:, u % SLOTS, l * P:(l + 1) * P]

            def hidden_layer(i):
                pe.wait_ge(blk_ready, i + 1)
                for l in range(CMP_LEN):
                    op = mm(ps[:, 2 + i, 0:NSA_G * N_CMP], raw_weights(UNITS[i][l // 16], l % 16),
                            blk[:, l].rearrange("p g n -> p (g n)"), start=(l == 0), stop=(l == CMP_LEN - 1))
                    if l % 16 == 15:
                        op.then_inc(direct_used, 1)

            def compressed_keys():
                w = raw_weights(UNITS[0][2], 0)
                pe.wait_ge(hid_ready, 1)
                mm(ps[:, 3, 0:P], w, hid[:, :, 3 * CPAD:4 * CPAD], start=True, stop=True).then_inc(direct_used, 1)

            def compressed_scores():
                pe.wait_ge(cmp_stored, 1)
                for t in range(T):
                    for hh in range(NSA_HEADS):
                        op = mm(ps[:, 7, S * t + 16 * hh:S * t + 16 * hh + N_CMP], heads[:, hh, t * P:(t + 1) * P],
                                kcmp[:, hh // HPG, 0:N_CMP], start=True, stop=True)
                op.then_inc(c_scores, 1)

            group(rows, xs, between={1: sums_and_bias})
            hidden_layer(0)
            group(rows, xs, between={1: compressed_keys, 4: compressed_scores})
            hidden_layer(1)
            st["par"] = 0
            bank_free(0)
            up, low = step(KC, 48)
            for k in range(KC):
                mm(ps[0:48, 0, :], up[:, k, :], xs[:, k].rearrange("p j s -> p (j s)"), start=(k == 0), stop=False,
                   skip_group_check=True)
                op = mm(ps[0:48, 0, 0:S], low[:, k, :], xs[:, k, 0, :], start=False, stop=(k == KC - 1),
                        skip_group_check=True)
            op.then_inc(step_used, 1)
            pe.wait_ge(evacuated, c.at("groups", -1))
            w = raw_weights(UNITS[1][2], 0)
            pe.wait_ge(hid_ready, 2)
            for g in range(NSA_G):
                for j in range(HPG):
                    op = mm(ps[:, 3 + g, j * DH:(j + 1) * DH], hid[:, g, (3 - j) * CPAD:(7 - j) * CPAD], w,
                            start=True, stop=True)
            op.then_inc(direct_used, 1)
            pe.wait_ge(gate_sum, 1)
            for t in range(T):
                op = nc.tensor.transpose(ps[:, 1, P * t:P * t + 48], gsum[:, 0, t * P:(t + 1) * P], ident[0:48, 0:48])
            op.then_inc(gate_turned, 1)
            pe.wait_ge(cmp_stored, 2)
            pe.wait_ge(gate_ready, 1)

            def score(n, kind, i, b):
                if n:
                    pe.wait_ge(exps, n)
                if kind == "swa":
                    pe.wait_ge(toe_landed[i % 2], 16 * (i // 2 + 1))
                for t in range(T):
                    w = P * (t + 1)
                    for j in range(HPG):
                        out = ps[:, 0, P * j:P * j + P] if t == 0 else ps[:, 1 + j // 2, S * (j % 2):S * (j % 2) + S]
                        first = j == 0 if t == 0 else j % 2 == 0
                        hh = HPG * i + j
                        if kind == "nsa":
                            pairs = [(heads[:, hh, t * P:(t + 1) * P], heads[:, 24 + 4 * b + i, 0:w])]
                        elif kind == "swa":
                            pairs = [(qa[:, hh // 2, t * P:(t + 1) * P], ka[:, i // 2, hh % 2, 0:w])]
                        else:
                            pairs = [(qn[:, hh, t * P:(t + 1) * P], kn[:, hh, 0:w]),
                                     (qr[:, hh // 2, t * P:(t + 1) * P], kr[:, hh % 2, 0:w])]
                        for q, k in pairs:
                            op = mm(out, q, k, start=first, stop=False, skip_group_check=True)
                            first = False
                        if kind == "swa":
                            for kt in range(t + 1):
                                x0 = P * (t - kt)
                                op = mm(out[:, P * kt:P * kt + P], toe[i % 2][:, j, x0:x0 + P], flip[:], start=False,
                                        stop=True, skip_group_check=True)
                if kind != "swa":
                    mask = causal_b[:].unsqueeze(1)
                    mm(ps[:, 0, :], ident_b[:], mask.to_broadcast([P, 4, P]), start=False, stop=True, skip_group_check=True)
                    for b_ in (1, 2):
                        out = ps[:, b_, :].rearrange("p (h k) -> p h k", k=S)[:, :, P:S]
                        op = mm(out, ident_b[:], mask.to_broadcast([P, 2, P]), start=False, stop=True, skip_group_check=True)
                op.then_inc(scores, 1)

            def turn_probs(n):
                pe.wait_ge(prob_ready, n + 1)
                if n:
                    pe.wait_ge(probT_ready, n)
                for j in range(HPG):
                    bank, o = 3 + j // 2, S * (j % 2)
                    p = prob[:, n % 2, :]
                    nc.tensor.transpose(ps[:, bank, o:o + P], p[:, P * j:P * j + P], ident[:])
                    nc.tensor.transpose(ps[:, bank, o + P:o + S], p[:, 512 + S * j:512 + S * j + P], ident[:])
                    op = nc.tensor.transpose(ps[:, 5, P * j:P * j + P], p[:, 512 + S * j + P:512 + S * j + S], ident[:])
                op.then_inc(prob_turned, 1)

            def mix(n, kind, i, b):
                pe.wait_ge(probT_ready, n + 1)
                if kind != "nsa" or not b:
                    if c.n.get(mix_ready, 0):
                        pe.wait_ge(mix_ready, c.at(mix_ready))
                    c.next(mix_ready)
                for j in range(HPG):
                    hh = HPG * i + j
                    if kind == "swa":
                        r = slice(64 * (j % 2), 64 * (j % 2) + 64)
                        out = ps[r, 6 + i % 2, S * (j // 2):S * (j // 2) + S]
                        v = [tok[:, kt, P + 64 * (i // 2):P + 64 * (i // 2) + 64] for kt in range(T)]
                        first = j < 2
                    else:
                        out = ps[:, 6 + j // 2, S * (j % 2):S * (j % 2) + S]
                        first = j % 2 == 0 and not b
                        v = [vtok[:, b, kt, i * DH:(i + 1) * DH] if kind == "nsa" else vb[:, kt, hh, :] for kt in range(T)]
                    if kind == "nsa" and not b:
                        mm(out, vcmp[:, hh, :], cprobT[:, i, :], start=first, stop=False, skip_group_check=True)
                        first = False
                    mm(out, v[0], probT[:, n % 2, S * j:S * j + S], start=first, stop=False, skip_group_check=True)
                    op = mm(out[:, P:S], v[1], probT[:, n % 2, 1024 + P * j:1024 + P * j + P], start=False, stop=True,
                            skip_group_check=True)
                op.then_inc(pv_done, 1)

            def attention(jobs, base, after_first=None):
                score(base, *jobs[0])
                for n in range(len(jobs)):
                    if n + 1 < len(jobs):
                        score(base + n + 1, *jobs[n + 1])
                    if n == 0 and after_first:
                        after_first()
                    if n:
                        mix(base + n - 1, *jobs[n - 1])
                    turn_probs(base + n)
                mix(base + len(jobs) - 1, *jobs[-1])

            def turn_compressed():
                pe.wait_ge(c_scaled, 1)
                for g in range(NSA_G):
                    for t in range(T):
                        op = nc.tensor.transpose(ps[:, 5 + g // 2, S * (g % 2) + P * t:S * (g % 2) + P * t + P],
                                                 cprob[:, t, HPG * g:HPG * g + HPG, :].rearrange("p h n -> p (h n)"), ident[:])
                op.then_inc(c_turned, 1)
                pe.wait_ge(c_prob, 1)

            attention(NSA_JOBS, 0, turn_compressed)

            def turn_inputs():
                pe.wait_ge(p_landed, 16)
                for k in range(2):
                    for t in range(T):
                        o = S * k + t * P
                        op = nc.tensor.transpose(ps[:, 2, o:o + P], prow[:, t, k * P:(k + 1) * P], ident[:])
                op.then_inc(p_turned, 1)

            pe.wait_ge(mix_ready, NSA_G)
            for g in range(NG):
                group(rows, xs, between=None if g else {1: turn_inputs})

            def quarter(norms, between):
                for g in range(NG):
                    if g == 0 and norms is not None:
                        group_turned(columns, norms)
                    else:
                        group(columns, xs)
                for g in range(NG):
                    def ready(s, g=g):
                        if g == 0 and s in (0, 6):
                            pe.wait_ge(hidden_ready, c.next(hidden_ready, 3 if s == 0 else 1))
                    group(rows, hidden, ready=ready, between={1: between} if between and g == 0 else None)

            def ffn(norms, modulated):
                def between():
                    sum_mod(c.at("mods", 0))
                    c.next("mods", KC)
                if modulated:
                    c.n["mods"] = 2 * KC
                quarter(norms, between if modulated else None)
                per = {lower_ready: 64, "groups": 8, hidden_ready: 4}
                if modulated:
                    per["mods"] = KC
                with loop(pe, c, QUARTERS - 1, per):
                    quarter(None, between if modulated else None)

            ffn(1, True)
            pe.wait_ge(p_ready, 1)
            for g in range(NG):
                st["par"] = (st["par"] + 1) % 2
                bank_free(st["par"])
                up, low = step(2, NW)
                for k in range(2):
                    op = rows(pin, st["par"], k, k, up, low, k == 0, k == 1)
                op.then_inc(step_used, 1)
            group_turned(rows, 2)
            for g in range(1, NG):
                group(rows, xs)
            pe.wait_ge(evacuated, c.at("groups"))
            sum_mod(6 * KC, 0)
            pe.wait_ge(mod_stored, 6)

            group_turned(columns, 3)
            group(columns, xs)
            def turn_modulation():
                op = nc.tensor.transpose(ps[0:6 * KC, 6, 0:P], modcol[:].rearrange("p m k -> p (m k)"), ident[:])
                op.then_inc(mod_turned, 1)

            group(rows, xs)
            group(rows, xs, n=320, between={1: turn_modulation})
            pe.wait_ge(evacuated, c.at("groups"))
            pe.wait_ge(lat_scaled, 1)
            for k in range(4):
                for t in range(T):
                    op = nc.tensor.transpose(ps[:, 4 + k // 2, S * (k % 2) + t * P:S * (k % 2) + (t + 1) * P],
                                             tok[:, t, 256 + k * P:256 + (k + 1) * P], ident[:])
                if k % 2:
                    op.then_inc(lat_turned, 1)
            pe.wait_ge(lat_ready, 4)
            for g in range(3):
                st["par"] = (st["par"] + 1) % 2
                bank_free(st["par"])
                for nk in (2, 1):
                    up, low = step(nk, NW)
                    for kk in range(nk):
                        k = kk + 2 * (nk == 1)
                        op = rows(cqs, st["par"], k, kk, up, low, k == 0, k == 2)
                    op.then_inc(step_used, 1)
            for s in range(2):
                pe.wait_ge(evacuated, c.at("groups"))
                if s:
                    pe.wait_ge(v_stored, s)
                c.next("groups")
                up, low = step(1, 1024)
                kv = [x.rearrange("p a (h d) -> p (a h) d", d=NOPE + VD) for x in (up, low)]
                both = ckvs[:, 0].rearrange("p j s -> p (j s)")
                for j in range(4):
                    mm(ps[:, j, :], kv[0][:, j, 0:NOPE], both, start=True, stop=False, skip_group_check=True)
                    mm(ps[:, j, 0:S], kv[1][:, j, 0:NOPE], ckvs[:, 0, 0, :], start=False, stop=True, skip_group_check=True)
                for t in range(T):
                    xu, xl = (ckvs[:, 0, j, t * P:(t + 1) * P] for j in range(2))
                    vu, vl = (x[:, :, NOPE:] for x in kv)
                    out = ps[:, 4 + t, :]
                    mm(out, xu, vu, start=True, stop=False)
                    mm(out, xu, vl, start=False, stop=False)
                    op = mm(out, xl, vu, start=False, stop=True)
                op.then_inc(step_used, 1)
            pe.wait_ge(evacuated, c.at("groups"))
            pe.wait_ge(v_stored, 2)
            pe.wait_ge(roped, 1)
            for hh in range(MLA_HEADS):
                for t in range(T):
                    o = S * (hh % 2) + t * P
                    op = nc.tensor.transpose(ps[:, hh // 2, o:o + P], qb[:, t, hh, 0:NOPE], ident[:])
            op.then_inc(heads_turned, 1)
            for j in range(MLA_HEADS // 2):
                for t in range(T):
                    o = S * (j % 2) + t * P
                    op = nc.tensor.transpose(ps[:, 4 + j // 2, o:o + P],
                                             qrope[:, t, 2 * j:2 * j + 2, :].rearrange("p h d -> p (h d)"), ident[:])
            op.then_inc(heads_turned, 1)
            for j in range(SWA_KV):
                for i in range(2):
                    for t in range(T):
                        o = S * i + t * P
                        op = nc.tensor.transpose(ps[:, 6 + j, o:o + P], kpad[:, t, j, i].rearrange("p a d -> p (a d)"), ident[:])
            op.then_inc(heads_turned, 1)
            pe.wait_ge(heads_copied, 1)
            for i in range(2):
                for t in range(T):
                    o = S * i + t * P
                    op = nc.tensor.transpose(ps[:, 0, o:o + P], krope[:, t, i].rearrange("p a d -> p (a d)"), ident[:])
            op.then_inc(heads_turned, 1)
            pe.wait_ge(heads_copied, 4)
            attention(LATE_JOBS, len(NSA_JOBS))
            pe.wait_ge(mix_ready, NSA_G + len(LATE_JOBS))
            for g in range(NG):
                group(rows, xs)
            ffn(4, False)


_INS = ["x", "p", "norm_mix", "norm_ffn", "norm_ple", "norm_final", "ffn_w1", "ffn_w2", "ple_w_proj", "ple_w_gate",
        "nsa_w_in", "nsa_w_out", "nsa_cmp_pos_k", "nsa_cmp_w1_k", "nsa_cmp_w2_k", "nsa_cmp_pos_v", "nsa_cmp_w1_v",
        "nsa_cmp_w2_v", "c_2", "w_mod_2", "b_mod_2", "attn_norm_g_2", "w_in_2", "swa_sinks_2", "rel_bias_2",
        "mla_q_norm_g_2", "w_uq_2", "mla_kv_norm_g_2", "w_ukv_2", "w_out_2", "mlp_norm_g_2", "w_ff1_2", "w_ff2_2",
        "final_norm_g_2"]


def shape_constants():
    half_ = ROPE // 2
    freq = np.float32(10000.0) ** (-np.arange(half_, dtype=np.float32) / np.float32(half_))
    ang = np.arange(S, dtype=np.float32)[:, None] * freq[None, :].astype(np.float32)
    exact = BUCKETS // 2
    dist = np.arange(P)
    far = exact + (np.log(np.maximum(dist, 1).astype(np.float32) / exact) / np.log(P / exact)
                   * (BUCKETS - exact)).astype(np.int32)
    bucket = np.where(dist < exact, dist, np.minimum(far, BUCKETS - 1))
    onehot = (bucket[None, :] == np.arange(BUCKETS)[:, None]).astype(np.float32)
    return {"cos": np.cos(ang).astype(np.float32), "sin": np.sin(ang).astype(np.float32), "bucket_onehot": onehot}


def kernel(**inputs):
    import numpy as _np
    import concourse.bacc as _bacc
    from concourse import mybir as _mybir
    from concourse.bass_utils import run_bass_kernel_spmd as _run

    nc = _bacc.Bacc("TRN2", target_bir_lowering=False, num_devices=1)
    arrays, args = {}, {}
    for name, a in [(n, inputs[n]) for n in _INS] + list(shape_constants().items()):
        a = _np.ascontiguousarray(a)
        arrays[f"in_{name}_dram"] = a
        args[name] = nc.dram_tensor(f"in_{name}_dram", a.shape, _mybir.dt.from_np(a.dtype), kind="ExternalInput").ap()
    args["out"] = nc.dram_tensor("out_0_dram", (1, S, D), _mybir.dt.float32, kind="ExternalOutput").ap()
    program(nc, args)
    r = _run(nc, [arrays], core_ids=[0])
    return r.results[0]["out_0_dram"]
```

```python
from contextlib import ExitStack, contextmanager

import concourse.bass as bass
from concourse import mybir
import numpy as np

F32 = mybir.dt.float32
F32R = mybir.dt.float32r
BF16 = mybir.dt.bfloat16
ALU = mybir.AluOpType
ACT = mybir.ActivationFunctionType
AX = mybir.AxisListType

P = 128
S = 256
D = 2048
T = S // P
KC = D // P
BANKS = KC // 2
NW = 512
NG = D // NW
D_FF = 4 * D
QUARTERS = D_FF // D
EPS = 1e-6
NEG = -1e30

NSA_HEADS, NSA_G, DH = 16, 4, 128
HPG = NSA_HEADS // NSA_G
CMP_LEN, CMP_STRIDE = 32, 16
N_CMP = (S - CMP_LEN) // CMP_STRIDE + 1
CPAD = 32

SWA_HEADS, SWA_KV, SWA_D, WINDOW, BUCKETS = 16, 2, 64, 128, 32
MLA_HEADS, Q_RANK, KV_RANK, NOPE, ROPE, VD = 8, 384, 128, 128, 64, 128
QK = NOPE + ROPE
GT = 3 * P

SLOTS = 4
RAW = 2048
SPLIT = 1024
MODS = 6 * KC


class Counts:

    def __init__(self):
        self.n, self.reg, self.per = {}, None, {}

    def at(self, sem, ahead=0):
        v = self.n.get(sem, 0) + ahead
        return self.reg * self.per[sem] + v if self.reg is not None and self.per.get(sem) else v

    def next(self, sem, k=1):
        self.n[sem] = self.n.get(sem, 0) + k
        return self.at(sem)


@contextmanager
def loop(engine, counts, trips, per):
    before = dict(counts.n)
    with engine.Fori(0, trips) as i:
        counts.reg, counts.per = i, per
        yield i
    counts.reg, counts.per = None, {}
    moved = {s: v - before.get(s, 0) for s, v in counts.n.items() if v != before.get(s, 0)}
    assert moved == per, moved
    for s, k in per.items():
        counts.n[s] = before.get(s, 0) + k * trips


def program(nc, a):
    with ExitStack() as ctx:
        base = (nc.sbuf_base + 63) // 64 * 64
        cursor = [base]

        def place(name, shape, dt=F32, at=None):
            size = int(np.prod(shape[1:])) * (2 if dt == BF16 else 4)
            where = cursor[0] if at is None else at
            if at is None:
                cursor[0] += (size + 31) // 32 * 32
            assert where + size <= nc.sbuf_usable_end, (name, where + size)
            return nc.alloc_sbuf_tensor_at(name, shape, dt, offset=where)

        def area(size):
            at = cursor[0]
            cursor[0] += size
            return at

        raw = place("raw", [P, SLOTS, RAW])
        upper = place("upper", [P, SLOTS, SPLIT], F32R)
        lower = place("lower", [P, SLOTS, SPLIT], F32R)
        xs_at = cursor[0]
        xs = place("xs", [P, KC, 2, S], F32R)
        h = place("h", [P, T, D])
        work = area(8192)
        half = place("half", [P, 4, S], at=work)
        summed = place("summed", [P, 4, S], at=work + 4096)
        kcmp = place("kcmp", [P, NSA_G, CPAD], at=work + 4096)
        cstat = place("cstat", [P, 3, T * NSA_HEADS], at=work + 4608)
        hid = place("hid", [P, NSA_G, 7 * CPAD], at=work)
        gsum = place("gsum", [3 * NSA_HEADS, 2, S], at=work + 5120)
        csig = place("csig", [P, NSA_G, N_CMP], at=work + 3584)
        M = area(24576)
        G = area(16384)
        U = area(43008)

        modraw = place("modraw", [P, 2, D], at=M)
        modacc = place("modacc", [P, D], at=M + 16384)
        prob = place("prob", [P, 2, 12 * P], at=M)
        probT = place("probT", [P, 2, 12 * P], at=M + 12288)

        blk = place("blk", [P, CMP_LEN, NSA_G, N_CMP], at=G)
        vcmp = place("vcmp", [P, NSA_HEADS, DH], at=G)
        cprob = place("cprob", [P, T, NSA_HEADS, CPAD], at=G + 8192)
        cprobT = place("cprobT", [P, NSA_G, S], at=G + 12288)

        pin = place("pin", [P, 2, 2, S], F32R, at=G)

        hidden = place("hidden", [P, KC, 2, S], F32R, at=U)
        heads = place("heads", [P, 32, S], at=U)
        vtok = place("vtok", [P, 2, T, NW], at=U + 32768)
        xn = place("xn", [P, T, D], at=U)
        vrow = place("vrow", [P, 3, P], at=U + 32768)
        gainrow = place("gainrow", [P, D], at=U + 16384)
        embed = place("embed", [P, T, D], at=U + 24576)
        prow = place("prow", [P, T, 2 * P], at=U + 40960)

        qa = place("qa", [P, 8, S], at=U)
        ka = place("ka", [P, SWA_KV, 2, S], at=U + 8192)
        qn = place("qn", [P, MLA_HEADS, S], at=U + 12288)
        qr = place("qr", [P, MLA_HEADS // 2, S], at=U + 20480)
        kr = place("kr", [P, 2, S], at=U + 24576)
        kn = place("kn", [P, MLA_HEADS, S], at=U + 26624)
        vb = place("vb", [P, T, MLA_HEADS, VD], at=U + 34816)
        tok = place("tok", [P, T, 832], at=G)
        cqs = place("cqs", [P, 3, 2, S], F32R, at=G + 6656)
        ckvs = place("ckvs", [P, 1, 2, S], F32R, at=G + 12800)
        qb = place("qb", [P, T, MLA_HEADS, QK], at=M)
        qrope = place("qrope", [P, T, MLA_HEADS, ROPE], at=M + 12288)
        rope_t = place("rope_t", [P, 2, MLA_HEADS, ROPE // 2], at=M + 16384)
        krope = place("krope", [P, T, 2, 2, ROPE], at=M + 18432)
        kpad = place("kpad", [P, T, SWA_KV, 2, 2, SWA_D], at=M + 20480)
        gain1 = place("gain1", [P, D], at=G)
        gain2 = place("gain2", [P, D], at=G + 8192)
        toes = place("toes", [P, SWA_HEADS // 4, 4, S], at=xs_at + KC // 2 * 2 * S * 4)

        ident = place("ident", [P, P])
        flip = place("flip", [P, P])
        ident_b = place("ident_b", [P, P], BF16)
        causal_b = place("causal_b", [P, P], BF16)
        vcol = place("vcol", [P, 2 * P + CMP_LEN])
        modcol = place("modcol", [P, 6, KC])
        modsum = place("modsum", [P, 2, KC // 2])
        silu_c = place("silu_c", [P, KC])
        gates = place("gates", [P, T, 3 * NSA_HEADS])
        cmask = place("cmask", [P, 2, T, N_CMP])
        stat = place("stat", [P, 5, 2, 8])
        sumsq = place("sumsq", [P, T, 4])
        norm = place("norm", [P, 3, 4])
        affine = place("affine", [P, KC])
        angle = place("angle", [P, 2, T, ROPE // 2])
        sinks = place("sinks", [P, SWA_HEADS])
        eps = place("eps", [P, 1])
        COL = dict(mix=0, ffn=16, ple=32, attn=48, mlp=64, c=80, q=96, kv=99, b=P, k=P + 96, v=2 * P)
        onehot = place("onehot", [BUCKETS, P], at=U + 40960)
        relb = place("relb", [BUCKETS, SWA_HEADS], at=U + 41472)
        table = place("table", [SWA_HEADS, GT], at=G + 12288)
        tmp = place("tmp", [P, 2, S], at=work)

        ps = ctx.enter_context(nc.psum_tensor("ps", [P, 8, 512], F32))
        modrow = place("modrow", [6 * KC, P], at=work + 4096)
        rows_scratch = nc.dram_tensor("modulation_rows", [6 * KC, P], F32).ap()
        scratch = nc.dram_tensor("bias_by_distance", [SWA_HEADS, GT], F32).ap()

        def sem(name):
            return ctx.enter_context(nc.semaphore(name))

        landed = [sem(f"landed{i}") for i in range(SLOTS)]
        upper_ready, lower_ready, step_used = sem("upper_ready"), sem("lower_ready"), sem("step_used")
        direct_used = sem("direct_used")
        half_copied, evacuated = sem("half_copied"), sem("evacuated")
        squared, hidden_upper, hidden_ready = sem("squared"), sem("hidden_upper"), sem("hidden_ready")
        mod_landed = [sem(f"mod_landed{i}") for i in range(2)]
        mod_added, mod_summed, mod_stored = sem("mod_added"), sem("mod_summed"), sem("mod_stored")
        x_landed = [sem(f"x_landed{i}") for i in range(T)]
        rows_landed, aux_landed, consts = sem("rows_landed"), sem("aux_landed"), sem("consts")
        rows_turned, cols_ready, c_sigmoid = sem("rows_turned"), sem("cols_ready"), sem("c_sigmoid")
        bias_placed, bias_sum, bias_table, bias_stored = sem("bias_placed"), sem("bias_sum"), sem("bias_table"), sem("bias_stored")
        h_ready, squares, squares_v, mean_ready = sem("h_ready"), sem("squares"), sem("squares_v"), sem("mean_ready")
        rms_ready, rstd_ready = sem("rms_ready"), sem("rstd_ready")
        scaled_a, scaled_v, turned, x_upper, x_ready = sem("scaled_a"), sem("scaled_v"), sem("turned"), sem("x_upper"), sem("x_ready")
        mod_cols = sem("mod_cols")
        gain_landed, p_landed, p_turned, p_upper, p_ready = sem("gain_landed"), sem("p_landed"), sem("p_turned"), sem("p_upper"), sem("p_ready")
        pv_done = sem("pv_done")
        ple_gate = sem("ple_gate")
        mod_turned, mod_rows, mod_rows_stored, gain_row = sem("mod_turned"), sem("mod_rows"), sem("mod_rows_stored"), sem("gain_row")
        blk_ready, cmp_sigmoid, hid_ready = sem("blk_ready"), sem("cmp_sigmoid"), sem("hid_ready")
        cmp_stored = sem("cmp_stored")
        gate_half, gate_sum, gate_turned, gate_ready = sem("gate_half"), sem("gate_sum"), sem("gate_turned"), sem("gate_ready")
        c_scores, c_shifted, c_exp, c_scaled, c_turned, c_prob = sem("c_scores"), sem("c_shifted"), sem("c_exp"), sem("c_scaled"), sem("c_turned"), sem("c_prob")
        scores, bias_ready, exps, prob_ready = sem("scores"), sem("bias_ready"), sem("exps"), sem("prob_ready")
        prob_turned, probT_ready, mixed, mix_upper, mix_ready = sem("prob_turned"), sem("probT_ready"), sem("mixed"), sem("mix_upper"), sem("mix_ready")
        toe_landed = [sem(f"toe_landed{i}") for i in range(4)]
        lat_squares, lat_rms, lat_scaled, lat_turned, lat_upper, lat_ready = sem("lat_squares"), sem("lat_rms"), sem("lat_scaled"), sem("lat_turned"), sem("lat_upper"), sem("lat_ready")
        v_stored = sem("v_stored")
        pads_ready, krope_ready, kv_done, queries_copied = sem("pads_ready"), sem("krope_ready"), sem("kv_done"), sem("queries_copied")
        roped, heads_turned, heads_copied = sem("roped"), sem("heads_turned"), sem("heads_copied")
        act_step, dve_step, pool_step = sem("act_step"), sem("dve_step"), sem("pool_step")
        stored = sem("stored")

        def chunks(w):
            return w.rearrange("(k p) n -> p k n", p=P)

        w_in, w_out = chunks(a["nsa_w_in"][0]), chunks(a["nsa_w_out"][0])
        ffn1, ffn2 = chunks(a["ffn_w1"][0]), chunks(a["ffn_w2"][0])
        w_gate, w_embed = chunks(a["ple_w_gate"][0]), chunks(a["ple_w_proj"][0])
        w_mod = a["w_mod_2"][0]
        w_in2, w_out2 = chunks(a["w_in_2"][0]), chunks(a["w_out_2"][0])
        ffn1b, ffn2b = chunks(a["w_ff1_2"][0]), chunks(a["w_ff2_2"][0])
        w_uq, w_ukv = chunks(a["w_uq_2"][0]), chunks(a["w_ukv_2"][0])
        NSA_Q = NSA_HEADS * DH
        KV_COLS = {"vs": NSA_Q + 3 * NW, "kw": NSA_Q + 4 * NW, "vw": NSA_Q + 5 * NW, "gates": NSA_Q + 6 * NW}
        STEPS_FFN = 8 * (10 + NG + 2 * NG * QUARTERS) + 1
        STEPS_FFN2 = STEPS_FFN + 4 + 8 * NG + 8 * 4 + 3 * 2 + 2 + 8 * NG + 8 * 2 * NG * QUARTERS
        GROUPS_UKV = 11 + NG + 2 * NG * QUARTERS + NG + NG + 4 + 3 + 2

        PIECES = [(0, 2 * NW), (2 * NW, NW), (3 * NW, NW)]
        HALVES = [(0, 2 * NW), (2 * NW, 2 * NW)]

        def slot_view(t, slot, k, n):
            return t[:, slot, 0:k * n].rearrange("p (k n) -> p k n", n=n)

        def std_steps(n):
            return [(0, 2, 0, n), (2, 2, 0, n)]

        def gate_view(t, g, branch):
            return gates[:, t, :].rearrange("p (h b) -> p h b", b=3)[:, HPG * g:HPG * g + HPG, branch]

        NSA_JOBS = [("nsa", g, b) for g in range(NSA_G) for b in range(2)]
        LATE_JOBS = [("swa", i, 0) for i in range(4)] + [("mla", i, 0) for i in range(2)]

        def banks_of(kind):
            return (3, 0) if kind == "nsa" else (0, 3)

        block = ctx.enter_context(nc.Block())

        @block.sync
        def _(sp):
            c = Counts()
            st = dict(unit=0, mod=0)
            release = []

            def free_slot():
                if len(release) >= SLOTS:
                    s, k = release.pop(0)
                    sp.wait_ge(s, c.next(s, k))

            def unit(src, K, N, frees=(lower_ready, 2)):
                free_slot()
                release.append(frees)
                slot = st["unit"] % SLOTS
                st["unit"] += 1
                dst = raw[:, slot, 0:K * N].rearrange("p (k n) -> p k n", n=N)
                sp.dma_start(dst, src).then_inc(landed[slot], 16)

            def mod_unit(row, col):
                slot = st["mod"] % 2
                if st["mod"] >= 2:
                    sp.wait_ge(mod_added, c.next(mod_added))
                st["mod"] += 1
                sp.dma_start(modraw[:, slot, :], w_mod[row, col]).then_inc(mod_landed[slot], 16)

            def section_rows(k, m):
                return [(bass.ds((k + j) * P, P), slice(m * D, (m + 1) * D)) for j in range(2)]

            def mods_of(u):
                return (slice(u % KC * P, (u % KC + 1) * P), slice(u // KC * D, (u // KC + 1) * D))

            def group(w, col, row=0, n=NW, mods=None):
                for j in range(4):
                    k = row + 4 * j
                    rows = bass.ds(k, 4) if not isinstance(row, int) else slice(k, k + 4)
                    cols = bass.ds(col, n) if not isinstance(col, int) else slice(col, col + n)
                    unit(w[:, rows, cols], 4, n)
                    if mods and j >= 2:
                        mod_unit(*mods[j - 2])

            for t in range(T):
                sp.dma_start(h[:, t, :], a["x"][0, t * P:(t + 1) * P, :]).then_inc(x_landed[t], 16)
            vecs = [(a["norm_mix"][0], 0, 0), (a["norm_ffn"][0], 16, 0), (a["norm_ple"][0], 32, 0),
                    (a["attn_norm_g_2"][0], 48, 0), (a["mlp_norm_g_2"][0], 64, 0), (a["c_2"][0], 80, 0),
                    (a["mla_q_norm_g_2"][0], 96, 0), (a["mla_kv_norm_g_2"][0], 99, 0),
                    (a["b_mod_2"][0], 0, 1)]
            for v, r, j in vecs:
                n = v.shape[0] // P
                sp.dma_start(vrow[r:r + n, j, :], v.rearrange("(r c) -> r c", c=P)).then_inc(rows_landed, 16)
            sp.dma_start(vrow[96:128, 1, :], a["nsa_cmp_pos_k"][0]).then_inc(rows_landed, 16)
            sp.dma_start(vrow[0:32, 2, :], a["nsa_cmp_pos_v"][0]).then_inc(rows_landed, 16)

            group(w_in, 0, mods=[mods_of(0), mods_of(1)])
            group(w_in, NW, mods=section_rows(2, 0))
            with loop(sp, c, 5, {lower_ready: 8, mod_added: 2}) as i:
                group(w_in, i * NW + 2 * NW, mods=section_rows(i * 2 + 4, 0))
            group(w_in, KV_COLS["kw"], mods=[mods_of(14), mods_of(15)])
            for name, values in (("k", "vs"), ("v", "vw")):
                group(w_in, KV_COLS[values])
                w1 = a[f"nsa_cmp_w1_{name}"][0].rearrange("(l p) n -> p l n", p=P)
                for u in range(2):
                    unit(w1[:, 16 * u:16 * u + 16, :], 16, P, (direct_used, 1))
                unit(a[f"nsa_cmp_w2_{name}"][0].rearrange("p (k n) -> p k n", k=1), 1, P, (direct_used, 1))
            unit(w_in[:, :, KV_COLS["gates"]:KV_COLS["gates"] + 48], KC, 48, (lower_ready, 1))
            group(w_out, 0)
            sp.wait_ge(pv_done, len(NSA_JOBS))
            for rows_cols in section_rows(0, 1):
                mod_unit(*rows_cols)
            with loop(sp, c, NG - 1, {lower_ready: 8, mod_added: 2}) as i:
                group(w_out, i * NW + NW, mods=section_rows(i * 2 + 2, 1))

            def quarter(w1, w2, q, mods):
                for g in range(NG):
                    group(w1, q * D + g * NW, mods=mods and mods[2 * g:2 * g + 2])
                for g in range(NG):
                    group(w2, g * NW, row=q * KC, mods=mods and mods[8 + 2 * g:10 + 2 * g])

            def quarter_mods(q):
                rows = [slice((8 + j) % KC * P, ((8 + j) % KC + 1) * P) for j in range(KC)]
                return [(rows[j], bass.ds((q + (1 if j < 8 else 2)) * D, D) if not isinstance(q, int)
                         else slice((q + (1 if j < 8 else 2)) * D, (q + (1 if j < 8 else 2) + 1) * D))
                        for j in range(KC)]

            quarter(ffn1, ffn2, 0, quarter_mods(0))
            with loop(sp, c, QUARTERS - 1, {lower_ready: 64, mod_added: 16}) as i:
                quarter(ffn1, ffn2, i + 1, quarter_mods(i + 1))
            for u in range(2):
                unit(w_embed[:, 0:2, u * 1024:(u + 1) * 1024], 2, 1024)
            with loop(sp, c, NG, {lower_ready: 8, mod_added: 2}) as i:
                group(w_gate, i * NW, mods=section_rows(i * 2 + 8, 5))
            group(w_in2, 2 * NW)
            group(w_in2, 3 * NW, n=320)
            group(w_in2, 0)
            group(w_in2, NW)
            for g in range(3):
                unit(w_uq[:, 0:3, g * NW:(g + 1) * NW], 3, NW)
            unit(w_ukv[:, 0:1, :], 1, D)
            group(w_out2, 0)
            with loop(sp, c, NG - 1, {lower_ready: 8}) as i:
                group(w_out2, i * NW + NW)
            quarter(ffn1b, ffn2b, 0, None)
            with loop(sp, c, QUARTERS - 1, {lower_ready: 64}) as i:
                quarter(ffn1b, ffn2b, i + 1, None)
            for t, (j, (o, n)) in [(t, x) for t in range(T) for x in enumerate(HALVES)]:
                sp.wait_ge(h_ready, 2 * T + 2 * t + j + 1)
                sp.dma_start(a["out"][0, t * P:(t + 1) * P, o:o + n], h[:, t, o:o + n]).then_inc(stored, 16)
            sp.wait_ge(stored, 16 * 2 * T)

        @block.gpsimd
        def _(pool):
            c = Counts()

            def link(op):
                op.then_inc(pool_step, 1)
                pool.wait_ge(pool_step, c.next(pool_step))

            nc.gpsimd.memset(ident[:], 0.0)
            nc.gpsimd.memset(flip[:], 0.0)
            nc.gpsimd.memset(causal_b[:], 0.0)
            nc.gpsimd.memset(cmask[:, 0], 0.0)
            nc.gpsimd.memset(cmask[:, 1], 1.0)
            link(nc.gpsimd.memset(eps[:], EPS))
            nc.gpsimd.affine_select(out=flip[:], in_=flip[:], compare_op=ALU.not_equal, fill=1.0,
                                    base=-(P - 1), pattern=[[1, P]], channel_multiplier=1)
            link(nc.gpsimd.affine_select(out=ident[:], in_=ident[:], compare_op=ALU.not_equal, fill=1.0,
                                         base=0, pattern=[[-1, P]], channel_multiplier=1))
            nc.gpsimd.affine_select(out=causal_b[:], in_=causal_b[:], compare_op=ALU.is_ge, fill=NEG,
                                    base=0, pattern=[[-1, P]], channel_multiplier=1)
            for m, fill in ((0, NEG), (1, 0.0)):
                nc.gpsimd.affine_select(out=cmask[:, m], in_=cmask[:, m], compare_op=ALU.is_ge, fill=fill,
                                        base=-(CMP_LEN - 1), pattern=[[P, T], [-CMP_STRIDE, N_CMP]],
                                        channel_multiplier=1)
            nc.gpsimd.tensor_copy(ident_b[:], ident[:]).then_inc(consts, 1)
            pool.dma_start(angle[:, 0], a["cos"].rearrange("(t p) f -> p t f", p=P)).then_inc(aux_landed, 16)
            pool.dma_start(angle[:, 1], a["sin"].rearrange("(t p) f -> p t f", p=P)).then_inc(aux_landed, 16)
            pool.dma_start(sinks[:], a["swa_sinks_2"][0].partition_broadcast(P)).then_inc(aux_landed, 16)
            pool.dma_start(onehot[:], a["bucket_onehot"]).then_inc(aux_landed, 16)
            pool.dma_start(relb[:], a["rel_bias_2"]).then_inc(aux_landed, 16)
            nc.gpsimd.memset(table[:], NEG).then_inc(bias_placed, 1)
            pool.wait_ge(bias_table, 1)
            pool.dma_start(scratch, table[:]).then_inc(bias_stored, 16)
            pool.wait_ge(bias_stored, 16)
            pool.dma_start(prow[:], a["p"][0, 0].rearrange("(t p) f -> p t f", p=P)).then_inc(p_landed, 16)
            pool.wait_ge(step_used, STEPS_FFN)
            pool.dma_start(gainrow[:], a["norm_final"].partition_broadcast(P)).then_inc(gain_landed, 16)
            pool.wait_ge(mod_stored, 6)
            nc.gpsimd.memset(krope[:], 0.0)
            link(nc.gpsimd.memset(kpad[:], 0.0))
            pool.wait_ge(evacuated, GROUPS_UKV - 8)
            for t in range(T):
                for i in range(2):
                    op = nc.gpsimd.tensor_copy(kpad[:, t, :, i, i, :], tok[:, t, 0:P].rearrange("p (v d) -> p v d", v=SWA_KV))
            op.then_inc(pads_ready, 1)
            pool.wait_ge(mod_rows, 1)
            pool.dma_start(rows_scratch, modrow[:]).then_inc(mod_rows_stored, 16)
            pool.wait_ge(mod_rows_stored, 16)
            pool.wait_ge(evacuated, GROUPS_UKV - 5)
            for i in range(4):
                src = bass.AP(scratch.tensor, 4 * i * GT, [[1, P], [GT, 4], [1, 2 * P]])
                pool.dma_start(toes[:, i], src).then_inc(toe_landed[i], 16)
            pool.wait_ge(pv_done, len(NSA_JOBS) + 4)
            for m, gain in ((2, gain1), (5, gain2)):
                src = bass.AP(rows_scratch.tensor, m * D, [[0, P], [1, D]])
                pool.dma_start(gain[:], src).then_inc(gain_row, 16)
            pool.wait_ge(step_used, STEPS_FFN2)
            pool.dma_start(gainrow[:], a["final_norm_g_2"].partition_broadcast(P)).then_inc(gain_landed, 16)

        @block.scalar
        def _(act):
            c = Counts()
            st = dict(unit=0, step=0)

            def link(op):
                op.then_inc(act_step, 1)
                act.wait_ge(act_step, c.next(act_step))

            def split(K, N, spec, first):
                k0, nk, n0, nn = spec
                if first:
                    slot = st["unit"] % SLOTS
                    act.wait_ge(landed[slot], c.next(landed[slot], 16))
                    st["unit"] += 1
                slot = (st["unit"] - 1) % SLOTS
                if st["step"] >= SLOTS:
                    act.wait_ge(step_used, c.at("steps", 1 - SLOTS))
                src = slot_view(raw, slot, K, N)[:, k0:k0 + nk, n0:n0 + nn]
                dst = slot_view(upper, st["step"] % SLOTS, nk, nn)
                nc.scalar.activation(dst, src, ACT.Copy).then_inc(upper_ready, 1)
                st["step"] += 1
                c.next("steps")

            def split_ahead(steps=SLOTS):
                for s in range(steps):
                    split(4, NW, std_steps(NW)[s % 2], s % 2 == 0)

            def group(before=(), n=NW, start=0):
                for s in range(start, 8):
                    split(4, n, std_steps(n)[s % 2], s % 2 == 0)
                    if 2 <= s < 2 + len(before):
                        before[s - 2](s + 1)

            def group_summed(ahead):
                act.wait_ge(step_used, c.at("steps", -ahead))

            def none(ahead):
                c.next("groups")

            def copy_half(parity):
                def f(ahead):
                    group_summed(ahead)
                    act.wait_ge(evacuated, c.at("groups"))
                    nc.scalar.activation(half[:], ps[:, 4 * parity:4 * parity + 4, S:2 * S],
                                         ACT.Copy).then_inc(half_copied, 1)
                    c.next("groups")
                return f

            def first_half(ahead):
                group_summed(ahead)
                nc.scalar.activation(half[:], ps[:, 0:4, S:2 * S], ACT.Copy).then_inc(half_copied, 1)
                c.next("groups")

            def upper_hidden(g):
                def f(ahead):
                    act.wait_ge(squared, c.next(squared))
                    nc.scalar.activation(hidden[:, 4 * g:4 * g + 4, 0, :], summed[:],
                                         ACT.Copy).then_inc(hidden_upper, 1)
                return f

            def square(t, i, o, n, sem_):
                out = summed[:].rearrange("p a s -> p (a s)")[:, 0:n]
                nc.scalar.activation(out, h[:, t, o:o + n], ACT.Square,
                                     accum_out=sumsq[:, t, i:i + 1]).then_inc(sem_, 1)
                act.wait_ge(sem_, c.next(sem_))

            def squares_ahead(load_roots=True):
                if load_roots:
                    link(nc.scalar.activation(norm[:, 1, 2:3], eps[:, 0:1], ACT.Sqrt))
                if st_groups():
                    act.wait_ge(evacuated, c.at("groups"))
                for i, (o, n) in enumerate(PIECES[:-1]):
                    square(0, i, o, n, act_step)

            def root():
                act.wait_ge(mean_ready, c.next(mean_ready))
                nc.scalar.activation(norm[:, 1, 0:2], norm[:, 0, 0:2], ACT.Sqrt, bias=eps[:, 0:1],
                                     scale=1.0 / D).then_inc(rms_ready, 1)
                c.next(rstd_ready)

            def root_mean(first):
                first()
                square(0, len(PIECES) - 1, *PIECES[-1], squares)
                root()

            def root_mean_rescaled():
                for t in range(T):
                    for i, (o, n) in enumerate(HALVES):
                        act.wait_ge(h_ready, 2 * t + i + 1)
                        square(t, i, o, n, act_step if (t, i) != (T - 1, 1) else squares)
                root()

            def to_features(gain, shift=None, ahead=SLOTS):
                act.wait_ge(rstd_ready, c.at(rstd_ready))
                b0 = 4 * ((st_groups() + 1) % 2)

                def scale(q):
                    nc.scalar.activation(xn[:, 0, q * NW:(q + 1) * NW], h[:, 0, q * NW:(q + 1) * NW], ACT.Copy,
                                         scale=norm[:, 2, 0:1]).then_inc(scaled_a, 1)

                scale(0)
                scale(1)
                for b in range(BANKS):
                    if b in (1, 3):
                        scale((b + 3) // 2)
                    if b == 0 and shift is not None:
                        act.wait_ge(mod_cols, c.next(mod_cols))
                    act.wait_ge(turned, c.next(turned))
                    for k in (2 * b, 2 * b + 1):
                        src = ps[:, b0 + b % 4, S * (k % 2):S * (k % 2) + S]
                        if shift is None:
                            op = nc.scalar.activation(xs[:, k, 0, :], src, ACT.Copy, scale=gain[:, k:k + 1])
                        else:
                            op = nc.scalar.activation(xs[:, k, 0, :], src, ACT.Identity, scale=gain[:, k:k + 1],
                                                      bias=shift[:, k:k + 1])
                    op.then_inc(x_upper, 1)
                    if b >= ahead:
                        split(4, NW, std_steps(NW)[b % 2], b % 2 == 0)

            def st_groups():
                return c.n.get("groups", 0)

            def all_evacuated():
                act.wait_ge(evacuated, c.at("groups"))

            act.wait_ge(consts, 1)
            act.wait_ge(x_landed[0], 16)
            squares_ahead()
            root_mean(lambda: None)
            split_ahead(2)
            act.wait_ge(cols_ready, 1)
            to_features(vcol[:, COL["mix"]:COL["mix"] + KC], ahead=2)
            nc.scalar.activation(silu_c[:], vcol[:, COL["c"]:COL["c"] + KC], ACT.Sigmoid).then_inc(c_sigmoid, 1)
            group([first_half])
            with loop(act, c, 3, {"steps": 16, "groups": 2, **{l: 32 for l in landed}}):
                group([copy_half(1)])
                group([copy_half(0)])
            def direct_units():
                for _ in range(3):
                    c.next(landed[st["unit"] % SLOTS], 16)
                    st["unit"] += 1

            def hidden_sigmoid(i):
                def f(ahead):
                    act.wait_ge(direct_used, 3 * i + 2)
                    nc.scalar.activation(csig[:], ps[:, 2 + i, 0:NSA_G * N_CMP], ACT.Sigmoid).then_inc(cmp_sigmoid, 1)
                return f

            group([copy_half(1)])
            direct_units()
            group([hidden_sigmoid(0)])
            direct_units()
            split(KC, 48, (0, KC, 0, 48), True)
            for _ in range(3):
                none(0)
            hidden_sigmoid(1)(0)
            group_summed(0)
            nc.scalar.activation(gsum[:, 0, :], ps[0:48, 0, S:2 * S], ACT.Copy).then_inc(gate_half, 1)
            act.wait_ge(gate_turned, 1)
            nc.scalar.activation(gates[:], ps[:, 1, 0:2 * P].rearrange("p (t n) -> p t n", t=T)[:, :, 0:48],
                                 ACT.Sigmoid).then_inc(gate_ready, 1)
            act.wait_ge(c_shifted, 1)
            cp = cprob[:].rearrange("p t h n -> p (t h) n")[:, :, 0:N_CMP]
            nc.scalar.activation(cp, cp, ACT.Exp).then_inc(c_exp, 1)

            def compressed_turned():
                act.wait_ge(c_turned, 1)
                nc.scalar.activation(cprobT[:].rearrange("p g s -> p (g s)"), ps[:, 1:3, :].rearrange("p b n -> p (b n)"),
                                     ACT.Copy).then_inc(c_prob, 1)

            def job_exps(n, kind, scale):
                act.wait_ge(bias_ready, c.next(bias_ready))
                if kind == "swa":
                    nc.scalar.activation(stat[:, 4, n % 2, :], stat[:, 4, n % 2, :], ACT.Exp)
                for t in range(T):
                    for j in range(HPG):
                        w = P * (t + 1)
                        sb = banks_of(kind)[0]
                        src = ps[:, sb, P * j:P * j + P] if t == 0 else ps[:, sb + 1 + j // 2, S * (j % 2):S * (j % 2) + S]
                        o = P * HPG * t + w * j
                        col = HPG * t + j
                        op = nc.scalar.activation(prob[:, n % 2, o:o + w], src, ACT.Exp,
                                                  bias=stat[:, 1, n % 2, col:col + 1], scale=scale,
                                                  accum_out=stat[:, 2, n % 2, col:col + 1])
                    op.then_inc(exps, 1)

            def job_turned(n, kind):
                act.wait_ge(prob_turned, c.next(prob_turned))
                tb = banks_of(kind)[1]
                if n >= 2:
                    act.wait_ge(pv_done, c.next(pv_done))
                nc.scalar.activation(probT[:, n % 2, :], ps[:, tb:tb + 3, :].rearrange("p b n -> p (b n)"),
                                     ACT.Copy).then_inc(probT_ready, 1)

            def mix_parts(jobs, n, base):
                kind, i, b = jobs[n]
                if kind == "nsa":
                    return (4 * i, 4, ps[:, 6:8, :].rearrange("p b (c s) -> p (b c) s", s=S)) if b else None
                if kind == "swa":
                    return 2 * i, 2, ps[:, 6 + i % 2, :].rearrange("p (c s) -> p c s", s=S)
                return 8 + 4 * i, 4, ps[:, 6:8, :].rearrange("p b (c s) -> p (b c) s", s=S)

            def attention(jobs, base, scale_of, after_first=None):
                for n in range(len(jobs) + 2):
                    if n < len(jobs):
                        job_exps(base + n, jobs[n][0], scale_of(jobs[n][0]))
                    if n == 0 and after_first:
                        after_first()
                    if 1 <= n <= len(jobs):
                        job_turned(base + n - 1, jobs[n - 1][0])
                    if 1 <= n <= SLOTS:
                        split(4, NW, std_steps(NW)[(n - 1) % 2], n % 2 == 1)
                    if n >= 2:
                        part = mix_parts(jobs, n - 2, base)
                        if part:
                            k, m, src = part
                            act.wait_ge(pv_done, base + n - 1)
                            nc.scalar.activation(xs[:, k:k + m, 0, :], src, ACT.Copy).then_inc(mix_upper, 1)

            SCALE = {"nsa": DH ** -0.5, "swa": 1.0, "mla": QK ** -0.5}
            attention(NSA_JOBS, 0, SCALE.get, compressed_turned)

            def nothing(ahead):
                pass

            def pin_upper(ahead):
                act.wait_ge(p_turned, 1)
                nc.scalar.activation(pin[:, :, 0, :], ps[:, 2, :].rearrange("p (k s) -> p k s", s=S),
                                     ACT.Copy).then_inc(p_upper, 1)

            group([nothing, nothing, pin_upper], start=SLOTS)
            for g in range(1, NG):
                group([none])

            def norm_behind(pending=none, load_roots=True):
                squares_ahead(load_roots)
                split_ahead()
                pending(SLOTS)
                root_mean(all_evacuated)

            norm_behind()

            def quarter(pending, p0, start):
                for g in range(NG):
                    if g or not start:
                        group(pending)
                    pending = [copy_half((p0 + g) % 2), upper_hidden(g)]
                for g in range(NG):
                    group(pending)
                    pending = [none]

            def ffn():
                p0 = st_groups() % 2
                quarter([], p0, 8)
                with loop(act, c, QUARTERS - 1, {"steps": 64, "groups": 8, squared: 4,
                                                 **{l: 128 for l in landed}}):
                    quarter([none], p0, 0)

            to_features(vcol[:, COL["ffn"]:COL["ffn"] + KC])
            ffn()

            squares_ahead()
            for u in range(2):
                for s in range(2):
                    split(2, 1024, (0, 2, 512 * s, 512), s == 0)
            none(0)
            root_mean(all_evacuated)
            for g in range(NG):
                none(0)
            to_features(vcol[:, COL["ple"]:COL["ple"] + KC], ahead=0)

            def gate_of(g):
                def f(ahead):
                    group_summed(ahead)
                    act.wait_ge(evacuated, c.at("groups"))
                    b = 4 * (c.n["groups"] % 2)
                    nc.scalar.activation(half[:].rearrange("p (t a) s -> p t (a s)", t=T), ps[:, b:b + 2, :],
                                         ACT.Sigmoid).then_inc(ple_gate, 1)
                    c.next("groups")
                return f

            for g in range(1, NG):
                group([gate_of(g - 1)])
            norm_behind(gate_of(NG - 1), load_roots=False)

            root_mean_rescaled()
            p0 = st_groups() % 2
            to_features(affine[:], modcol[:, 0, :])
            def latent_roots(ahead):
                act.wait_ge(lat_squares, 1)
                nc.scalar.activation(norm[:, 1, 0:2], norm[:, 0, 0:2], ACT.Sqrt, bias=eps[:, 0:1], scale=1.0 / Q_RANK)
                nc.scalar.activation(norm[:, 1, 2:4], norm[:, 0, 2:4], ACT.Sqrt, bias=eps[:, 0:1],
                                     scale=1.0 / KV_RANK).then_inc(lat_rms, 1)

            def latent_upper(ahead):
                for k in range(4):
                    act.wait_ge(lat_turned, k // 2 + 1)
                    dst = cqs[:, k, 0, :] if k < 3 else ckvs[:, 0, 0, :]
                    op = nc.scalar.activation(dst, ps[:, 2 + k // 2, S * (k % 2):S * (k % 2) + S], ACT.Copy,
                                              scale=vcol[:, COL["q"] + k:COL["q"] + k + 1])
                    if k % 2:
                        op.then_inc(lat_upper, 1)

            def heads_out(turn, dst, b, n):
                act.wait_ge(heads_turned, turn)
                nc.scalar.activation(dst, ps[:, b:b + n, :].rearrange("p b n -> p (b n)"), ACT.Copy).then_inc(heads_copied, 1)

            def split_uq():
                split(3, NW, (0, 2, 0, NW), True)
                split(3, NW, (2, 1, 0, NW), False)

            group([none], n=320)
            group([none, nothing, latent_roots, nothing, nothing, latent_upper])
            group([copy_half(p0)])
            split_uq()
            copy_half(1 - p0)(2)
            split_uq()
            heads_out(1, ka[:].rearrange("p v a s -> p (v a s)"), 6, 2)
            split_uq()
            split(1, D, (0, 1, 0, 1024), True)
            split(1, D, (0, 1, 1024, 1024), False)
            heads_out(2, kr[:].rearrange("p a s -> p (a s)"), 2, 1)
            for g in range(3):
                none(0)
            for s in range(2):
                if s == 0:
                    act.wait_ge(kv_done, 1)
                else:
                    group_summed(0)
                act.wait_ge(evacuated, c.at("groups"))
                nc.scalar.activation(half[:], ps[:, 0:4, S:2 * S], ACT.Copy).then_inc(half_copied, 1)
                none(0)
                if s == 0:
                    for v in range(2):
                        if v == 0:
                            group_summed(1)
                        else:
                            act.wait_ge(kv_done, 2)
                        nc.scalar.activation(vb[:, :, 4 * v:4 * v + 4, :],
                                             ps[:, 4 + 2 * v:6 + 2 * v, :].rearrange("p t (h d) -> p t h d", d=VD),
                                             ACT.Copy).then_inc(v_stored, 1)
            heads_out(3, qn[:, 0:4, :].rearrange("p h s -> p (h s)"), 6, 2)
            heads_out(5, qr[:].rearrange("p h s -> p (h s)"), 0, 2)
            attention(LATE_JOBS, len(NSA_JOBS), SCALE.get)
            group(start=SLOTS)
            for g in range(1, NG):
                group([none])
            norm_behind()
            to_features(affine[:], modcol[:, 3, :])
            ffn()
            squares_ahead()
            none(0)
            root_mean(all_evacuated)

        @block.vector
        def _(dve):
            c = Counts()
            st = dict(unit=0, step=0, mod=0)

            def link(op):
                op.then_inc(dve_step, 1)
                dve.wait_ge(dve_step, c.next(dve_step))

            def split(K, N, spec, first):
                k0, nk, n0, nn = spec
                st["unit"] += first
                slot = (st["unit"] - 1) % SLOTS
                dve.wait_ge(upper_ready, c.next(upper_ready))
                src = slot_view(raw, slot, K, N)[:, k0:k0 + nk, n0:n0 + nn]
                up, low = (slot_view(x, st["step"] % SLOTS, nk, nn) for x in (upper, lower))
                nc.vector.tensor_tensor(low, src, up, ALU.subtract).then_inc(lower_ready, 1)
                st["step"] += 1
                c.next("steps")

            def add_mod(k):
                slot = st["mod"] % 2
                dve.wait_ge(mod_landed[slot], c.next(mod_landed[slot], 16))
                if st["mod"]:
                    dve.wait_ge(mod_added, c.at(mod_added))
                w, s = modraw[:, slot, :], silu_c[:, bass.ds(k, 1)]
                if isinstance(k, int) and k == 0:
                    op = nc.vector.tensor_scalar(modacc[:], w, s, None, ALU.mult)
                else:
                    op = nc.vector.scalar_tensor_tensor(modacc[:], w, s, modacc[:], ALU.mult, ALU.add)
                op.then_inc(mod_added, 1)
                c.next(mod_added)
                st["mod"] += 1

            def store_mod(m):
                dve.wait_ge(mod_summed, c.next(mod_summed))
                if isinstance(m, int):
                    dst, b = modcol[:, m, :], vcol[:, COL["b"] + KC * m:COL["b"] + KC * (m + 1)]
                else:
                    dst, b = modcol[:, bass.ds(m, 1), :].rearrange("p a k -> p (a k)"), vcol[:, bass.ds(m * KC + COL["b"], KC)]
                for i, bank in enumerate((2, 6)):
                    op = nc.vector.tensor_reduce(modsum[:, i], ps[:, bank:bank + 2, :].rearrange("p b (k n) -> p (b k) n", n=P),
                                                 AX.X, ALU.add)
                link(op)
                nc.vector.tensor_tensor(dst, modsum[:].rearrange("p a k -> p (a k)"), b, ALU.add).then_inc(mod_stored, 1)

            def split_ahead(first, last):
                for s in range(first, last):
                    split(4, NW, std_steps(NW)[s % 2], s % 2 == 0)

            def group(before=(), n=NW, mods=None, store=None, at=(3, 6), start=0):
                for s in range(start, 8):
                    split(4, n, std_steps(n)[s % 2], s % 2 == 0)
                    if 2 <= s < 2 + len(before):
                        before[s - 2](s + 1)
                    if s == 3 and store is not None:
                        store_mod(store)
                    if mods is not None and s in at:
                        add_mod(mods + (s == at[1]))

            def group_summed(ahead):
                dve.wait_ge(step_used, c.at("steps", -ahead))

            def done(op):
                op.then_inc(evacuated, 1)
                c.next("groups")

            def own_before():
                if c.n.get("groups", 0):
                    dve.wait_ge(evacuated, c.at("groups"))

            def columns_out(parity, dst):
                def f(ahead):
                    dve.wait_ge(half_copied, c.next(half_copied))
                    done(nc.vector.tensor_tensor(dst, ps[:, 4 * parity:4 * parity + 4, 0:S], half[:], ALU.add))
                return f

            def square(parity):
                def f(ahead):
                    dve.wait_ge(half_copied, c.next(half_copied))
                    done(nc.vector.tensor_tensor(summed[:], ps[:, 4 * parity:4 * parity + 4, 0:S], half[:], ALU.add))
                    own_before()
                    nc.vector.scalar_tensor_tensor(summed[:], summed[:], 0.0, summed[:], ALU.max,
                                                   ALU.mult).then_inc(squared, 1)
                return f

            def lower_hidden(g):
                def f(ahead):
                    dve.wait_ge(hidden_upper, c.next(hidden_upper))
                    nc.vector.tensor_tensor(hidden[:, 4 * g:4 * g + 4, 1, :], summed[:],
                                            hidden[:, 4 * g:4 * g + 4, 0, :], ALU.subtract).then_inc(hidden_ready, 1)
                return f

            def rows_of(parity):
                return ps[:, 4 * parity:4 * parity + 2, :]

            def add_rows(parity, g, gain=None):
                def f(ahead):
                    group_summed(ahead)
                    hv = h[:, :, g * NW:(g + 1) * NW]
                    own_before()
                    if gain is None:
                        done(nc.vector.tensor_tensor(hv, rows_of(parity), hv, ALU.add))
                        return
                    gv = gain[:, g * NW:(g + 1) * NW].unsqueeze(1).to_broadcast([P, T, NW])
                    sv = half[:].rearrange("p (t a) s -> p t (a s)", t=T)
                    link(nc.vector.tensor_tensor(sv, rows_of(parity), gv, ALU.mult))
                    done(nc.vector.tensor_tensor(hv, sv, hv, ALU.add))
                return f

            def copy_rows(parity, dst):
                def f(ahead):
                    group_summed(ahead)
                    done(nc.vector.tensor_copy(dst, rows_of(parity)[:, :, 0:dst.shape[-1]]))
                return f

            def square_piece(i, junk, sem_):
                o, n = PIECES[i]
                v = h[:, 1, o:o + n]
                nc.vector.tensor_tensor_reduce(junk[:, 0:n], v, v, 1.0, 0.0, ALU.mult, ALU.add,
                                               sumsq[:, 1, i:i + 1]).then_inc(sem_, 1)
                dve.wait_ge(sem_, c.next(sem_))

            half_flat = half[:].rearrange("p a s -> p (a s)")

            def squares_ahead(junk=half_flat):
                own_before()
                for i in range(len(PIECES) - 1):
                    square_piece(i, junk, squares_v)

            def mean(pieces):
                dve.wait_ge(squares, c.next(squares))
                nc.vector.tensor_reduce(norm[:, 0, 0:2], sumsq[:, :, 0:pieces], AX.X, ALU.add).then_inc(mean_ready, 1)
                dve.wait_ge(rms_ready, c.next(rms_ready))
                nc.vector.reciprocal(norm[:, 2, 0:2], norm[:, 1, 0:2]).then_inc(rstd_ready, 1)
                dve.wait_ge(rstd_ready, c.next(rstd_ready))

            def root_mean(first, junk=half_flat):
                first()
                square_piece(len(PIECES) - 1, junk, squares_v)
                mean(len(PIECES))

            def scale_tile(shift=None, gain=None):
                for q in range(4):
                    nc.vector.tensor_scalar(xn[:, 1, q * NW:(q + 1) * NW], h[:, 1, q * NW:(q + 1) * NW],
                                            norm[:, 2, 1:2], None, ALU.mult).then_inc(scaled_v, 1)
                if shift is not None:
                    nc.vector.scalar_tensor_tensor(affine[:], shift[1], 1.0, gain, ALU.add, ALU.mult).then_inc(mod_cols, 1)
                    dve.wait_ge(mod_cols, c.next(mod_cols))

            def to_features(gain, shift=None, ahead=SLOTS, mods=None):
                b0 = 4 * ((c.n.get("groups", 0) + 1) % 2)
                for b in range(BANKS):
                    dve.wait_ge(x_upper, c.next(x_upper))
                    for k in (2 * b, 2 * b + 1):
                        src = ps[:, b0 + b % 4, S * (k % 2):S * (k % 2) + S]
                        if shift is None:
                            op = nc.vector.scalar_tensor_tensor(xs[:, k, 1, :], src, gain[:, k:k + 1], xs[:, k, 0, :],
                                                                ALU.mult, ALU.subtract)
                        else:
                            op = nc.vector.tensor_scalar(tmp[:, k % 2, :], src, affine[:, k:k + 1],
                                                         shift[0][:, k:k + 1], ALU.mult, ALU.add)
                    if shift is not None:
                        link(op)
                        op = nc.vector.tensor_tensor(xs[:, 2 * b:2 * b + 2, 1, :], tmp[:], xs[:, 2 * b:2 * b + 2, 0, :],
                                                     ALU.subtract)
                    op.then_inc(x_ready, 1)
                    if shift is not None:
                        dve.wait_ge(x_ready, c.at(x_ready, b + 1))
                    if b >= ahead:
                        split(4, NW, std_steps(NW)[b % 2], b % 2 == 0)
                    if mods is not None and b in (5, 7):
                        add_mod(mods + (b == 7))
                c.next(x_ready, BANKS)

            def final_norm(gain_wait):
                dve.wait_ge(gain_landed, gain_wait)
                for t in range(T):
                    for o, n in HALVES:
                        nc.vector.scalar_tensor_tensor(h[:, t, o:o + n], h[:, t, o:o + n], norm[:, 2, t:t + 1],
                                                       gainrow[:, o:o + n], ALU.mult, ALU.mult).then_inc(h_ready, 1)
                dve.wait_ge(h_ready, c.next(h_ready, 2 * T))

            dve.wait_ge(x_landed[1], 16)
            squares_ahead()
            root_mean(lambda: None)
            scale_tile()
            dve.wait_ge(rows_turned, 1)
            nc.vector.tensor_copy(vcol[:, 0:100], ps[:, 0, 0:100])
            nc.vector.tensor_copy(vcol[:, P:], ps[:, 0, P:2 * P + CMP_LEN]).then_inc(cols_ready, 1)
            dve.wait_ge(cols_ready, 1)
            split_ahead(0, 2)
            to_features(vcol[:, COL["mix"]:COL["mix"] + KC], ahead=2)
            dve.wait_ge(c_sigmoid, 1)
            link(nc.vector.tensor_tensor(silu_c[:], silu_c[:], vcol[:, COL["c"]:COL["c"] + KC], ALU.mult))
            add_mod(0)
            add_mod(1)

            def nothing(ahead):
                pass

            def bias_table_out(ahead):
                dve.wait_ge(bias_sum, 1)
                dve.wait_ge(bias_placed, 1)
                nc.vector.tensor_copy(table[:, P - 1:2 * P - 1], ps[0:SWA_HEADS, 4, 0:P]).then_inc(bias_table, 1)

            def heads_out(parity, i):
                return columns_out(parity, heads[:, bass.ds(i * 4, 4), :])

            group([heads_out(0, 0)], mods=2)
            per = {"steps": 16, "groups": 2, upper_ready: 16, half_copied: 2, mod_added: 4,
                   mod_landed[0]: 32, mod_landed[1]: 32}
            with loop(dve, c, 3, per) as i:
                group([heads_out(1, i * 2 + 1)], mods=i * 4 + 4)
                group([heads_out(0, i * 2 + 2)], mods=i * 4 + 6)
            def clear(what):
                def f(ahead):
                    own_before()
                    link(nc.vector.memset(what, 0.0))
                return f

            def blocks(i, half_):
                def f(ahead):
                    src = heads[:, 16 + 4 * i:20 + 4 * i, :].rearrange("p g (m b) -> p g m b", b=CMP_STRIDE)
                    dst = blk[:, CMP_STRIDE * half_:CMP_STRIDE * (half_ + 1)].rearrange("p l g n -> p g n l")
                    o = COL["kv"[i]] + CMP_STRIDE * half_
                    for g in range(NSA_G):
                        op = nc.vector.tensor_tensor(dst[:, g], src[:, g, half_:half_ + N_CMP],
                                                     vcol[:, o:o + CMP_STRIDE].unsqueeze(1).to_broadcast([P, N_CMP, CMP_STRIDE]),
                                                     ALU.add)
                    if half_:
                        op.then_inc(blk_ready, 1)
                return f

            def hidden_silu(i):
                def f(ahead):
                    dve.wait_ge(cmp_sigmoid, i + 1)
                    nc.vector.tensor_tensor(hid[:, :, 3 * CPAD:3 * CPAD + N_CMP],
                                            ps[:, 2 + i, 0:NSA_G * N_CMP].rearrange("p (g n) -> p g n", n=N_CMP),
                                            csig[:], ALU.mult).then_inc(hid_ready, 1)
                return f

            def keys_out(ahead):
                dve.wait_ge(direct_used, 3)
                nc.vector.tensor_copy(kcmp[:].rearrange("p g n -> p (g n)"), ps[:, 3, 0:P]).then_inc(cmp_stored, 1)

            group([heads_out(1, 7), clear(hid[:]), clear(cprob[:]), bias_table_out, blocks(0, 0), blocks(0, 1)],
                  store=0)
            st["unit"] += 3
            group([copy_rows(0, vtok[:, 0]), hidden_silu(0), keys_out, blocks(1, 0), blocks(1, 1)])
            st["unit"] += 3
            split(KC, 48, (0, KC, 0, 48), True)
            copy_rows(1, vtok[:, 1])(1)
            dve.wait_ge(c_scores, 1)
            flat = cprob[:].rearrange("p t h n -> p (t h) n")[:, :, 0:N_CMP]
            for t in range(T):
                op = nc.vector.scalar_tensor_tensor(
                    cprob[:, t, :, 0:N_CMP], ps[:, 7, S * t:S * t + S].rearrange("p (h n) -> p h n", n=16)[:, :, 0:N_CMP],
                    DH ** -0.5, cmask[:, 0, t].unsqueeze(1).to_broadcast([P, NSA_HEADS, N_CMP]), ALU.mult, ALU.add)
            link(op)
            link(nc.vector.tensor_reduce(cstat[:, 0, :], flat, AX.X, ALU.max))
            nc.vector.tensor_tensor(flat, flat, cstat[:, 0, :].unsqueeze(2).to_broadcast([P, T * NSA_HEADS, N_CMP]),
                                    ALU.subtract).then_inc(c_shifted, 1)
            hidden_silu(1)(0)
            dve.wait_ge(gate_half, 1)
            done(nc.vector.tensor_tensor(gsum[:, 1, :], ps[0:48, 0, 0:S], gsum[:, 0, :], ALU.add))
            own_before()
            nc.vector.tensor_copy(gsum[:, 0, :], gsum[:, 1, :]).then_inc(gate_sum, 1)
            dve.wait_ge(direct_used, 6)
            nc.vector.tensor_copy(vcmp[:].rearrange("p h n -> p (h n)"),
                                  ps[:, 3:7, :].rearrange("p b n -> p (b n)")).then_inc(cmp_stored, 1)
            dve.wait_ge(c_exp, 1)
            link(nc.vector.tensor_reduce(cstat[:, 1, :], flat, AX.X, ALU.add))
            link(nc.vector.reciprocal(cstat[:, 2, :], cstat[:, 1, :]))
            dve.wait_ge(gate_ready, 1)
            dve.wait_ge(bias_stored, 16)
            link(nc.vector.tensor_tensor(cstat[:, 2, :].rearrange("p (t h) -> p t h", t=T),
                                         cstat[:, 2, :].rearrange("p (t h) -> p t h", t=T),
                                         gates[:].rearrange("p t (h b) -> p t h b", b=3)[:, :, :, 0], ALU.mult))
            for t in range(T):
                op = nc.vector.tensor_tensor(cprob[:, t, :, 0:N_CMP], cprob[:, t, :, 0:N_CMP],
                                             cmask[:, 1, t].unsqueeze(1).to_broadcast([P, NSA_HEADS, N_CMP]), ALU.mult)
            link(op)
            nc.vector.tensor_tensor(flat, flat, cstat[:, 2, :].unsqueeze(2).to_broadcast([P, T * NSA_HEADS, N_CMP]),
                                    ALU.mult).then_inc(c_scaled, 1)

            def mix_lower(jobs, n):
                kind, i, b = jobs[n]
                if kind == "nsa" and not b:
                    return
                dve.wait_ge(mix_upper, c.next(mix_upper))
                if kind == "swa":
                    k, w, src = 2 * i, 2, ps[:, 6 + i % 2, :].rearrange("p (c s) -> p c s", s=S)
                else:
                    k, w = (4 * i if kind == "nsa" else 8 + 4 * i), 4
                    src = ps[:, 6:8, :].rearrange("p b (c s) -> p (b c) s", s=S)
                nc.vector.tensor_tensor(xs[:, k:k + w, 1, :], src, xs[:, k:k + w, 0, :],
                                        ALU.subtract).then_inc(mix_ready, 1)

            def attention(jobs, base):
                for n in range(len(jobs)):
                    kind, i, b = jobs[n]
                    m, par = base + n, (base + n) % 2
                    sb = banks_of(kind)[0]
                    dve.wait_ge(scores, 2 * m + 1)
                    nc.vector.tensor_reduce(stat[:, 0, par, 0:4], ps[:, sb, :].rearrange("p (h k) -> p h k", k=P), AX.X, ALU.max)
                    dve.wait_ge(scores, 2 * m + 2)
                    wide = ps[:, sb + 1:sb + 3, :].rearrange("p b (h k) -> p (b h) k", k=S)
                    link(nc.vector.tensor_reduce(stat[:, 0, par, 4:8], wide, AX.X, ALU.max))
                    if kind == "swa":
                        sk = sinks[:, 4 * i:4 * i + 4].unsqueeze(1).to_broadcast([P, T, 4])
                        v = stat[:, 0, par, :].rearrange("p (t h) -> p t h", t=T)
                        link(nc.vector.tensor_tensor(v, v, sk, ALU.max))
                        nc.vector.tensor_tensor(stat[:, 4, par, :].rearrange("p (t h) -> p t h", t=T), sk, v, ALU.subtract)
                    scale = {"nsa": DH ** -0.5, "swa": 1.0, "mla": QK ** -0.5}[kind]
                    nc.vector.tensor_scalar(stat[:, 1, par, :], stat[:, 0, par, :], -scale, None,
                                            ALU.mult).then_inc(bias_ready, 1)
                    if n >= 3:
                        mix_lower(jobs, n - 3)
                    if 2 <= n < 2 + SLOTS:
                        split(4, NW, std_steps(NW)[n % 2], n % 2 == 0)
                    dve.wait_ge(exps, 2 * m + 2)
                    if kind == "swa":
                        link(nc.vector.tensor_tensor(stat[:, 2, par, :], stat[:, 2, par, :], stat[:, 4, par, :], ALU.add))
                    link(nc.vector.reciprocal(stat[:, 3, par, :], stat[:, 2, par, :]))
                    if kind == "nsa":
                        for t in range(T):
                            v = stat[:, 3, par, 4 * t:4 * t + 4]
                            op = nc.vector.tensor_tensor(v, v, gate_view(t, i, 1 + b), ALU.mult)
                        link(op)
                    for t in range(T):
                        w = P * (t + 1)
                        v = prob[:, par, 512 * t:512 * t + 4 * w].rearrange("p (h k) -> p h k", k=w)
                        r = stat[:, 3, par, 4 * t:4 * t + 4].unsqueeze(2).to_broadcast([P, 4, w])
                        op = nc.vector.tensor_tensor(v, v, r, ALU.mult)
                    op.then_inc(prob_ready, 1)
                for n in range(len(jobs) - 3, len(jobs)):
                    mix_lower(jobs, n)

            attention(NSA_JOBS, 0)
            st_par = lambda: c.n["groups"] % 2

            def norm_behind(pending, junk, shift=None, gain_cols=None):
                squares_ahead(junk)
                split_ahead(0, SLOTS - 1)
                pending(SLOTS - 1)
                root_mean(own_before, junk)
                scale_tile(shift, gain_cols)
                split_ahead(SLOTS - 1, SLOTS)

            def project(gain=None, mods=None, first=(), **norm_args):
                p0 = st_par()
                for g in range(NG):
                    group([add_rows((p0 + g - 1) % 2, g - 1, gain)] if g else first,
                          mods=None if mods is None else mods + 2 * g, at=(3, 6) if g else (6, 7),
                          start=0 if g else SLOTS)
                norm_behind(add_rows((p0 + NG - 1) % 2, NG - 1, gain), junk=xn[:, 1, :], **norm_args)

            def pin_lower(ahead):
                dve.wait_ge(p_upper, 1)
                nc.vector.tensor_tensor(pin[:, :, 1, :], ps[:, 2, :].rearrange("p (k s) -> p k s", s=S), pin[:, :, 0, :],
                                        ALU.subtract).then_inc(p_ready, 1)

            project(mods=0, first=[nothing, nothing, pin_lower])

            def quarter(pending, p0, gain, m, first_split=False):
                for g in range(NG):
                    if g or not first_split:
                        group(pending, mods=None if m is None else 8 + 2 * g)
                    pending = [square((p0 + g) % 2), lower_hidden(g)]
                for g in range(NG):
                    group(pending, mods=None if m is None else 2 * g, store=m if g == 0 else None)
                    pending = [add_rows((p0 + g) % 2, g, gain)]

            def ffn(gain, modulated):
                p0 = st_par()
                last = add_rows((p0 + 1) % 2, NG - 1, gain)
                quarter([], p0, gain, 1 if modulated else None, first_split=True)
                per = {"steps": 64, "groups": 8, upper_ready: 64, half_copied: 4, hidden_upper: 4}
                if gain is not None:
                    per[dve_step] = 4
                if modulated:
                    per[dve_step] = 1
                    per.update({mod_landed[0]: 128, mod_landed[1]: 128, mod_added: 16, mod_summed: 1})
                with loop(dve, c, QUARTERS - 1, per) as i:
                    quarter([last], p0, gain, i + 2 if modulated else None)
                return last

            to_features(vcol[:, COL["ffn"]:COL["ffn"] + KC], mods=8)
            last = ffn(None, True)

            squares_ahead()
            for g in range(NG - 1):
                split(2, 1024, (0, 2, 512 * (g % 2), 512), g % 2 == 0)
            last(NG - 1)
            split(2, 1024, (0, 2, 512, 512), False)
            root_mean(own_before)
            scale_tile()
            for g in range(NG):
                copy_rows(st_par(), embed[:, :, g * NW:(g + 1) * NW])(NG - 1 - g)
            to_features(vcol[:, COL["ple"]:COL["ple"] + KC], ahead=0, mods=8)

            def gated(g):
                def f(ahead):
                    sv, hv = half[:].rearrange("p (t a) s -> p t (a s)", t=T), h[:, :, g * NW:(g + 1) * NW]
                    dve.wait_ge(ple_gate, c.next(ple_gate))
                    link(nc.vector.tensor_tensor(sv, sv, embed[:, :, g * NW:(g + 1) * NW], ALU.mult))
                    done(nc.vector.tensor_tensor(hv, sv, hv, ALU.add))
                return f

            for g in range(1, NG):
                group([gated(g - 1)], mods=8 + 2 * g)
            squares_ahead(xn[:, 1, :])
            split_ahead(0, SLOTS - 1)
            gated(NG - 1)(SLOTS - 1)
            root_mean(own_before, xn[:, 1, :])
            final_norm(16)

            store_mod(5)
            dve.wait_ge(mod_stored, 6)
            mean(len(HALVES))
            scale_tile((modcol[:, 0, :], modcol[:, 1, :]), vcol[:, COL["attn"]:COL["attn"] + KC])
            split_ahead(SLOTS - 1, SLOTS)
            p0 = st_par()
            to_features(None, (modcol[:, 0, :], modcol[:, 1, :]))

            def scaled_queries(parity, dst):
                def f(ahead):
                    dve.wait_ge(half_copied, c.next(half_copied))
                    done(nc.vector.tensor_tensor(dst, ps[:, 4 * parity:4 * parity + 4, 0:S], half[:], ALU.add))
                    own_before()
                    link(nc.vector.tensor_scalar(dst, dst, SWA_D ** -0.5, None, ALU.mult))
                return f

            LATENTS = ((256, Q_RANK), (640, KV_RANK))
            R = ROPE // 2

            def modulation_rows(ahead):
                dve.wait_ge(mod_turned, 1)
                nc.vector.tensor_copy(modrow[:], ps[0:6 * KC, 2, 0:P]).then_inc(mod_rows, 1)

            def latent_squares(t):
                def f(ahead):
                    if t == 0:
                        copy_rows(1 - p0, tok[:, :, NW:832])(ahead)
                        own_before()
                    for i, (o, n) in enumerate(LATENTS):
                        op = nc.vector.tensor_tensor_reduce(half_flat[:, 0:n], tok[:, t, o:o + n], tok[:, t, o:o + n], 1.0, 0.0,
                                                            ALU.mult, ALU.add, norm[:, 0, 2 * i + t:2 * i + t + 1])
                        if t and i:
                            op.then_inc(lat_squares, 1)
                            dve.wait_ge(lat_squares, 1)
                        else:
                            link(op)
                return f

            def latent_scale(ahead):
                dve.wait_ge(lat_rms, 1)
                link(nc.vector.reciprocal(norm[:, 2, :], norm[:, 1, :]))
                for i, (o, n) in enumerate(LATENTS):
                    for t in range(T):
                        v = tok[:, t, o:o + n]
                        op = nc.vector.tensor_scalar(v, v, norm[:, 2, 2 * i + t:2 * i + t + 1], None, ALU.mult)
                op.then_inc(lat_scaled, 1)

            def latent_lower(ahead):
                for k in range(4):
                    dve.wait_ge(lat_upper, k // 2 + 1)
                    up, low = (cqs[:, k, j, :] if k < 3 else ckvs[:, 0, j, :] for j in range(2))
                    nc.vector.scalar_tensor_tensor(low, ps[:, 2 + k // 2, S * (k % 2):S * (k % 2) + S],
                                                   vcol[:, COL["q"] + k:COL["q"] + k + 1], up,
                                                   ALU.mult, ALU.subtract).then_inc(lat_ready, 1)

            def rotate(x1, x2, o1, o2, cos, sin, t1, t2):
                nc.vector.tensor_tensor(t1, x1, cos, ALU.mult)
                link(nc.vector.tensor_tensor(t2, x2, sin, ALU.mult))
                link(nc.vector.tensor_tensor(o1, t1, t2, ALU.subtract))
                nc.vector.tensor_tensor(t1, x2, cos, ALU.mult)
                link(nc.vector.tensor_tensor(t2, x1, sin, ALU.mult))
                return nc.vector.tensor_tensor(o2, t1, t2, ALU.add)

            def rotate_keys(ahead):
                dve.wait_ge(aux_landed, 16 * 5)
                dve.wait_ge(pads_ready, 1)
                for t in range(T):
                    link(rotate(tok[:, t, 768:768 + R], tok[:, t, 768 + R:832], krope[:, t, 0, 0, 0:R], krope[:, t, 0, 0, R:ROPE],
                                angle[:, 0, t], angle[:, 1, t], rope_t[:, 0, 0], rope_t[:, 1, 0]))
                nc.vector.tensor_copy(krope[:, :, 1, 1, :], krope[:, :, 0, 0, :]).then_inc(krope_ready, 1)

            def rotate_queries(t):
                cos, sin = (angle[:, j, t].unsqueeze(1).to_broadcast([P, MLA_HEADS, R]) for j in range(2))
                op = rotate(qb[:, t, :, NOPE:NOPE + R], qb[:, t, :, NOPE + R:QK], qrope[:, t, :, 0:R],
                            qrope[:, t, :, R:ROPE], cos, sin, rope_t[:, 0], rope_t[:, 1])
                op.then_inc(roped, 1)
                dve.wait_ge(roped, t + 1)

            def split_uq():
                split(3, NW, (0, 2, 0, NW), True)
                split(3, NW, (2, 1, 0, NW), False)

            def queries_out(parity, g):
                return copy_rows(parity, qb[:].rearrange("p t h d -> p t (h d)")[:, :, g * NW:(g + 1) * NW])

            group([copy_rows(p0, tok[:, :, 0:NW]), modulation_rows], n=320)
            group([latent_squares(0), latent_squares(1), latent_scale, nothing, nothing, latent_lower])
            group([scaled_queries(p0, qa[:, 0:4, :]), nothing, rotate_keys])
            split_uq()
            scaled_queries(1 - p0, qa[:, 4:8, :])(2)
            split_uq()
            queries_out(p0, 0)(2)
            split_uq()
            queries_out(1 - p0, 1)(2)
            split(1, D, (0, 1, 0, 1024), True)
            split(1, D, (0, 1, 1024, 1024), False)
            queries_out(p0, 2)(2)
            own_before()
            columns_out(0, kn[:, 0:4, :])(0)
            rotate_queries(0)
            columns_out(0, kn[:, 4:8, :])(0)
            rotate_queries(1)
            dve.wait_ge(heads_turned, 4)
            nc.vector.tensor_copy(qn[:, 4:8, :].rearrange("p h s -> p (h s)"),
                                  ps[:, 4:6, :].rearrange("p b n -> p (b n)")).then_inc(queries_copied, 1)
            attention(LATE_JOBS, len(NSA_JOBS))
            dve.wait_ge(gain_row, 16 * 2)
            shift = (modcol[:, 3, :], modcol[:, 4, :])
            project(gain1, shift=shift, gain_cols=vcol[:, COL["mlp"]:COL["mlp"] + KC])
            to_features(None, shift)
            last = ffn(gain2, False)
            squares_ahead()
            last(0)
            root_mean(own_before)
            final_norm(32)

        @block.tensor
        def _(pe):
            c = Counts()
            st = dict(step=0)
            mm = nc.tensor.matmul

            def parity():
                return c.n.get("groups", 0) % 2

            def bank_free(p):
                if c.reg is not None or c.n.get("groups", 0) >= 2:
                    pe.wait_ge(evacuated, c.at("groups", -1))
                c.next("groups")

            def step(nk, nn, ready=None):
                if ready:
                    pe.wait_ge(*ready)
                pe.wait_ge(lower_ready, c.next(lower_ready))
                slot = st["step"] % SLOTS
                st["step"] += 1
                return slot_view(upper, slot, nk, nn), slot_view(lower, slot, nk, nn)

            def rows(x, par, k, kk, up, low, first, last):
                n = up.shape[-1]
                for t in range(T):
                    out = ps[:, 4 * par + t, 0:n]
                    xu, xl = (x[:, k, j, t * P:(t + 1) * P] for j in range(2))
                    mm(out, xu, up[:, kk, :], start=first, stop=False)
                    mm(out, xu, low[:, kk, :], start=False, stop=False)
                    op = mm(out, xl, up[:, kk, :], start=False, stop=last)
                return op

            def columns(x, par, k, kk, up, low, first, last):
                for f in range(4):
                    both = x[:, k].rearrange("p j s -> p (j s)")
                    mm(ps[:, 4 * par + f, :], up[:, kk, f * P:(f + 1) * P], both, start=first, stop=False,
                       skip_group_check=True)
                    op = mm(ps[:, 4 * par + f, 0:S], low[:, kk, f * P:(f + 1) * P], x[:, k, 0, :],
                            start=False, stop=last, skip_group_check=True)
                return op

            def group(form, x, n=NW, ready=None, between=None):
                p = st["par"] = (st["par"] + 1) % 2
                bank_free(p)
                for s in range(8):
                    if ready:
                        ready(s)
                    up, low = step(2, n)
                    for kk in range(2):
                        k = 2 * s + kk
                        op = form(x, p, k, kk, up, low, k == 0, k == KC - 1)
                    op.then_inc(step_used, 1)
                    if between and s in between:
                        between[s]()

            st["par"] = 1

            def group_turned(form, norms):
                p = st["par"] = (st["par"] + 1) % 2
                b0 = 4 * (1 - p)
                if c.n.get("groups", 0):
                    pe.wait_ge(evacuated, c.at("groups"))
                c.next("groups")

                def turn(b):
                    if b % 2 == 0:
                        pe.wait_ge(scaled_a, 4 * norms + b // 2 + 1)
                        pe.wait_ge(scaled_v, 4 * norms + b // 2 + 1)
                    for k in (2 * b, 2 * b + 1):
                        for t in range(T):
                            o = S * (k % 2) + t * P
                            op = nc.tensor.transpose(ps[:, b0 + b % 4, o:o + P], xn[:, t, k * P:(k + 1) * P], ident[:])
                    op.then_inc(turned, 1)

                for b in range(4):
                    turn(b)
                for s in range(8):
                    pe.wait_ge(x_ready, BANKS * norms + s + 1)
                    up, low = step(2, NW)
                    for kk in range(2):
                        k = 2 * s + kk
                        op = form(xs, p, k, kk, up, low, k == 0, k == KC - 1)
                    op.then_inc(step_used, 1)
                    if s + 4 < BANKS:
                        turn(s + 4)

            def sum_mod(wait, before=-1):
                pe.wait_ge(mod_added, wait)
                pe.wait_ge(evacuated, c.at("groups", before))
                for k in range(KC):
                    op = nc.tensor.transpose(ps[:, (2, 3, 6, 7)[k // 4], k % 4 * P:(k % 4 + 1) * P],
                                             modacc[:, k * P:(k + 1) * P], ident[:])
                op.then_inc(mod_summed, 1)

            pe.wait_ge(consts, 1)
            pe.wait_ge(rows_landed, 16 * 11)
            for j, n in ((0, 100), (1, P), (2, CMP_LEN)):
                op = nc.tensor.transpose(ps[:, 0, j * P:j * P + n], vrow[0:n, j, :], ident[0:n, 0:n])
            op.then_inc(rows_turned, 1)

            group_turned(columns, 0)
            group(columns, xs)
            with loop(pe, c, 3, {lower_ready: 16, "groups": 2}):
                group(columns, xs)
                group(columns, xs)

            def sums_and_bias():
                sum_mod(KC)
                pe.wait_ge(aux_landed, 16 * 5)
                mm(ps[0:SWA_HEADS, 4, 0:P], relb[:], onehot[:], start=True, stop=True).then_inc(bias_sum, 1)

            UNITS = [(36, 37, 38), (43, 44, 45)]

            def raw_weights(u, l):
                if l == 0:
                    pe.wait_ge(landed[u % SLOTS], 16 * (u // SLOTS + 1))
                return raw[:, u % SLOTS, l * P:(l + 1) * P]

            def hidden_layer(i):
                pe.wait_ge(blk_ready, i + 1)
                for l in range(CMP_LEN):
                    op = mm(ps[:, 2 + i, 0:NSA_G * N_CMP], raw_weights(UNITS[i][l // 16], l % 16),
                            blk[:, l].rearrange("p g n -> p (g n)"), start=(l == 0), stop=(l == CMP_LEN - 1))
                    if l % 16 == 15:
                        op.then_inc(direct_used, 1)

            def compressed_keys():
                w = raw_weights(UNITS[0][2], 0)
                pe.wait_ge(hid_ready, 1)
                mm(ps[:, 3, 0:P], w, hid[:, :, 3 * CPAD:4 * CPAD], start=True, stop=True).then_inc(direct_used, 1)

            def compressed_scores():
                pe.wait_ge(cmp_stored, 1)
                for t in range(T):
                    for hh in range(NSA_HEADS):
                        op = mm(ps[:, 7, S * t + 16 * hh:S * t + 16 * hh + N_CMP], heads[:, hh, t * P:(t + 1) * P],
                                kcmp[:, hh // HPG, 0:N_CMP], start=True, stop=True)
                op.then_inc(c_scores, 1)

            group(rows, xs, between={1: sums_and_bias})
            hidden_layer(0)
            group(rows, xs, between={1: compressed_keys, 4: compressed_scores})
            hidden_layer(1)
            st["par"] = 0
            bank_free(0)
            up, low = step(KC, 48)
            for k in range(KC):
                mm(ps[0:48, 0, :], up[:, k, :], xs[:, k].rearrange("p j s -> p (j s)"), start=(k == 0), stop=False,
                   skip_group_check=True)
                op = mm(ps[0:48, 0, 0:S], low[:, k, :], xs[:, k, 0, :], start=False, stop=(k == KC - 1),
                        skip_group_check=True)
            op.then_inc(step_used, 1)
            pe.wait_ge(evacuated, c.at("groups", -1))
            w = raw_weights(UNITS[1][2], 0)
            pe.wait_ge(hid_ready, 2)
            for g in range(NSA_G):
                for j in range(HPG):
                    op = mm(ps[:, 3 + g, j * DH:(j + 1) * DH], hid[:, g, (3 - j) * CPAD:(7 - j) * CPAD], w,
                            start=True, stop=True)
            op.then_inc(direct_used, 1)
            pe.wait_ge(gate_sum, 1)
            for t in range(T):
                op = nc.tensor.transpose(ps[:, 1, P * t:P * t + 48], gsum[:, 0, t * P:(t + 1) * P], ident[0:48, 0:48])
            op.then_inc(gate_turned, 1)
            pe.wait_ge(cmp_stored, 2)
            pe.wait_ge(gate_ready, 1)

            def score(n, kind, i, b):
                sb = banks_of(kind)[0]
                if kind == "swa":
                    pe.wait_ge(toe_landed[i], 16)
                for t in range(T):
                    w = P * (t + 1)
                    if n:
                        pe.wait_ge(exps, 2 * n - 1 + t)
                    for j in range(HPG):
                        out = ps[:, sb, P * j:P * j + P] if t == 0 else ps[:, sb + 1 + j // 2, S * (j % 2):S * (j % 2) + S]
                        first = j == 0 if t == 0 else j % 2 == 0
                        hh = HPG * i + j
                        if kind == "nsa":
                            pairs = [(heads[:, hh, t * P:(t + 1) * P], heads[:, 24 + 4 * b + i, 0:w])]
                        elif kind == "swa":
                            pairs = [(qa[:, hh // 2, t * P:(t + 1) * P], ka[:, i // 2, hh % 2, 0:w])]
                        else:
                            pairs = [(qn[:, hh, t * P:(t + 1) * P], kn[:, hh, 0:w]),
                                     (qr[:, hh // 2, t * P:(t + 1) * P], kr[:, hh % 2, 0:w])]
                        for q, k in pairs:
                            op = mm(out, q, k, start=first, stop=False, skip_group_check=True)
                            first = False
                        if kind == "swa":
                            for kt in range(t + 1):
                                x0 = P * (t - kt)
                                op = mm(out[:, P * kt:P * kt + P], toes[:, i, j, x0:x0 + P], flip[:], start=False,
                                        stop=True, skip_group_check=True)
                    if kind != "swa":
                        mask = causal_b[:].unsqueeze(1)
                        if t == 0:
                            op = mm(ps[:, sb, :], ident_b[:], mask.to_broadcast([P, 4, P]), start=False, stop=True, skip_group_check=True)
                        else:
                            for b_ in (1, 2):
                                out = ps[:, sb + b_, :].rearrange("p (h k) -> p h k", k=S)[:, :, P:S]
                                op = mm(out, ident_b[:], mask.to_broadcast([P, 2, P]), start=False, stop=True, skip_group_check=True)
                    op.then_inc(scores, 1)

            def turn_probs(n, kind):
                tb = banks_of(kind)[1]
                pe.wait_ge(prob_ready, n + 1)
                if n:
                    pe.wait_ge(probT_ready, n)
                for j in range(HPG):
                    bank, o = tb + j // 2, S * (j % 2)
                    p = prob[:, n % 2, :]
                    nc.tensor.transpose(ps[:, bank, o:o + P], p[:, P * j:P * j + P], ident[:])
                    nc.tensor.transpose(ps[:, bank, o + P:o + S], p[:, 512 + S * j:512 + S * j + P], ident[:])
                    op = nc.tensor.transpose(ps[:, tb + 2, P * j:P * j + P], p[:, 512 + S * j + P:512 + S * j + S], ident[:])
                op.then_inc(prob_turned, 1)

            def mix(n, kind, i, b):
                pe.wait_ge(probT_ready, n + 1)
                if kind != "nsa" or not b:
                    if c.n.get(mix_ready, 0):
                        pe.wait_ge(mix_ready, c.at(mix_ready, -1 if kind == "swa" and i else 0))
                    c.next(mix_ready)
                for j in range(HPG):
                    hh = HPG * i + j
                    if kind == "swa":
                        r = slice(64 * (j % 2), 64 * (j % 2) + 64)
                        out = ps[r, 6 + i % 2, S * (j // 2):S * (j // 2) + S]
                        v = [tok[:, kt, P + 64 * (i // 2):P + 64 * (i // 2) + 64] for kt in range(T)]
                        first = j < 2
                    else:
                        out = ps[:, 6 + j // 2, S * (j % 2):S * (j % 2) + S]
                        first = j % 2 == 0 and not b
                        v = [vtok[:, b, kt, i * DH:(i + 1) * DH] if kind == "nsa" else vb[:, kt, hh, :] for kt in range(T)]
                    if kind == "nsa" and not b:
                        mm(out, vcmp[:, hh, :], cprobT[:, i, :], start=first, stop=False, skip_group_check=True)
                        first = False
                    mm(out, v[0], probT[:, n % 2, S * j:S * j + S], start=first, stop=False, skip_group_check=True)
                    op = mm(out[:, P:S], v[1], probT[:, n % 2, 1024 + P * j:1024 + P * j + P], start=False, stop=True,
                            skip_group_check=True)
                op.then_inc(pv_done, 1)

            def attention(jobs, base, after_first=None):
                score(base, *jobs[0])
                for n in range(len(jobs)):
                    if n + 1 < len(jobs):
                        score(base + n + 1, *jobs[n + 1])
                    if n == 0 and after_first:
                        after_first()
                    turn_probs(base + n, jobs[n][0])
                    if n:
                        mix(base + n - 1, *jobs[n - 1])

            def product_behind(jobs, base, ready_at, also):
                def ready(s):
                    if s in ready_at:
                        pe.wait_ge(mix_ready, ready_at[s])
                group(rows, xs, ready=ready, between={1: lambda: mix(base + len(jobs) - 1, *jobs[-1]), **also})

            def turn_compressed():
                pe.wait_ge(c_scaled, 1)
                for g in range(NSA_G):
                    for t in range(T):
                        op = nc.tensor.transpose(ps[:, 1 + g // 2, S * (g % 2) + P * t:S * (g % 2) + P * t + P],
                                                 cprob[:, t, HPG * g:HPG * g + HPG, :].rearrange("p h n -> p (h n)"), ident[:])
                op.then_inc(c_turned, 1)
                pe.wait_ge(c_prob, 1)

            attention(NSA_JOBS, 0, turn_compressed)

            def turn_inputs():
                pe.wait_ge(p_landed, 16)
                for k in range(2):
                    for t in range(T):
                        o = S * k + t * P
                        op = nc.tensor.transpose(ps[:, 2, o:o + P], prow[:, t, k * P:(k + 1) * P], ident[:])
                op.then_inc(p_turned, 1)

            product_behind(NSA_JOBS, 0, {0: NSA_G - 1, 6: NSA_G}, {2: turn_inputs})
            for g in range(1, NG):
                group(rows, xs)

            def quarter(norms, between):
                for g in range(NG):
                    if g == 0 and norms is not None:
                        group_turned(columns, norms)
                    else:
                        group(columns, xs)
                for g in range(NG):
                    def ready(s, g=g):
                        if g == 0 and s in (0, 6):
                            pe.wait_ge(hidden_ready, c.next(hidden_ready, 3 if s == 0 else 1))
                    group(rows, hidden, ready=ready, between={1: between} if between and g == 0 else None)

            def ffn(norms, modulated):
                def between():
                    sum_mod(c.at("mods", 0))
                    c.next("mods", KC)
                if modulated:
                    c.n["mods"] = 2 * KC
                quarter(norms, between if modulated else None)
                per = {lower_ready: 64, "groups": 8, hidden_ready: 4}
                if modulated:
                    per["mods"] = KC
                with loop(pe, c, QUARTERS - 1, per):
                    quarter(None, between if modulated else None)

            ffn(1, True)
            pe.wait_ge(p_ready, 1)
            for g in range(NG):
                st["par"] = (st["par"] + 1) % 2
                bank_free(st["par"])
                up, low = step(2, NW)
                for k in range(2):
                    op = rows(pin, st["par"], k, k, up, low, k == 0, k == 1)
                op.then_inc(step_used, 1)
            group_turned(rows, 2)
            for g in range(1, NG):
                group(rows, xs)
            pe.wait_ge(evacuated, c.at("groups"))
            sum_mod(6 * KC, 0)
            pe.wait_ge(mod_stored, 6)

            def turn_modulation():
                nc.tensor.transpose(ps[0:6 * KC, 2, 0:P], modcol[:].rearrange("p m k -> p (m k)"),
                                    ident[:]).then_inc(mod_turned, 1)

            def turn_latents():
                pe.wait_ge(lat_scaled, 1)
                for k in range(4):
                    for t in range(T):
                        o = S * (k % 2) + t * P
                        op = nc.tensor.transpose(ps[:, 2 + k // 2, o:o + P], tok[:, t, 256 + k * P:256 + (k + 1) * P], ident[:])
                    if k % 2:
                        op.then_inc(lat_turned, 1)

            group_turned(rows, 3)
            group(rows, xs, n=320, between={1: turn_modulation})
            group(columns, xs, between={4: turn_latents})
            pe.wait_ge(lat_ready, 4)
            group(columns, xs)

            def turn_pads(g):
                if g == 0:
                    pe.wait_ge(pads_ready, 1)
                    for j in range(SWA_KV):
                        for i in range(2):
                            for t in range(T):
                                o = S * i + t * P
                                op = nc.tensor.transpose(ps[:, 6 + j, o:o + P], kpad[:, t, j, i].rearrange("p a d -> p (a d)"), ident[:])
                    op.then_inc(heads_turned, 1)
                if g == 1:
                    pe.wait_ge(krope_ready, 1)
                    for i in range(2):
                        for t in range(T):
                            o = S * i + t * P
                            op = nc.tensor.transpose(ps[:, 2, o:o + P], krope[:, t, i].rearrange("p a d -> p (a d)"), ident[:])
                    op.then_inc(heads_turned, 1)

            for g in range(3):
                st["par"] = (st["par"] + 1) % 2
                bank_free(st["par"])
                for nk in (2, 1):
                    up, low = step(nk, NW)
                    for kk in range(nk):
                        k = kk + 2 * (nk == 1)
                        op = rows(cqs, st["par"], k, kk, up, low, k == 0, k == 2)
                    op.then_inc(step_used, 1)
                turn_pads(g)
            pe.wait_ge(evacuated, c.at("groups"))
            pe.wait_ge(heads_copied, 2)
            halves = [[x.rearrange("p a (h d) -> p (a h) d", d=NOPE + VD) for x in step(1, 1024)] for _ in range(2)]

            def keys(kv):
                both = ckvs[:, 0].rearrange("p j s -> p (j s)")
                for j in range(4):
                    mm(ps[:, j, :], kv[0][:, j, 0:NOPE], both, start=True, stop=False, skip_group_check=True)
                    op = mm(ps[:, j, 0:S], kv[1][:, j, 0:NOPE], ckvs[:, 0, 0, :], start=False, stop=True,
                            skip_group_check=True)
                return op

            def values(kv, b):
                for t in range(T):
                    xu, xl = (ckvs[:, 0, j, t * P:(t + 1) * P] for j in range(2))
                    vu, vl = (x[:, :, NOPE:] for x in kv)
                    out = ps[:, b + t, :]
                    mm(out, xu, vu, start=True, stop=False)
                    mm(out, xu, vl, start=False, stop=False)
                    op = mm(out, xl, vu, start=False, stop=True)
                return op

            keys(halves[0]).then_inc(kv_done, 1)
            values(halves[0], 4).then_inc(step_used, 1)
            values(halves[1], 6).then_inc(kv_done, 1)
            c.next("groups")
            pe.wait_ge(evacuated, c.at("groups"))
            keys(halves[1]).then_inc(step_used, 1)
            c.next("groups")

            def turn_queries(h0, b):
                for hh in range(h0, h0 + 4):
                    for t in range(T):
                        o = S * (hh % 2) + t * P
                        op = nc.tensor.transpose(ps[:, b + (hh - h0) // 2, o:o + P], qb[:, t, hh, 0:NOPE], ident[:])
                op.then_inc(heads_turned, 1)

            pe.wait_ge(v_stored, 2)
            turn_queries(0, 6)
            turn_queries(4, 4)
            pe.wait_ge(evacuated, c.at("groups"))
            pe.wait_ge(roped, T)
            for j in range(MLA_HEADS // 2):
                for t in range(T):
                    o = S * (j % 2) + t * P
                    op = nc.tensor.transpose(ps[:, j // 2, o:o + P],
                                             qrope[:, t, 2 * j:2 * j + 2, :].rearrange("p h d -> p (h d)"), ident[:])
            op.then_inc(heads_turned, 1)
            pe.wait_ge(heads_copied, 4)
            pe.wait_ge(queries_copied, 1)
            attention(LATE_JOBS, len(NSA_JOBS))
            product_behind(LATE_JOBS, len(NSA_JOBS), {0: NSA_G + 4, 4: NSA_G + 5, 6: NSA_G + 6}, {})
            for g in range(1, NG):
                group(rows, xs)
            ffn(4, False)


_INS = ["x", "p", "norm_mix", "norm_ffn", "norm_ple", "norm_final", "ffn_w1", "ffn_w2", "ple_w_proj", "ple_w_gate",
        "nsa_w_in", "nsa_w_out", "nsa_cmp_pos_k", "nsa_cmp_w1_k", "nsa_cmp_w2_k", "nsa_cmp_pos_v", "nsa_cmp_w1_v",
        "nsa_cmp_w2_v", "c_2", "w_mod_2", "b_mod_2", "attn_norm_g_2", "w_in_2", "swa_sinks_2", "rel_bias_2",
        "mla_q_norm_g_2", "w_uq_2", "mla_kv_norm_g_2", "w_ukv_2", "w_out_2", "mlp_norm_g_2", "w_ff1_2", "w_ff2_2",
        "final_norm_g_2"]


def shape_constants():
    half_ = ROPE // 2
    freq = np.float32(10000.0) ** (-np.arange(half_, dtype=np.float32) / np.float32(half_))
    ang = np.arange(S, dtype=np.float32)[:, None] * freq[None, :].astype(np.float32)
    exact = BUCKETS // 2
    dist = np.arange(P)
    far = exact + (np.log(np.maximum(dist, 1).astype(np.float32) / exact) / np.log(P / exact)
                   * (BUCKETS - exact)).astype(np.int32)
    bucket = np.where(dist < exact, dist, np.minimum(far, BUCKETS - 1))
    onehot = (bucket[None, :] == np.arange(BUCKETS)[:, None]).astype(np.float32)
    return {"cos": np.cos(ang).astype(np.float32), "sin": np.sin(ang).astype(np.float32), "bucket_onehot": onehot}


def kernel(**inputs):
    import numpy as _np
    import concourse.bacc as _bacc
    from concourse import mybir as _mybir
    from concourse.bass_utils import run_bass_kernel_spmd as _run

    nc = _bacc.Bacc("TRN2", target_bir_lowering=False, num_devices=1)
    arrays, args = {}, {}
    for name, a in [(n, inputs[n]) for n in _INS] + list(shape_constants().items()):
        a = _np.ascontiguousarray(a)
        arrays[f"in_{name}_dram"] = a
        args[name] = nc.dram_tensor(f"in_{name}_dram", a.shape, _mybir.dt.from_np(a.dtype), kind="ExternalInput").ap()
    args["out"] = nc.dram_tensor("out_0_dram", (1, S, D), _mybir.dt.float32, kind="ExternalOutput").ap()
    program(nc, args)
    r = _run(nc, [arrays], core_ids=[0])
    return r.results[0]["out_0_dram"]
```
